# Optimizing a Trainium2 kernel written in Bass

```python
import jax, jax.numpy as jnp
from jax import lax
import numpy as np

D_MODEL = 1024
BATCH = 1
SEQ = 1024
DEPTH = 1
DEC_BATCH = 1
DEC_SEQ = 32
PAST_LEN = 256

CHUNK = 64
A_HEADS = 8
A_DK = 128
A_DV = 128
A_WIDTH = A_HEADS * A_DK
POOL_WINDOWS = (2, 4, 8, 16)
POOL_GROUPS = 4
POOL_GDIM = 128
B_WIDTH = POOL_GROUPS * POOL_GDIM
POOL_BUF = max(POOL_WINDOWS) - 1
D_FF = 2816
PLE_DIM = 256
IN_WIDTH = 4 * A_WIDTH + B_WIDTH + 2 * D_MODEL
IN_SPLITS = (A_WIDTH, 2 * A_WIDTH, 3 * A_WIDTH, 4 * A_WIDTH,
             4 * A_WIDTH + B_WIDTH, 4 * A_WIDTH + B_WIDTH + D_MODEL)
N_NORMS = 8
EPS = 1e-6

kernel_name = 'hgrn2_pool_macaron_streaming_step'

def rmsnorm(x, g):
    xf = x.astype(jnp.float32)
    y = xf * lax.rsqrt(jnp.mean(xf * xf, axis=-1, keepdims=True) + EPS)
    return (y * g.astype(jnp.float32)).astype(x.dtype)

def swiglu(h, w_gu, w_down):
    a, b = jnp.split(h @ w_gu, 2, axis=-1)
    return (jax.nn.silu(a) * b) @ w_down

def hgrn_chunked(q, k, v, logf, s0, chunk):
    bsz, t_len, n_h, _ = q.shape
    n_c = t_len // chunk

    def to_chunks(a):
        return a.reshape(bsz, n_c, chunk, n_h, a.shape[-1]).transpose(1, 0, 3, 2, 4)

    mask = jnp.tril(jnp.ones((chunk, chunk), dtype=bool))[:, :, None]

    def step(S, inp):
        qc, kc, vc, gc = inp
        G = jnp.cumsum(gc, axis=-2)
        o_inter = jnp.einsum('bhtk,bhkv->bhtv', qc * jnp.exp(G), S)
        diff = G[:, :, :, None, :] - G[:, :, None, :, :]
        decay = jnp.exp(jnp.where(mask, diff, -jnp.inf))
        att = jnp.einsum('bhtk,bhsk,bhtsk->bhts', qc, kc, decay)
        o = o_inter + jnp.einsum('bhts,bhsv->bhtv', att, vc)
        G_last = G[:, :, -1:, :]
        S_new = (jnp.exp(G_last[:, :, 0, :])[..., None] * S
                 + jnp.einsum('bhsk,bhsv->bhkv', kc * jnp.exp(G_last - G), vc))
        return S_new, o

    S, o = lax.scan(step, s0, (to_chunks(q), to_chunks(k), to_chunks(v), to_chunks(logf)))
    o = o.transpose(1, 0, 3, 2, 4).reshape(bsz, t_len, n_h, v.shape[-1])
    return o, S

def pool_mix(u, buf, start_pos, w_pool, scale):
    bsz, t_len, width = u.shape
    uf = u.astype(jnp.float32)
    xp = jnp.concatenate([buf.astype(jnp.float32), uf], axis=1)
    c = jnp.cumsum(jnp.pad(xp, ((0, 0), (1, 0), (0, 0))), axis=1)
    end = c[:, POOL_BUF + 1:]
    pos = start_pos + jnp.arange(t_len)
    groups = []
    for g, w in enumerate(POOL_WINDOWS):
        sl = slice(g * POOL_GDIM, (g + 1) * POOL_GDIM)
        start = c[:, POOL_BUF + 1 - w: POOL_BUF + 1 - w + t_len, sl]
        cnt = jnp.minimum(w, pos + 1).astype(jnp.float32)[None, :, None]
        groups.append((end[..., sl] - start) / cnt - uf[..., sl])
    pooled = jnp.stack(groups, axis=2)
    mixed = jnp.einsum('btgc,gcd->btgd', pooled, w_pool.astype(jnp.float32))
    mixed = mixed.reshape(bsz, t_len, width) * scale.astype(jnp.float32)
    return mixed.astype(u.dtype), xp[:, -POOL_BUF:].astype(u.dtype)

def layer(x, p, s_hgrn, s_pool, start_pos, chunk, lb, gains,
          w_ffn1_gu, w_ffn1_down, w_in, a_gnorm, w_a_up, w_pool, pool_scale,
          w_b_up, w_out, w_ffn2_gu, w_ffn2_down, w_ple_proj, w_ple_gate):
    bsz, t_len, _ = x.shape
    x = x + 0.5 * rmsnorm(swiglu(rmsnorm(x, gains[0]), w_ffn1_gu, w_ffn1_down), gains[1])
    h = rmsnorm(x, gains[2])
    z = h @ w_in
    q, fz, iv, og, u, ga, gb = jnp.split(z, IN_SPLITS, axis=-1)
    lb_h = lb.reshape(A_HEADS, A_DK)
    fz = fz.astype(jnp.float32).reshape(bsz, t_len, A_HEADS, A_DK)
    logf = jnp.logaddexp(jnp.log(lb_h), jnp.log1p(-lb_h) + jax.nn.log_sigmoid(fz))
    k = (1.0 - lb_h) * jax.nn.sigmoid(-fz)
    qh = jax.nn.silu(q.astype(jnp.float32)).reshape(bsz, t_len, A_HEADS, A_DK)
    vh = iv.astype(jnp.float32).reshape(bsz, t_len, A_HEADS, A_DV)
    o, s_new = hgrn_chunked(qh, k, vh, logf, s_hgrn.astype(jnp.float32), chunk)
    o = o * lax.rsqrt(jnp.mean(o * o, axis=-1, keepdims=True) + EPS) * a_gnorm.astype(jnp.float32)
    o = o.reshape(bsz, t_len, A_WIDTH).astype(x.dtype) * jax.nn.silu(og)
    y_a = o @ w_a_up
    pooled, buf_new = pool_mix(u, s_pool, start_pos, w_pool, pool_scale)
    y_b = pooled @ w_b_up
    m = jax.nn.sigmoid(ga) * y_a + jax.nn.sigmoid(gb) * y_b
    x = x + rmsnorm(m @ w_out, gains[3])
    x = x + 0.5 * rmsnorm(swiglu(rmsnorm(x, gains[4]), w_ffn2_gu, w_ffn2_down), gains[5])
    e = p.astype(x.dtype) @ w_ple_proj
    gate = jax.nn.sigmoid(rmsnorm(x, gains[6]) @ w_ple_gate)
    x = x + rmsnorm(gate * e, gains[7])
    return x, s_new, buf_new

def setup_inputs(seed: int = 0) -> dict:
    key = jax.random.key(seed)
    ks = jax.random.split(key, 24)

    def nrm(k, shape, scale):
        return jax.random.normal(k, shape, jnp.float32) * scale

    return {
        'x_prompt': nrm(ks[0], (BATCH, SEQ, D_MODEL), 1.0),
        'x_sample': nrm(ks[1], (DEC_BATCH, DEC_SEQ, D_MODEL), 1.0),
        'p_prompt': nrm(ks[2], (DEPTH, BATCH, SEQ, PLE_DIM), 1.0),
        'p_sample': nrm(ks[3], (DEPTH, DEC_BATCH, DEC_SEQ, PLE_DIM), 1.0),
        'state_hgrn': nrm(ks[4], (DEPTH, DEC_BATCH, A_HEADS, A_DK, A_DV), 0.5),
        'state_pool': nrm(ks[5], (DEPTH, DEC_BATCH, POOL_BUF, B_WIDTH), 1.0),
        'norm_gains': 1.0 + nrm(ks[6], (DEPTH, N_NORMS, D_MODEL), 0.02),
        'lb_logits': nrm(ks[7], (DEPTH + 1, A_WIDTH), 0.1),
        'w_ffn1_gu': nrm(ks[8], (DEPTH, D_MODEL, 2 * D_FF), D_MODEL ** -0.5),
        'w_ffn1_down': nrm(ks[9], (DEPTH, D_FF, D_MODEL), D_FF ** -0.5),
        'w_in': nrm(ks[10], (DEPTH, D_MODEL, IN_WIDTH), D_MODEL ** -0.5),
        'a_gnorm': 1.0 + nrm(ks[11], (DEPTH, A_DV), 0.02),
        'w_a_up': nrm(ks[12], (DEPTH, A_WIDTH, D_MODEL), A_WIDTH ** -0.5),
        'w_pool': nrm(ks[13], (DEPTH, POOL_GROUPS, POOL_GDIM, POOL_GDIM), POOL_GDIM ** -0.5),
        'pool_scale': 1.0 + nrm(ks[14], (DEPTH, B_WIDTH), 0.1),
        'w_b_up': nrm(ks[15], (DEPTH, B_WIDTH, D_MODEL), B_WIDTH ** -0.5),
        'w_out': nrm(ks[16], (DEPTH, D_MODEL, D_MODEL), D_MODEL ** -0.5),
        'w_ffn2_gu': nrm(ks[17], (DEPTH, D_MODEL, 2 * D_FF), D_MODEL ** -0.5),
        'w_ffn2_down': nrm(ks[18], (DEPTH, D_FF, D_MODEL), D_FF ** -0.5),
        'w_ple_proj': nrm(ks[19], (DEPTH, PLE_DIM, D_MODEL), PLE_DIM ** -0.5),
        'w_ple_gate': nrm(ks[20], (DEPTH, D_MODEL, D_MODEL), D_MODEL ** -0.5),
    }

def reference(x_prompt, x_sample, p_prompt, p_sample, state_hgrn, state_pool,
              norm_gains, lb_logits, w_ffn1_gu, w_ffn1_down, w_in, a_gnorm, w_a_up,
              w_pool, pool_scale, w_b_up, w_out, w_ffn2_gu, w_ffn2_down,
              w_ple_proj, w_ple_gate):
    lb_all = jnp.cumsum(jax.nn.softmax(lb_logits.astype(jnp.float32), axis=0), axis=0)
    bsz_p = x_prompt.shape[0]
    dec_len = x_sample.shape[1]
    xp, xs = x_prompt, x_sample
    hp_list, bp_list, hs_list, bs_list = [], [], [], []
    for l in range(DEPTH):
        weights = (w_ffn1_gu[l], w_ffn1_down[l], w_in[l], a_gnorm[l], w_a_up[l], w_pool[l],
                   pool_scale[l], w_b_up[l], w_out[l], w_ffn2_gu[l], w_ffn2_down[l],
                   w_ple_proj[l], w_ple_gate[l])
        s0 = jnp.zeros((bsz_p, A_HEADS, A_DK, A_DV), jnp.float32)
        b0 = jnp.zeros((bsz_p, POOL_BUF, B_WIDTH), xp.dtype)
        xp, hp, bp = layer(xp, p_prompt[l], s0, b0, 0, CHUNK, lb_all[l], norm_gains[l], *weights)
        xs, hs, bs = layer(xs, p_sample[l], state_hgrn[l], state_pool[l], PAST_LEN, dec_len,
                           lb_all[l], norm_gains[l], *weights)
        hp_list.append(hp)
        bp_list.append(bp)
        hs_list.append(hs)
        bs_list.append(bs)
    new_hgrn_prompt = jnp.stack(hp_list)
    new_pool_prompt = jnp.stack(bp_list)
    new_hgrn_sample = jnp.stack(hs_list)
    new_pool_sample = jnp.stack(bs_list)
    return (xp, xs, new_hgrn_prompt, new_pool_prompt, new_hgrn_sample, new_pool_sample)


_drawn_inputs = setup_inputs


def setup_inputs(seed=0):
    import zlib

    import numpy as np

    out = dict(_drawn_inputs(seed))
    spreads = {}
    factors = {}
    for name, (base, spread) in spreads.items():
        noise = np.random.default_rng([zlib.crc32(name.encode()), seed]).standard_normal(out[name].shape)
        drawn = base * np.exp(spread * noise) if base else spread * noise
        out[name] = __import__('jax').numpy.asarray(drawn.astype(out[name].dtype))
    for name, factor in factors.items():
        out[name] = (out[name] * factor).astype(out[name].dtype)
    return out
```

```python
from contextlib import ExitStack

import concourse.bass as bass
from concourse import mybir

ALU = mybir.AluOpType
ACT = mybir.ActivationFunctionType
F32 = mybir.dt.float32
F16 = mybir.dt.float16
BF16 = mybir.dt.bfloat16
U8 = mybir.dt.uint8
AX_X = mybir.AxisListType.X

P = 128
D_MODEL, SEQ, DEC_SEQ, D_FF = 1024, 1024, 32, 2816
HEADS, DK = 8, 128
POOL_WINDOWS, POOL_BUF = (2, 4, 8, 16), 15
PLE_DIM = 256
EPS = 1e-6
KD = D_MODEL // P
KF = D_FF // P
KP = PLE_DIM // P
T = SEQ + DEC_SEQ
G = 3
N = T // G
C = 64
NC = (T + C - 1) // C
TP = NC * C
PT = SEQ // C
WS = 32.0
UT = 4
RING = 12

STAGES = {
    "ffn1_up": dict(units=8, turns=11, ks=[KD] * 4, kinds="G" + "P" * 10, banks=6),
    "ffn1_down": dict(units=11, turns=4, ks=[KF] * 2, kinds="MMMG", banks=6),
    "heads": dict(units=8, turns=HEADS + 1, ks=[KD] * 4, kinds="G" + "M" * HEADS, banks=4),
    "pool": dict(units=1, turns=1, ks=[1] * 4, kinds="M", banks=4),
    "gates": dict(units=7, turns=8, ks=[KD, KD, KD, 4], kinds="M" * 8, banks=6),
    "out": dict(units=8, turns=2, ks=[KD] * 4, kinds="MG", banks=6),
    "ffn2_up": dict(units=8, turns=11, ks=[KD] * 4, kinds="G" + "P" * 10, banks=6),
    "ffn2_down": dict(units=11, turns=4, ks=[KF] * 2, kinds="MMMG", banks=6),
    "ple": dict(units=10, turns=2, ks=[KD, KP] * 4, kinds="GG", banks=6),
}
ORDER = list(STAGES)

HG_PIECES = (["vT"] * 3 + ["kT"] * 3 + ["L32"] * 2 + ["L16"] * 2 + ["D16"] * 2
             + ["P"] * 5 + ["O"] * 4 + ["SS"] * 3)
HG_FIRST = {k: HG_PIECES.index(k) for k in dict.fromkeys(HG_PIECES)}
TOK_TILES = [(0, 4), (4, 7), (7, 9)]
P_CHUNKS = [range(0, 8, 2), range(1, 8, 2), range(8, 16, 2), range(9, 16, 2), range(16, 17)]
O_CHUNKS = [range(0, 16, 2), range(1, 8, 2), range(9, 16, 2), range(16, 17)]
NORM_CALLS = 3 + 3 * 6 + 3


def jobs_of(name, kind):
    a = len(STAGES[name]["ks"])
    if kind == "M":
        return [(t, g) for t in range(a) for g in range(G)]
    if kind == "G":
        return [(t, g) for g in range(G) for t in range(a)]
    return [(2 * q + r, g) for q in range(a // 2) for g in range(G) for r in range(2)]


class Plan:

    def __init__(self):
        uses = [0] * 8
        unit = 0
        loads = [0] * RING
        self.base, self.unit0, self.load0 = {}, {}, {}
        self.hg_base = None
        self.norm = []
        norm_uses = iter(range(NORM_CALLS))

        def norms(k):
            for _ in range(k):
                c = next(norm_uses)
                b = 6 + c % 2
                self.norm.append((b, uses[b]))
                uses[b] += 1

        before = {"ffn1_up": 3, "heads": 6, "ffn2_up": 6, "ple": 6}
        for name in ORDER:
            s = STAGES[name]
            norms(before.get(name, 0))
            self.base[name] = list(uses)
            self.unit0[name] = unit
            self.load0[name] = list(loads)
            per = len(s["ks"]) * G // s["banks"]
            for b in range(s["banks"]):
                uses[b] += per * s["turns"]
            unit += s["units"] * s["turns"]
            for u in range(s["units"]):
                loads[u] += s["turns"]
            if name == "heads":
                self.hg_base = list(uses)
                for b in range(4, 8):
                    uses[b] += HEADS * len(HG_PIECES) // 4
        norms(3)
        self.units = unit

    def job(self, name, i, pos):
        s = STAGES[name]
        r = s["banks"]
        per = len(s["ks"]) * G // r
        return pos % r, i * per + (self.base[name][pos % r] + pos // r)

    def piece(self, head, n):
        b = 4 + n % 4
        return b, head * (len(HG_PIECES) // 4) + (self.hg_base[b] + n // 4)

    def freed_by(self, name, i, u):
        s = STAGES[name]
        kind = s["kinds"][i] if isinstance(i, int) else "M" if "M" in s["kinds"] else "P"
        ends, t = [], 0
        for k in s["ks"]:
            ends.append((t // UT, (t + k - 1) // UT))
            t += k
        pos = max(n for n, (t, _) in enumerate(jobs_of(name, kind)) if ends[t][0] <= u <= ends[t][1])
        return self.job(name, i, pos)


class Tally:

    def __init__(self, sem):
        self.sem, self.base, self.n, self.loop = sem, 0, 0, None

    def inc(self, ins, k=1):
        ins.then_inc(self.sem, k)
        self.n += k

    @property
    def value(self):
        return self.base + self.n

    def enter(self, i, first, per):
        at = self.base + self.n
        self.loop = (at, per)
        self.base = i * per + (at - first * per) if per else at
        self.n = 0

    def leave(self, trips):
        at, per = self.loop
        assert self.n == per, (str(self.sem), self.n, per)
        self.base, self.n, self.loop = at + trips * per, 0, None


def turn_runs(name):
    s = STAGES[name]
    runs = []
    for i, k in enumerate(s["kinds"]):
        if runs and runs[-1][2] == k and i > 1:
            runs[-1][1] = i + 1
        else:
            runs.append([i, i + 1, k])
    return runs


def build(nc, xT, pT, weights, cols, lbT, consts, masks, inv_count, state_in, pool_in,
          out_x, out_states, out_pools):
    plan = Plan()
    with ExitStack() as ctx:
        def sb(name, shape, dt):
            return ctx.enter_context(nc.sbuf_tensor(name, shape, dt))

        def sem(name):
            return ctx.enter_context(nc.semaphore(name))

        x = sb("x", [P, KD, T], F32)
        hy = sb("hy", [P, G, KD, 2 * N], F16)
        hid = sb("hid", [P, KF, G, 2 * N], F16)
        ring = sb("ring", [P, RING, 2 * UT * P], F16)
        wtmp = sb("wtmp", [P, UT * P], F32)
        scratch = sb("scratch", [P, KD, N], F32)
        wconst = sb("wconst", [P, 2], F32)
        u1 = sb("u1", [P, TP], F32)
        sbuf2 = sb("sbuf2", [P, 2, N], F32)
        ssum = sb("ssum", [P, N], F32)
        rinv = sb("rinv", [P, N], F32)
        cst = sb("cst", [P, 2 * P], F32)
        msk = sb("msk", [P, 3, 512], U8)
        invc = sb("invc", [P, 4, 16], F32)
        col = sb("col", [P, 8 * KD + 1 + 4 + 2], F32)
        lbl = sb("lbl", [P, 2, HEADS], F32)
        oneml = sb("oneml", [P, HEADS], F32)
        mark = sb("mark", [P, 8], F32)
        eg = sb("eg", [P, NC], F32)
        bank = [ctx.enter_context(nc.psum_tensor(f"bank{b}", [P, 512], F32)) for b in range(8)]

        ident, ones = cst[:, 0:P], cst[:, P:2 * P]
        gain = lambda n, k: col[:, n * KD + k:n * KD + k + 1]
        anorm = col[:, 8 * KD:8 * KD + 1]
        pscale = lambda j: col[:, 8 * KD + 1 + j:8 * KD + 2 + j]
        eps, one = col[:, 8 * KD + 5:8 * KD + 6], col[:, 8 * KD + 6:8 * KD + 7]

        def xg(g, k=None):
            return x[:, :, g * N:(g + 1) * N] if k is None else x[:, k, g * N:(g + 1) * N]

        def hyp(g, k, w):
            return hy[:, g, k, w * N:(w + 1) * N]

        yv = hy[:, :, :, :].rearrange("p g k n -> p (g k n)").bitcast(F32).rearrange(
            "p (g k n) -> p g k n", g=G, k=KD)
        hidf = hid[:, :, :, :].rearrange("p s g n -> p (s g n)").bitcast(F32)
        hidv = hidf.rearrange("p (s g n) -> p s g n", s=KF, g=G)
        area = hidf[:, 8 * T:KF * T]

        def arr(n):
            return area[:, n * TP:(n + 1) * TP]

        V, Q, K_, GG = arr(0), arr(1), arr(2), arr(3)
        W = [arr(4 + n) for n in range(6)]
        vtok = area[:, 10 * TP:10 * TP + 9 * P]
        ktok = area[:, 10 * TP + 9 * P:10 * TP + 18 * P]
        att = area[:, 10 * TP + 18 * P:10 * TP + 18 * P + 9 * C]
        a0 = 10 * TP + 18 * P + 9 * C
        smask = area[:, a0:a0 + TP // 2].bitcast(BF16)
        S = scratch[:, :, :].rearrange("p k n -> p (k n)")[:, 0:18 * P]

        def Sn(n):
            return S[:, n * P:(n + 1) * P]

        S_IN, S_OUT = 16, 17
        U = [V, u1[:, :], Q, K_]
        UP, US = POOL_BUF, POOL_BUF + SEQ + POOL_BUF
        hid16 = hid[:, :, :, :].rearrange("p s g n -> p (s g n)")
        pooled = [hid16[:, 16 * T + 2 * (4 + j) * TP:16 * T + 2 * (4 + j) * TP + 2 * T].rearrange(
            "p (g n) -> p g n", g=G) for j in range(4)]
        M0, TMP0, MIX0 = 8, 16, 18
        Y0, PL0 = 0, 8
        p_raw = hidv[:, PL0 + 3 * KP:PL0 + 6 * KP, 0, :]
        p_split = hid[:, PL0:PL0 + 3 * KP, 0, :]

        slot_loaded = [sem(f"slot_loaded{u}") for u in range(RING)]
        unit_ready = sem("unit_ready")
        bank_full = [sem(f"bank_full{b}") for b in range(8)]
        bank_read = [sem(f"bank_read{b}") for b in range(8)]
        consts_loaded = sem("consts_loaded")
        x_loaded = [sem(f"x_loaded{g}") for g in range(G)]
        p_loaded = sem("p_loaded")
        p_ready = sem("p_ready")
        cols_ready = sem("cols_ready")
        lb_diff = sem("lb_diff")
        lb_ready = sem("lb_ready")
        squares_ready = sem("squares_ready")
        sums_ready = sem("sums_ready")
        rinv_ready = sem("rinv_ready")
        x_updated = sem("x_updated")
        hfull_ready = sem("hfull_ready")
        hhi_ready = sem("hhi_ready")
        h_ready = sem("h_ready")
        hidden_ready = sem("hidden_ready")
        sigmoid_ready = sem("sigmoid_ready")
        k_ready = sem("k_ready")
        logf_ready = sem("logf_ready")
        cum_ready = sem("cum_ready")
        diff_ready = sem("diff_ready")
        exp_ready = sem("exp_ready")
        operand_ready = sem("operand_ready")
        o_ready = sem("o_ready")
        osq_ready = sem("osq_ready")
        ss_ready = sem("ss_ready")
        orstd_ready = sem("orstd_ready")
        head_ready = sem("head_ready")
        chain_ready = sem("chain_ready")
        state_loaded = sem("state_loaded")
        state_stored = sem("state_stored")
        pads_set = sem("pads_set")
        wconst_set = sem("wconst_set")
        pool_loaded = sem("pool_loaded")
        u_ready = sem("u_ready")
        pool_stored = sem("pool_stored")
        pooled_ready = sem("pooled_ready")
        mixed_ready = sem("mixed_ready")
        yple_ready = sem("yple_ready")
        x_final = sem("x_final")
        x_stored = sem("x_stored")
        vec_chain = sem("vec_chain")
        act_chain = sem("act_chain")
        pool_chain = sem("pool_chain")

        block = ctx.enter_context(nc.Block())

        def loops(eng, name, body, runs=None):
            for a, b, kind in runs or turn_runs(name):
                if b - a >= 3:
                    with eng.Fori(a, b) as i:
                        body(i, kind)
                else:
                    for i in range(a, b):
                        body(i, kind)

        @block.sync
        def _(sp):
            last = {}

            def load(name, i, u, freed):
                if freed is not None:
                    sp.wait_ge(bank_full[freed[0]], freed[1] + 1)
                n = i * STAGES[name]["units"] + (plan.unit0[name] + u)
                src = weights[n, :, :] if isinstance(n, int) else weights[
                    bass.ds(n, 1), :, :].rearrange("a p c -> p (a c)")
                sp.dma_start(ring[:, u, :].bitcast(F32), src).then_inc(slot_loaded[u], 16)

            for name in ORDER:
                s = STAGES[name]
                runs = []
                for i in range(s["turns"]):
                    k = s["kinds"][i - 1] if i else None
                    if runs and runs[-1][2] == k:
                        runs[-1][1] = i + 1
                    else:
                        runs.append([i, i + 1, k])
                for a, b, k in runs:
                    if b - a >= 3:
                        with sp.Fori(a, b) as i:
                            for u in range(s["units"]):
                                load(name, i, u, plan.freed_by(name, i - 1, u))
                    else:
                        for i in range(a, b):
                            for u in range(s["units"]):
                                load(name, i, u, plan.freed_by(name, i - 1, u) if i else last.get(u))
                for u in range(s["units"]):
                    last[u] = plan.freed_by(name, s["turns"] - 1, u)

        @block.gpsimd
        def _(pool):
            chain = Tally(pool_chain)
            done = Tally(unit_ready)
            ws_all = wconst[:, 0:1].to_broadcast([P, UT * P])
            one_all = wconst[:, 1:2].to_broadcast([P, UT * P])
            nc.gpsimd.memset(wconst[:, 0:1], WS).then_inc(wconst_set, 1)
            nc.gpsimd.memset(wconst[:, 1:2], 1.0).then_inc(wconst_set, 1)
            pool.wait_ge(wconst_set, 2)

            def split(name, i, u):
                raw = ring[:, u, :].bitcast(F32)
                hi, lo = ring[:, u, 0:UT * P], ring[:, u, UT * P:2 * UT * P]
                pool.wait_ge(slot_loaded[u], i * 16 + 16 * (plan.load0[name][u] + 1))
                if not (isinstance(i, int) and name == ORDER[0] and i == 0 and u == 0):
                    pool.wait_ge(unit_ready, done.value)
                chain.inc(nc.gpsimd.tensor_tensor(wtmp[:], raw, ws_all, ALU.mult))
                pool.wait_ge(pool_chain, chain.value)
                chain.inc(nc.gpsimd.tensor_tensor(hi, wtmp[:], one_all, ALU.mult))
                pool.wait_ge(pool_chain, chain.value)
                done.inc(nc.gpsimd.tensor_tensor(lo, wtmp[:], hi, ALU.subtract))

            for name in ORDER:
                s = STAGES[name]
                first = 1 if name == ORDER[0] else 0
                for i in range(first):
                    for u in range(s["units"]):
                        split(name, i, u)
                if s["turns"] - first >= 3:
                    with pool.Fori(first, s["turns"]) as i:
                        chain.enter(i, first, 2 * s["units"])
                        done.enter(i, first, s["units"])
                        for u in range(s["units"]):
                            split(name, i, u)
                    chain.leave(s["turns"] - first)
                    done.leave(s["turns"] - first)
                else:
                    for i in range(first, s["turns"]):
                        for u in range(s["units"]):
                            split(name, i, u)

        @block.tensor
        def _(pe):
            def take(b, uses):
                if not (isinstance(uses, int) and uses == 0):
                    pe.wait_ge(bank_read[b], uses)

            def turn(name, i, kind, rhs, ready=None, hooks=None):
                s = STAGES[name]
                starts = [sum(s["ks"][:t]) for t in range(len(s["ks"]))]
                seen = set()
                for pos, (t, g) in enumerate(jobs_of(name, kind)):
                    b, uses = plan.job(name, i, pos)
                    if ready:
                        ready(i, t, g, pos)
                    take(b, uses)
                    for k in range(s["ks"][t]):
                        u, q = divmod(starts[t] + k, UT)
                        if u not in seen:
                            seen.add(u)
                            pe.wait_ge(unit_ready, i * s["units"] + (plan.unit0[name] + u + 1))
                        whi = ring[:, u, q * P:(q + 1) * P]
                        wlo = ring[:, u, (UT + q) * P:(UT + q + 1) * P]
                        out = bank[b][:, 0:N]
                        end = k == s["ks"][t] - 1
                        nc.tensor.matmul(out, whi, rhs(t, k, g, 0), start=(k == 0), stop=False)
                        nc.tensor.matmul(out, whi, rhs(t, k, g, 1), start=False, stop=False)
                        mm = nc.tensor.matmul(out, wlo, rhs(t, k, g, 0), start=False, stop=end)
                        if end:
                            mm.then_inc(bank_full[b], 1)
                        elif hooks and (pos, k) in hooks:
                            for f in hooks[(pos, k)]:
                                f()
                    if hooks and (pos, None) in hooks:
                        for f in hooks[(pos, None)]:
                            f()

            def norm(c):
                b, uses = plan.norm[c]
                pe.wait_ge(sums_ready, c + 1)
                take(b, uses)
                nc.tensor.matmul(bank[b][:, 0:N], ones, ssum[:], start=True, stop=True).then_inc(bank_full[b], 1)

            def h_rhs(t, k, g, w):
                return hyp(g, k, w)

            def hid_rhs(base):
                return lambda t, k, g, w: hid[:, base + k, g, w * N:(w + 1) * N]

            def h_wait(p):
                def ready(i, t, g, pos):
                    if isinstance(i, int) and i == 0 and t == 0:
                        pe.wait_ge(h_ready, 3 * p + g + 1)
                return ready

            def up(name, p, hooks):
                for a, b, kind in turn_runs(name):
                    if a == 0:
                        turn(name, 0, kind, h_rhs, h_wait(p), hooks)
                    else:
                        with pe.Fori(a, b) as i:
                            turn(name, i, kind, h_rhs)

            def down(name, f, hooks):
                def ready(i, t, g, pos):
                    if isinstance(i, int) and i == 0 and pos == 0:
                        pe.wait_ge(hidden_ready, 66 * (f + 1))
                turn(name, 0, "M", hid_rhs(0), ready)
                for i in (1, 2):
                    turn(name, i, "M", hid_rhs(0))
                turn(name, 3, "G", hid_rhs(0), None, hooks)

            def calls(*cs):
                return [lambda c=c: norm(c) for c in cs]

            def piece(head, n, fill):
                b, uses = plan.piece(head, n)
                take(b, uses)
                fill(b).then_inc(bank_full[b], 1)

            def head_transposes(head, kind, src):
                for r, (j0, j1) in enumerate(TOK_TILES):
                    def fill(b, j0=j0, j1=j1):
                        for j in range(j0, j1):
                            w = min(P, TP - j * P)
                            last = nc.tensor.transpose(bank[b][0:w, (j - j0) * P:(j - j0 + 1) * P],
                                                       src[:, j * P:j * P + w], ident)
                        return last
                    piece(head, HG_FIRST[kind] + r, fill)

            def head_scores(head, kind, kk, qq):
                for r, (c0, c1) in enumerate([(0, PT), (PT, NC)]):
                    def fill(b, c0=c0, c1=c1):
                        for c in range(c0, c1):
                            h0 = C * (c % 2)
                            last = nc.tensor.matmul(bank[b][h0:h0 + C, (c - c0) // 2 * C:((c - c0) // 2 + 1) * C],
                                                    kk[:, c * C:(c + 1) * C], qq[:, c * C:(c + 1) * C],
                                                    start=True, stop=True)
                        return last
                    piece(head, HG_FIRST[kind] + r, fill)

            def head_updates(head):
                for r in range(5):
                    def fill(b, r=r):
                        for n, c in enumerate(P_CHUNKS[r]):
                            h0 = C * (c % 2)
                            j = c // 2
                            last = nc.tensor.matmul(bank[b][:, n * P:(n + 1) * P],
                                                    ktok[h0:h0 + C, j * P:(j + 1) * P],
                                                    vtok[h0:h0 + C, j * P:(j + 1) * P], start=True, stop=True)
                        return last
                    piece(head, HG_FIRST["P"] + r, fill)

            def head_outputs(head):
                pe.wait_ge(chain_ready, head * 1 + 1)
                for r, cs in enumerate(O_CHUNKS):
                    def fill(b, cs=cs):
                        for n, c in enumerate(cs):
                            h0, j = C * (c % 2), c // 2
                            nc.tensor.matmul(bank[b][:, n * C:(n + 1) * C], vtok[h0:h0 + C, j * P:(j + 1) * P],
                                             att[h0:h0 + C, j * C:(j + 1) * C],
                                             start=(n == 0), stop=True, skip_group_check=True)
                        for n, c in enumerate(cs):
                            if c:
                                last = nc.tensor.matmul(bank[b][:, n * C:(n + 1) * C],
                                                        Sn(c - 1 if c < PT else S_IN), W[5][:, c * C:(c + 1) * C],
                                                        start=False, stop=True, skip_group_check=True)
                        return last
                    piece(head, HG_FIRST["O"] + r, fill)

            def head_sumsq(head):
                pe.wait_ge(osq_ready, head * 1 + 1)
                for r in range(3):
                    c0, c1 = r * 512, min(r * 512 + 512, TP)
                    def fill(b, c0=c0, c1=c1):
                        return nc.tensor.matmul(bank[b][:, 0:c1 - c0], ones, W[4][:, c0:c1], start=True, stop=True)
                    piece(head, HG_FIRST["SS"] + r, fill)

            def v_there(head):
                for g in range(G):
                    pos = jobs_of("heads", "M").index((0, g)) if not (isinstance(head, int) and head == 0) \
                        else jobs_of("heads", "G").index((0, g))
                    b, uses = plan.job("heads", head, pos)
                    pe.wait_ge(bank_read[b], uses + 1)

            def operands(head, n):
                pe.wait_ge(operand_ready, head * 8 + n)

            def head_hooks(h):
                hh = h - 1
                return {
                    (3, None): [lambda: operands(hh, 1), lambda: head_transposes(hh, "kT", W[3])],
                    (4, None): [lambda: operands(hh, 3), lambda: head_scores(hh, "L32", W[0], W[0])],
                    (5, None): [lambda: operands(hh, 5), lambda: head_scores(hh, "L16", W[1], W[1]),
                                lambda: operands(hh, 7), lambda: head_scores(hh, "D16", W[4], W[2])],
                    (6, None): [lambda: head_updates(hh)],
                    (8, None): [lambda: operands(hh, 8), lambda: head_outputs(hh)],
                    (10, None): [lambda: head_sumsq(hh)],
                }

            pe.wait_ge(consts_loaded, 16 * 5)
            norm(0)
            up("ffn1_up", 0, {(0, 3): calls(1), (1, 3): calls(2)})
            down("ffn1_down", 0, {(2, 10): calls(3), (3, 16): calls(4), (4, 12): calls(5), (5, 16): calls(6)})
            turn("heads", 0, "G", h_rhs, h_wait(1), {(0, 6): calls(7), (3, 6): calls(8)})
            with pe.Fori(1, HEADS + 1) as h:
                for g in range(G):
                    b, uses = plan.job("heads", h - 1, 0)
                pe.wait_ge(k_ready, h)
                head_transposes(h - 1, "vT", V)
                turn("heads", h, "M", h_rhs, None, head_hooks(h))

            def pooled_rhs(t, k, g, w):
                return pooled[t][:, g, w * N:(w + 1) * N]

            turn("pool", 0, "M", pooled_rhs, lambda i, t, g, pos: pe.wait_ge(pooled_ready, t + 1) if g == 0 else None)

            def gate_rhs(t, k, g, w):
                if t < 2:
                    return hyp(g, k, w)
                return hid[:, (0 if t == 2 else MIX0) + k, g, w * N:(w + 1) * N]

            pe.wait_ge(head_ready, HEADS)
            pe.wait_ge(mixed_ready, 12)
            with pe.Fori(0, 8) as i:
                turn("gates", i, "M", gate_rhs)
            pe.wait_ge(mixed_ready, 12 + 24)
            turn("out", 0, "M", hid_rhs(M0))
            turn("out", 1, "G", hid_rhs(M0), None,
                 {(5, 6): calls(9), (8, 6): calls(10), (9, 6): calls(11)})
            up("ffn2_up", 2, {(1, 6): calls(12), (2, 6): calls(13), (5, 6): calls(14)})
            down("ffn2_down", 1, {(2, 10): calls(15), (3, 16): calls(16), (4, 12): calls(17), (5, 16): calls(18)})

            def ple_rhs(t, k, g, w):
                return hyp(g, k, w) if t % 2 == 0 else p_split[:, G * k + g, w * N:(w + 1) * N]

            def ple_ready(i, t, g, pos):
                if i == 0 and t == 0:
                    pe.wait_ge(h_ready, 9 + g + 1)
                if i == 0 and t == 1 and g == 0:
                    pe.wait_ge(p_ready, 1)

            turn("ple", 0, "G", ple_rhs, ple_ready, {(0, 6): calls(19), (4, 6): calls(20)})
            turn("ple", 1, "G", ple_rhs, None, {(10, 3): calls(21), (18, 3): calls(22)})
            norm(23)

        @block.scalar
        def _(act):
            chain = Tally(act_chain)

            act.dma_start(cst[:], consts).then_inc(consts_loaded, 16)
            act.dma_start(col[:], cols).then_inc(consts_loaded, 16)
            act.dma_start(lbl[:], lbT).then_inc(consts_loaded, 16)
            for g in range(G):
                act.dma_start(xg(g), xT[:, :, g * N:(g + 1) * N]).then_inc(x_loaded[g], 16)
            act.dma_start(u1[:, 0:3 * C], masks).then_inc(consts_loaded, 16)
            act.dma_start(invc[:], inv_count).then_inc(consts_loaded, 16)
            act.wait_ge(lb_diff, 1)
            nc.scalar.activation(oneml[:], oneml[:], ACT.Sigmoid).then_inc(lb_ready, 1)
            act.wait_ge(cols_ready, 1)

            def step(ins):
                chain.inc(ins)
                act.wait_ge(act_chain, chain.value)

            def norm(c, src, before):
                before()
                if c:
                    act.wait_ge(sums_ready, c)
                nc.scalar.activation(scratch[:], src, ACT.Square).then_inc(squares_ready, 1)
                b, uses = plan.norm[c]
                act.wait_ge(bank_full[b], uses + 1)
                nc.scalar.activation(rinv[:], bank[b][:, 0:N], ACT.Ln, scale=1.0 / D_MODEL, bias=eps)\
                    .then_inc(bank_read[b], 1)
                act.wait_ge(bank_read[b], uses + 1)
                nc.scalar.activation(rinv[:], rinv[:], ACT.Exp, scale=-0.5).then_inc(rinv_ready, 1)

            def pre(p, c, g):
                def before():
                    if p == 0:
                        act.wait_ge(x_loaded[g], 16)
                        if g:
                            act.wait_ge(h_ready, g)
                    else:
                        act.wait_ge(x_updated, 3 * (p - 1) + g + 1)
                norm(c, xg(g), before)
                act.wait_ge(hfull_ready, 3 * p + g + 1)
                nc.scalar.activation(hy[:, g, :, 0:N], scratch[:], ACT.Copy).then_inc(hhi_ready, 1)

            def post(q, c, g, src, before):
                def ready():
                    act.wait_ge(h_ready, 3 * (q + 1) + (g if q < 3 else 0))
                    if q == 3 and g:
                        act.wait_ge(x_final, g)
                    before()
                norm(c, src, ready)

            def up(name, f):
                def body(i, kind):
                    jobs = jobs_of(name, kind)
                    n = 0
                    for pos, (t, g) in enumerate(jobs):
                        if t % 2:
                            continue
                        b, uses = plan.job(name, i, pos)
                        if not (isinstance(i, int) and i == 0 and n < 2 and f == 0):
                            act.wait_ge(hidden_ready, i * 6 + (66 * f + n - 1))
                        act.wait_ge(bank_full[b], uses + 1)
                        nc.scalar.activation(sbuf2[:, n % 2, :], bank[b][:, 0:N], ACT.Silu, scale=1.0 / WS)\
                            .then_inc(bank_read[b], 1)
                        n += 1
                loops(act, name, body)

            def evac_y(name, i, pos, m, g):
                b, uses = plan.job(name, i, pos)
                act.wait_ge(bank_full[b], uses + 1)
                nc.scalar.activation(yv[:, g, m, :], bank[b][:, 0:N], ACT.Copy, scale=1.0 / WS)\
                    .then_inc(bank_read[b], 1)
                return lambda: act.wait_ge(bank_read[b], uses + 1)

            def seams(name, i, per_turn, q):
                jobs = jobs_of(name, "G")
                for g in range(G):
                    for pos, (t, gg) in enumerate(jobs):
                        if gg == g:
                            done = evac_y(name, i, pos, per_turn * i + t, g)
                    if q == 2 and g == 0:
                        done()
                        act.dma_start(p_raw, pT).then_inc(p_loaded, 16)
                    c = 3 + 6 * q + 2 * g
                    post(q, c, g, yv[:, g, :, :], done)
                    pre(q + 1, c + 1, g)

            def down(name, q):
                for i in range(3):
                    for pos, (t, g) in enumerate(jobs_of(name, "M")):
                        evac_y(name, i, pos, 2 * i + t, g)
                seams(name, 3, 2, q)

            def head_job(h, kind, t, g):
                pos = jobs_of("heads", kind).index((t, g))
                b, uses = plan.job("heads", h, pos)
                act.wait_ge(bank_full[b], uses + 1)
                return b

            def gcols(a, g):
                return a[:, g * N:(g + 1) * N]

            def wait_piece(head, kind, r):
                b, uses = plan.piece(head, HG_FIRST[kind] + r)
                act.wait_ge(bank_full[b], uses + 1)

            def v_copy(h, kind, g, first):
                if not first:
                    for r in range(3):
                        wait_piece(h - 1, "vT", r)
                b = head_job(h, kind, 0, g)
                nc.scalar.activation(gcols(V, g), bank[b][:, 0:N], ACT.Copy, scale=1.0 / WS).then_inc(bank_read[b], 1)

            def og_sigmoid(h, kind, g):
                b = head_job(h, kind, 1, g)
                dst = hidv[:, h, g, :] if isinstance(h, int) else hidv[:, bass.ds(h, 1), g, :].rearrange(
                    "p a n -> p (a n)")
                nc.scalar.activation(dst, bank[b][:, 0:N], ACT.Sigmoid, scale=1.0 / WS).then_inc(sigmoid_ready, 1)

            def q_sigmoid(h, kind, g):
                b = head_job(h, kind, 2, g)
                nc.scalar.activation(gcols(Q, g), bank[b][:, 0:N], ACT.Sigmoid, scale=1.0 / WS).then_inc(sigmoid_ready, 1)

            def f_sigmoid(h, kind, g):
                b = head_job(h, kind, 3, g)
                nc.scalar.activation(gcols(K_, g), bank[b][:, 0:N], ACT.Sigmoid, scale=-1.0 / WS)\
                    .then_inc(bank_read[b], 1)

            def halves(a, w, right):
                v = a.rearrange("p (b s w) -> p b s w", s=2, w=w // 2)
                return v[:, :, 1 if right else 0, :]

            def onorm(head):
                act.wait_ge(ss_ready, head + 1)
                step(nc.scalar.activation(W[1], W[1], ACT.Ln, scale=1.0 / DK, bias=eps))
                nc.scalar.activation(W[1], W[1], ACT.Exp, scale=-0.5).then_inc(orstd_ready, 1)

            def logf(head):
                act.wait_ge(k_ready, head + 1)
                nc.scalar.activation(GG, K_, ACT.Ln, scale=-1.0, bias=one).then_inc(logf_ready, 1)

            def exps(head, first):
                def e(out, in_, scale, last=False):
                    nc.scalar.activation(out, in_, ACT.Exp, scale=scale).then_inc(exp_ready, 1)
                act.wait_ge(diff_ready, head * 4 + 1)
                e(W[3], W[3], 1.0)
                act.wait_ge(diff_ready, head * 4 + 2)
                e(halves(W[0], 64, False), halves(W[0], 64, False), -1.0)
                e(halves(W[0], 64, True), halves(W[0], 64, True), 1.0)
                act.wait_ge(diff_ready, head * 4 + 3)
                e(halves(W[1], 32, False), halves(W[1], 32, False), -1.0)
                e(halves(W[1], 32, True), halves(W[1], 32, True), 1.0)
                act.wait_ge(diff_ready, head * 4 + 4)
                e(W[4], W[2], -1.0)
                act.wait_ge(exp_ready, head * 9 + 6)
                e(W[2], W[2], 1.0)
                act.wait_ge(cum_ready, head + 1)
                e(W[5], GG, 1.0)
                e(eg[:], GG.rearrange("p (c t) -> p c t", t=C)[:, :, C - 1], 1.0)

            def osquare(head):
                act.wait_ge(o_ready, head + 1)
                nc.scalar.activation(W[4], W[3], ACT.Square).then_inc(osq_ready, 1)

            def state_load(head):
                if not (isinstance(head, int) and head == 0):
                    wait_piece(head - 1, "O", 3)
                else:
                    act.wait_ge(h_ready, 6)
                    act.wait_ge(pads_set, 3)
                src = state_in[head] if isinstance(head, int) else state_in[
                    bass.ds(head, 1), :, :].rearrange("a k v -> k (a v)")
                act.dma_start(Sn(S_IN), src).then_inc(state_loaded, 16)

            def state_store(head):
                act.wait_ge(chain_ready, head + 1)
                for w, n in ((0, PT - 1), (1, S_OUT)):
                    dst = out_states[w, head] if isinstance(head, int) else out_states[
                        w, bass.ds(head, 1), :, :].rearrange("a k v -> k (a v)")
                    act.dma_start(dst, Sn(n)).then_inc(state_stored, 16)

            def head_turn(h, with_norm, u_turn=False):
                hh = h - 1
                if with_norm:
                    onorm(h - 2)
                logf(hh)
                state_load(hh)
                if u_turn:
                    for g in range(G):
                        u_copy(0, g)
                else:
                    for g in range(G):
                        v_copy(h, "M", g, False)
                exps(hh, False)
                if u_turn:
                    for g in range(G):
                        u_copy(1, g)
                    act.wait_ge(operand_ready, hh * 8 + 8)
                    for g in range(G):
                        u_copy(2, g)
                else:
                    for g in range(G):
                        og_sigmoid(h, "M", g)
                    act.wait_ge(operand_ready, hh * 8 + 8)
                    for g in range(G):
                        q_sigmoid(h, "M", g)
                for g in range(G):
                    if u_turn:
                        u_copy(3, g)
                    else:
                        f_sigmoid(h, "M", g)
                    if g == 0:
                        osquare(hh)
                state_store(hh)

            def u_copy(j, g):
                if j == 0:
                    for r in range(3):
                        wait_piece(HEADS - 1, "vT", r)
                b = head_job(HEADS, "M", j, g)
                end = min((g + 1) * N, SEQ) - g * N
                ins = nc.scalar.activation(U[j][:, UP + g * N:UP + g * N + end], bank[b][:, 0:end],
                                           ACT.Copy, scale=1.0 / WS)
                if g < G - 1:
                    ins.then_inc(bank_read[b], 1)
                    return
                nc.scalar.activation(U[j][:, US:US + DEC_SEQ], bank[b][:, end:N], ACT.Copy, scale=1.0 / WS)\
                    .then_inc(bank_read[b], 1)
                act.wait_ge(bank_read[b], plan.job("heads", HEADS, jobs_of("heads", "M").index((j, g)))[1] + 1)
                act.dma_start(U[j][:, US - POOL_BUF:US], pool_in[:, j, :]).then_inc(pool_loaded, 16)
                act.dma_start(out_pools[0, j], U[j][:, UP + SEQ - POOL_BUF:UP + SEQ]).then_inc(pool_stored, 16)
                act.dma_start(out_pools[1, j], U[j][:, US + DEC_SEQ - POOL_BUF:US + DEC_SEQ])\
                    .then_inc(pool_stored, 16)

            def gates():
                with act.Fori(0, 8) as i:
                    for t in range(2):
                        for g in range(G):
                            b, uses = plan.job("gates", i, 3 * t + g)
                            act.wait_ge(mixed_ready, i * 3 + (12 - 3 + g + 1))
                            act.wait_ge(bank_full[b], uses + 1)
                            nc.scalar.activation(hidv[:, TMP0 + t, g, :], bank[b][:, 0:N], ACT.Sigmoid,
                                                 scale=1.0 / WS).then_inc(bank_read[b], 1)

            for g in range(G):
                pre(0, g, g)
            up("ffn1_up", 0)
            act.wait_ge(hidden_ready, 66)
            down("ffn1_down", 0)
            act.wait_ge(pads_set, 3)
            for g in range(G):
                v_copy(0, "G", g, True)
                og_sigmoid(0, "G", g)
                q_sigmoid(0, "G", g)
                f_sigmoid(0, "G", g)
            head_turn(1, False)
            with act.Fori(2, HEADS) as h:
                chain.enter(h, 2, 1)
                head_turn(h, True)
            chain.leave(HEADS - 2)
            head_turn(HEADS, True, True)
            onorm(HEADS - 1)
            act.wait_ge(mixed_ready, 12)
            act.wait_ge(state_stored, 32 * HEADS)
            gates()
            for pos, (t, g) in enumerate(jobs_of("out", "M")):
                evac_y("out", 0, pos, t, g)
            seams("out", 1, 4, 1)
            up("ffn2_up", 1)
            act.wait_ge(hidden_ready, 132)
            down("ffn2_down", 2)
            for i in range(2):
                for g in range(G):
                    for pos, (t, gg) in enumerate(jobs_of("ple", "G")):
                        if gg != g or t % 2:
                            continue
                        n = i * 12 + g * 4 + t // 2
                        b, uses = plan.job("ple", i, pos)
                        if n >= 2:
                            act.wait_ge(yple_ready, n - 1)
                        act.wait_ge(bank_full[b], uses + 1)
                        nc.scalar.activation(sbuf2[:, n % 2, :], bank[b][:, 0:N], ACT.Sigmoid, scale=1.0 / WS)\
                            .then_inc(bank_read[b], 1)
                    if i == 1:
                        post(3, 21 + g, g, hidv[:, Y0:Y0 + KD, g, :],
                             lambda g=g: act.wait_ge(yple_ready, 12 + 4 * g + 4))
            for g in range(G):
                act.wait_ge(x_final, g + 1)
                act.dma_start(out_x[:, :, g * N:(g + 1) * N], xg(g)).then_inc(x_stored, 16)
            act.wait_ge(x_stored, 16 * G)
            act.wait_ge(state_stored, 32 * HEADS)
            act.wait_ge(pool_stored, 32 * 4)

        @block.vector
        def _(dve):
            chain = Tally(vec_chain)

            def step(ins):
                chain.inc(ins)
                dve.wait_ge(vec_chain, chain.value)

            V_ = nc.vector
            dve.wait_ge(consts_loaded, 16 * 5)
            V_.tensor_tensor(oneml[:], lbl[:, 1, :], lbl[:, 0, :], ALU.subtract).then_inc(lb_diff, 1)
            step(V_.memset(mark[:], 0.0))
            step(V_.tensor_copy(msk[:].rearrange("p m (r c) -> p m r c", c=C), u1[:, 0:3 * C].rearrange(
                "p (m c) -> p m c", m=3).unsqueeze(2).to_broadcast([P, 3, 512 // C, C])))
            for n in (1, 5):
                step(V_.tensor_scalar(col[:, n * KD:(n + 1) * KD], col[:, n * KD:(n + 1) * KD], 0.5, None, ALU.mult))
            V_.tensor_scalar(col[:, 8 * KD + 1:8 * KD + 5], col[:, 8 * KD + 1:8 * KD + 5], 1.0 / WS, None, ALU.mult)\
                .then_inc(cols_ready, 1)
            dve.wait_ge(cols_ready, 1)

            def norm(c):
                dve.wait_ge(squares_ready, c + 1)
                V_.tensor_reduce(ssum[:], scratch[:].rearrange("p k n -> p n k"), AX_X, ALU.add)\
                    .then_inc(sums_ready, 1)
                dve.wait_ge(rinv_ready, c + 1)

            def pre(p, c, g):
                norm(c)
                for k in range(KD):
                    ins = V_.scalar_tensor_tensor(out=scratch[:, k, :], in0=xg(g, k), scalar=gain(2 * p, k),
                                                  in1=rinv[:], op0=ALU.mult, op1=ALU.mult)
                ins.then_inc(hfull_ready, 1)
                dve.wait_ge(hhi_ready, 3 * p + g + 1)
                V_.tensor_tensor(hy[:, g, :, N:2 * N], scratch[:], hy[:, g, :, 0:N], ALU.subtract)\
                    .then_inc(h_ready, 1)

            def post(q, c, g, y, done):
                norm(c)
                step(V_.tensor_tensor(y, y, rinv[:].unsqueeze(1).to_broadcast([P, KD, N]), ALU.mult))
                for k in range(KD):
                    ins = V_.scalar_tensor_tensor(out=xg(g, k), in0=y[:, k, :], scalar=gain(2 * q + 1, k),
                                                  in1=xg(g, k), op0=ALU.mult, op1=ALU.add)
                ins.then_inc(done, 1)

            def seams(q):
                for g in range(G):
                    c = 3 + 6 * q + 2 * g
                    post(q, c, g, yv[:, g, :, :], x_updated)
                    dve.wait_ge(x_updated, 3 * q + g + 1)
                    pre(q + 1, c + 1, g)
                    if q == 2 and g == 0:
                        split_p()

            def up(name, f):
                per = 12
                def body(i, kind):
                    jobs = jobs_of(name, kind)
                    n = 0
                    for pos, (t, g) in enumerate(jobs):
                        if not t % 2:
                            continue
                        ba, uses_a = plan.job(name, i, pos - 1)
                        b, uses = plan.job(name, i, pos)
                        s = sbuf2[:, n % 2, :]
                        m = i * 2 + t // 2
                        dst = hid[:, m, g, :] if isinstance(m, int) else hid[:, bass.ds(m, 1), g, :].rearrange(
                            "p a n -> p (a n)")
                        dve.wait_ge(bank_read[ba], uses_a + 1)
                        dve.wait_ge(bank_full[b], uses + 1)
                        V_.scalar_tensor_tensor(out=s, in0=bank[b][:, 0:N], scalar=1.0 / WS, in1=s,
                                                op0=ALU.mult, op1=ALU.mult).then_inc(bank_read[b], 1)
                        dve.wait_ge(bank_read[b], uses + 1)
                        step(V_.tensor_scalar(dst[:, 0:N], s, 1.0, None, ALU.mult))
                        V_.tensor_tensor(dst[:, N:2 * N], s, dst[:, 0:N], ALU.subtract).then_inc(hidden_ready, 1)
                        n += 1
                for a, b, kind in turn_runs(name):
                    if b - a >= 3:
                        with dve.Fori(a, b) as i:
                            chain.enter(i, a, 6)
                            body(i, kind)
                        chain.leave(b - a)
                    else:
                        for i in range(a, b):
                            body(i, kind)

            def gcols(a, g):
                return a[:, g * N:(g + 1) * N]

            def head_bank(h, kind, t, g):
                pos = jobs_of("heads", kind).index((t, g))
                return plan.job("heads", h, pos)

            def slot(h, g):
                return hidv[:, h, g, :] if isinstance(h, int) else hidv[:, bass.ds(h, 1), g, :].rearrange(
                    "p a n -> p (a n)")

            def silu_og(h, kind, g, n):
                b, _ = head_bank(h, kind, 1, g)
                dve.wait_ge(sigmoid_ready, h * 6 + n)
                V_.scalar_tensor_tensor(out=slot(h, g), in0=bank[b][:, 0:N], scalar=1.0 / WS, in1=slot(h, g),
                                        op0=ALU.mult, op1=ALU.mult).then_inc(bank_read[b], 1)

            def silu_q(h, kind, g, n):
                b, _ = head_bank(h, kind, 2, g)
                dve.wait_ge(sigmoid_ready, h * 6 + n)
                V_.scalar_tensor_tensor(out=gcols(Q, g), in0=bank[b][:, 0:N], scalar=1.0 / WS, in1=gcols(Q, g),
                                        op0=ALU.mult, op1=ALU.mult).then_inc(bank_read[b], 1)

            def evac(head, kind, r, f):
                b, uses = plan.piece(head, HG_FIRST[kind] + r)
                dve.wait_ge(bank_full[b], uses + 1)
                if kind in ("L32", "L16", "D16"):
                    if kind != "L32":
                        b1, uses1 = plan.piece(head, HG_FIRST[kind] + r - 2)
                        dve.wait_ge(bank_read[b1], uses1 + 1)
                    n = 2 + 2 * ("L32", "L16", "D16").index(kind) + r
                    V_.tensor_copy(mark[:, n:n + 1], mark[:, 0:1])
                f(bank[b]).then_inc(bank_read[b], 1)
                return b, uses

            def evac_tok(head, kind, dst):
                def copy(b, j0, j1):
                    if j1 == 9:
                        V_.tensor_copy(dst[:, j0 * P:8 * P], b[:, 0:(8 - j0) * P])
                        return V_.tensor_copy(dst[0:C, 8 * P:9 * P], b[0:C, (8 - j0) * P:(9 - j0) * P])
                    return V_.tensor_copy(dst[:, j0 * P:j1 * P], b[:, 0:(j1 - j0) * P])
                for r, (j0, j1) in enumerate(TOK_TILES):
                    evac(head, kind, r, lambda b: copy(b, j0, j1))

            def evac_scores(head, kind, m):
                evac(head, kind, 0, lambda b: V_.copy_predicated(att[:, 0:512], msk[:, m, :], b[:, 0:512]))
                evac(head, kind, 1, lambda b: V_.copy_predicated(att[0:C, 512:512 + C], msk[0:C, m, 0:C],
                                                                 b[0:C, 0:C]))

            def chunks(a, w):
                return a.rearrange("p (b w) -> p b w", w=w)

            def halves(a, w, right):
                v = a.rearrange("p (b s w) -> p b s w", s=2, w=w // 2)
                return v[:, :, 1 if right else 0, :]

            def minus_ref(out, w, at):
                v = chunks(GG, w)
                ref = v[:, :, at:at + 1].to_broadcast([P, TP // w, w])
                V_.tensor_tensor(chunks(out, w), v, ref, ALU.subtract).then_inc(diff_ready, 1)

            def decay_keys(head):
                if isinstance(head, int) and head == 0:
                    kind = "G"
                else:
                    kind = "M"
                for t in (0, 3):
                    for g in range(G):
                        b, uses = head_bank(head, kind, t, g)
                        dve.wait_ge(bank_read[b], uses + 1)
                sc = oneml[:, head:head + 1] if isinstance(head, int) else oneml[:, bass.ds(head, 1)]
                V_.tensor_scalar(K_[:, 0:T], K_[:, 0:T], sc, None, ALU.mult).then_inc(k_ready, 1)

            def onorm(head):
                dve.wait_ge(orstd_ready, head + 1)
                step(V_.scalar_tensor_tensor(out=W[3], in0=W[3], scalar=anorm, in1=W[1],
                                             op0=ALU.mult, op1=ALU.mult))
                s32 = hidv[:, head, :, :] if isinstance(head, int) else hidv[:, bass.ds(head, 1), :, :].rearrange(
                    "p a g n -> p (a g) n")
                s16 = hid[:, head, :, :] if isinstance(head, int) else hid[:, bass.ds(head, 1), :, :].rearrange(
                    "p a g n -> p (a g) n")
                o = W[3][:, 0:T].rearrange("p (g n) -> p g n", g=G)
                step(V_.tensor_tensor(o, o, s32, ALU.mult))
                step(V_.tensor_scalar(s16[:, :, 0:N], o, 1.0, None, ALU.mult))
                V_.tensor_tensor(s16[:, :, N:2 * N], o, s16[:, :, 0:N], ALU.subtract).then_inc(head_ready, 1)

            def operand(out, in0, head, n):
                dve.wait_ge(exp_ready, head * 9 + n)
                V_.tensor_tensor(out, out, in0, ALU.mult).then_inc(operand_ready, 1)

            def head_turn(h, with_norm, u_turn=False):
                hh = h - 1
                evac_tok(hh, "vT", vtok)
                if with_norm:
                    onorm(h - 2)
                dve.wait_ge(logf_ready, hh + 1)
                V_.tensor_tensor_scan(W[2], smask, GG, 0.0, ALU.mult, ALU.add).then_inc(vec_chain, 1)
                chain.n += 1
                dve.wait_ge(vec_chain, chain.value)
                V_.tensor_copy(GG, W[2]).then_inc(cum_ready, 1)
                dve.wait_ge(cum_ready, hh + 1)
                v = chunks(GG, C)
                V_.tensor_tensor(chunks(W[3], C), v[:, :, C - 1:C].to_broadcast([P, NC, C]), v, ALU.subtract)\
                    .then_inc(diff_ready, 1)
                minus_ref(W[0], 64, 31)
                minus_ref(W[1], 32, 15)
                minus_ref(W[2], 16, 7)
                operand(W[3], K_, hh, 1)
                operand(halves(W[0], 64, False), halves(K_, 64, False), hh, 2)
                operand(halves(W[0], 64, True), halves(Q, 64, True), hh, 3)
                operand(halves(W[1], 32, False), halves(K_, 32, False), hh, 4)
                operand(halves(W[1], 32, True), halves(Q, 32, True), hh, 5)
                operand(W[4], K_, hh, 6)
                operand(W[2], Q, hh, 7)
                operand(W[5], Q, hh, 8)
                evac_tok(hh, "kT", ktok)
                evac_scores(hh, "L32", 0)
                evac_scores(hh, "L16", 1)
                evac_scores(hh, "D16", 2)
                if not u_turn:
                    for g in range(G):
                        silu_og(h, "M", g, g + 1)
                dve.wait_ge(exp_ready, hh * 9 + 9)
                dve.wait_ge(state_loaded, hh * 16 + 16)
                if not (isinstance(hh, int) and hh == 0):
                    dve.wait_ge(state_stored, hh * 32)
                for rs in ((0, 1), (2, 3), (4,)):
                    for r in rs:
                        b, uses = plan.piece(hh, HG_FIRST["P"] + r)
                        dve.wait_ge(bank_full[b], uses + 1)
                    for c in sorted(c for r in rs for c in P_CHUNKS[r]):
                        r = next(r for r in rs if c in P_CHUNKS[r])
                        b, uses = plan.piece(hh, HG_FIRST["P"] + r)
                        n = P_CHUNKS[r].index(c)
                        src = bank[b][:, n * P:(n + 1) * P]
                        if c == 0:
                            ins = V_.tensor_copy(Sn(0), src)
                        elif c < PT:
                            ins = V_.scalar_tensor_tensor(out=Sn(c), in0=Sn(c - 1), scalar=eg[:, c:c + 1], in1=src,
                                                          op0=ALU.mult, op1=ALU.add)
                        else:
                            ins = V_.scalar_tensor_tensor(out=Sn(S_OUT), in0=Sn(S_IN), scalar=eg[:, c:c + 1],
                                                          in1=src, op0=ALU.mult, op1=ALU.add)
                        if c == P_CHUNKS[r][-1]:
                            ins.then_inc(bank_read[b], 1)
                            if c < NC - 1:
                                dve.wait_ge(bank_read[b], uses + 1)
                        else:
                            step(ins)
                dve.wait_ge(bank_read[b], uses + 1)
                V_.tensor_copy(mark[:, 1:2], mark[:, 0:1]).then_inc(chain_ready, 1)
                if not u_turn:
                    for g in range(G):
                        silu_q(h, "M", g, g + 4)
                for r, cs in enumerate(O_CHUNKS):
                    dst = chunks(W[3], C)[:, cs[0]:cs[-1] + 1:cs.step, :]
                    b, uses = evac(hh, "O", r, lambda b: V_.tensor_copy(
                        dst, b[:, 0:len(cs) * C].rearrange("p (c t) -> p c t", t=C)))
                dve.wait_ge(bank_read[b], uses + 1)
                V_.tensor_copy(mark[:, 1:2], mark[:, 0:1]).then_inc(o_ready, 1)
                for r in range(3):
                    w = min(512, TP - r * 512)
                    b, uses = evac(hh, "SS", r, lambda b: V_.tensor_copy(W[1][:, r * 512:r * 512 + w], b[:, 0:w]))
                dve.wait_ge(bank_read[b], uses + 1)
                V_.tensor_copy(mark[:, 1:2], mark[:, 0:1]).then_inc(ss_ready, 1)
                if not u_turn:
                    decay_keys(h)

            HEAD_STEPS = 3 + 1 + 12

            def pooling():
                dve.wait_ge(pool_loaded, 64)
                for j, w in enumerate(POOL_WINDOWS):
                    for g in range(G):
                        b, uses = head_bank(HEADS, "M", j, g)
                        dve.wait_ge(bank_read[b], uses + 1)
                    src, n, bufs = U[j], 1, [W[4], W[5]]
                    end = US + DEC_SEQ
                    k = 0
                    while n < w:
                        dst = bufs[k % 2]
                        step(V_.tensor_tensor(dst[:, 2 * n - 1:end], src[:, 2 * n - 1:end],
                                              src[:, n - 1:end - n], ALU.add))
                        src, n, k = dst, 2 * n, k + 1
                    t = bufs[k % 2]
                    step(V_.tensor_tensor(t[:, 0:POOL_BUF], src[:, UP:UP + POOL_BUF], invc[:, j, 0:POOL_BUF], ALU.mult))
                    step(V_.tensor_tensor(t[:, 0:POOL_BUF], t[:, 0:POOL_BUF], U[j][:, UP:UP + POOL_BUF], ALU.subtract))
                    step(V_.scalar_tensor_tensor(out=t[:, POOL_BUF:SEQ], in0=src[:, UP + POOL_BUF:UP + SEQ],
                                                 scalar=1.0 / w, in1=U[j][:, UP + POOL_BUF:UP + SEQ],
                                                 op0=ALU.mult, op1=ALU.subtract))
                    step(V_.scalar_tensor_tensor(out=t[:, SEQ:T], in0=src[:, US:US + DEC_SEQ], scalar=1.0 / w,
                                                 in1=U[j][:, US:US + DEC_SEQ], op0=ALU.mult, op1=ALU.subtract))
                    tg = t[:, 0:T].rearrange("p (g n) -> p g n", g=G)
                    step(V_.tensor_copy(pooled[j][:, :, 0:N], tg))
                    V_.tensor_tensor(pooled[j][:, :, N:2 * N], tg, pooled[j][:, :, 0:N], ALU.subtract)\
                        .then_inc(pooled_ready, 1)
                    dve.wait_ge(pooled_ready, j + 1)

            def mixed():
                for pos, (t, g) in enumerate(jobs_of("pool", "M")):
                    b, uses = plan.job("pool", 0, pos)
                    s = sbuf2[:, pos % 2, :]
                    dst = hid[:, MIX0 + t, g, :]
                    dve.wait_ge(bank_full[b], uses + 1)
                    V_.tensor_scalar(s, bank[b][:, 0:N], pscale(t), None, ALU.mult).then_inc(bank_read[b], 1)
                    dve.wait_ge(bank_read[b], uses + 1)
                    step(V_.tensor_copy(dst[:, 0:N], s))
                    V_.tensor_tensor(dst[:, N:2 * N], s, dst[:, 0:N], ALU.subtract).then_inc(mixed_ready, 1)
                    dve.wait_ge(mixed_ready, pos + 1)

            def gates():
                with dve.Fori(0, 8) as i:
                    chain.enter(i, 0, 6)
                    for t in (2, 3):
                        for g in range(G):
                            bs, uses_s = plan.job("gates", i, 3 * (t - 2) + g)
                            b, uses = plan.job("gates", i, 3 * t + g)
                            s = hidv[:, TMP0 + t - 2, g, :]
                            dve.wait_ge(bank_read[bs], uses_s + 1)
                            dve.wait_ge(bank_full[b], uses + 1)
                            V_.scalar_tensor_tensor(out=s, in0=bank[b][:, 0:N], scalar=1.0 / WS, in1=s,
                                                    op0=ALU.mult, op1=ALU.mult).then_inc(bank_read[b], 1)
                            if t == 3:
                                a = hidv[:, TMP0, g, :]
                                dst = hid[:, bass.ds(i + M0, 1), g, :].rearrange("p a n -> p (a n)")
                                dve.wait_ge(bank_read[b], uses + 1)
                                step(V_.tensor_tensor(a, a, s, ALU.add))
                                step(V_.tensor_scalar(dst[:, 0:N], a, 1.0, None, ALU.mult))
                                V_.tensor_tensor(dst[:, N:2 * N], a, dst[:, 0:N], ALU.subtract).then_inc(mixed_ready, 1)
                chain.leave(8)

            def split_p():
                dve.wait_ge(p_loaded, 16)
                step(V_.tensor_copy(p_split[:, :, 0:N], p_raw))
                V_.tensor_tensor(p_split[:, :, N:2 * N], p_raw, p_split[:, :, 0:N], ALU.subtract)\
                    .then_inc(p_ready, 1)

            for g in range(G):
                dve.wait_ge(x_loaded[g], 16)
                pre(0, g, g)
            up("ffn1_up", 0)
            seams(0)
            V_.memset(V[:, T:TP], 0.0).then_inc(pads_set, 1)
            V_.memset(Q[:, T:TP], 0.0)
            V_.memset(K_[:, T:TP], 0.0).then_inc(pads_set, 1)
            V_.memset(att, 0.0).then_inc(pads_set, 1)
            step(V_.memset(smask, 1.0))
            step(V_.memset(smask.rearrange("p (c t) -> p c t", t=C)[:, :, 0], 0.0))
            for g in range(G):
                silu_og(0, "G", g, 2 * g + 1)
                silu_q(0, "G", g, 2 * g + 2)
            dve.wait_ge(lb_ready, 1)
            decay_keys(0)
            head_turn(1, False)
            with dve.Fori(2, HEADS) as h:
                chain.enter(h, 2, HEAD_STEPS + 0)
                head_turn(h, True)
            chain.leave(HEADS - 2)
            head_turn(HEADS, True, True)
            for j in range(4):
                ins = V_.memset(U[j][:, 0:POOL_BUF], 0.0)
            ins.then_inc(pads_set, 1)
            dve.wait_ge(pads_set, 4)
            onorm(HEADS - 1)
            pooling()
            mixed()
            dve.wait_ge(pool_stored, 32 * 4)
            gates()
            seams(1)
            up("ffn2_up", 1)
            seams(2)
            for i in range(2):
                for g in range(G):
                    for pos, (t, gg) in enumerate(jobs_of("ple", "G")):
                        if gg != g or not t % 2:
                            continue
                        n = i * 12 + g * 4 + t // 2
                        ba, uses_a = plan.job("ple", i, pos - 1)
                        b, uses = plan.job("ple", i, pos)
                        dve.wait_ge(bank_read[ba], uses_a + 1)
                        dve.wait_ge(bank_full[b], uses + 1)
                        V_.scalar_tensor_tensor(out=hidv[:, Y0 + 4 * i + t // 2, g, :], in0=bank[b][:, 0:N],
                                                scalar=1.0 / WS, in1=sbuf2[:, n % 2, :],
                                                op0=ALU.mult, op1=ALU.mult).then_inc(bank_read[b], 1)
                        dve.wait_ge(bank_read[b], uses + 1)
                        V_.tensor_copy(mark[:, 1:2], mark[:, 0:1]).then_inc(yple_ready, 1)
                    if i == 1:
                        post(3, 21 + g, g, hidv[:, Y0:Y0 + KD, g, :], x_final)


def kernel(x_prompt, x_sample, p_prompt, p_sample, state_hgrn, state_pool, norm_gains, lb_logits,
           w_ffn1_gu, w_ffn1_down, w_in, a_gnorm, w_a_up, w_pool, pool_scale, w_b_up, w_out,
           w_ffn2_gu, w_ffn2_down, w_ple_proj, w_ple_gate):
    import numpy as np
    import concourse.bacc as bacc
    from concourse.bass_utils import run_bass_kernel_spmd

    f32 = np.float32

    def tiles(w):
        w = np.asarray(w)
        r, c = w.shape
        return w.reshape(r // P, P, c // P, P).transpose(0, 2, 1, 3)

    stream = []

    def column(w, m):
        stream.append(w[:, m])

    def ffn(gu, dn):
        gu, dn = tiles(gu), tiles(dn)
        for j in range(KF):
            column(gu, j)
            column(gu, KF + j)
        for m in range(KD):
            column(dn, m)

    ffn(w_ffn1_gu[0], w_ffn1_down[0])
    win = tiles(w_in[0])
    q0, f0, i0, og0, up0 = 0, 8, 16, 24, 32
    ga0, gb0 = 36, 44
    for h in range(HEADS):
        for base in (i0, og0, q0, f0):
            column(win, base + h)
    for j in range(4):
        column(win, up0 + j)
    for j in range(4):
        stream.append(np.asarray(w_pool)[0, j][None])
    wa, wb = tiles(w_a_up[0]), tiles(w_b_up[0])
    for m in range(KD):
        column(win, ga0 + m)
        column(win, gb0 + m)
        column(wa, m)
        column(wb, m)
    wo = tiles(w_out[0])
    for m in range(KD):
        column(wo, m)
    ffn(w_ffn2_gu[0], w_ffn2_down[0])
    wg, wp = tiles(w_ple_gate[0]), tiles(w_ple_proj[0])
    for m in range(KD):
        column(wg, m)
        column(wp, m)
    st = np.concatenate(stream, axis=0)
    units = st.shape[0] // UT
    st = np.ascontiguousarray(st.reshape(units, UT, P, P).transpose(0, 2, 1, 3).reshape(units, P, UT * P))

    def feature_major(a, b):
        t = np.concatenate([np.asarray(a), np.asarray(b)], axis=0).T
        return np.ascontiguousarray(t.reshape(t.shape[0] // P, P, T).transpose(1, 0, 2))

    def by_partition(v):
        return np.asarray(v).reshape(-1, P).T

    cols = np.concatenate([by_partition(norm_gains[0]), by_partition(a_gnorm[0]), by_partition(pool_scale[0]),
                           np.full((P, 1), EPS, f32), np.ones((P, 1), f32)], axis=1)
    s, t = np.arange(P)[:, None] % C, np.arange(C)[None, :]
    masks = np.stack([(s < 32) & (t >= 32),
                      (s // 32 == t // 32) & (s % 32 < 16) & (t % 32 >= 16),
                      (s // 16 == t // 16) & (s <= t)], axis=1).astype(f32).reshape(P, 3 * C)
    count = np.array([[1.0 / min(w, n + 1) for n in range(16)] for w in POOL_WINDOWS], f32)
    arrays = {
        "xT": feature_major(x_prompt[0], x_sample[0]),
        "pT": feature_major(p_prompt[0, 0], p_sample[0, 0]).reshape(P, KP * G, N),
        "weights": st,
        "cols": np.ascontiguousarray(cols),
        "lbT": np.ascontiguousarray(np.asarray(lb_logits).reshape(2, HEADS, P).transpose(2, 0, 1)),
        "consts": np.concatenate([np.eye(P, dtype=f32), np.ones((P, P), f32)], axis=1),
        "masks": masks,
        "inv_count": np.ascontiguousarray(np.broadcast_to(count, (P, 4, 16))),
        "state_in": np.ascontiguousarray(state_hgrn[0, 0]),
        "pool_in": np.ascontiguousarray(np.asarray(state_pool)[0, 0].T.reshape(4, P, POOL_BUF).transpose(1, 0, 2)),
    }
    outs = {"out_x": (P, KD, T), "out_states": (2, HEADS, DK, DK), "out_pools": (2, 4, P, POOL_BUF)}

    nc = bacc.Bacc("TRN2", target_bir_lowering=False, num_devices=1)
    args = {n: nc.dram_tensor(n, a.shape, mybir.dt.from_np(a.dtype), kind="ExternalInput").ap()
            for n, a in arrays.items()}
    args.update({n: nc.dram_tensor(n, sh, F32, kind="ExternalOutput").ap() for n, sh in outs.items()})
    build(nc, **args)
    r = run_bass_kernel_spmd(nc, [arrays], core_ids=[0]).results[0]

    y = np.asarray(r["out_x"]).transpose(1, 0, 2).reshape(D_MODEL, T).T
    states, pools = np.asarray(r["out_states"]), np.asarray(r["out_pools"])
    pools = pools.reshape(2, 4 * P, POOL_BUF).transpose(0, 2, 1)
    return (np.ascontiguousarray(y[None, :SEQ]), np.ascontiguousarray(y[None, SEQ:]),
            states[None, 0:1], np.ascontiguousarray(pools[None, 0:1]),
            states[None, 1:2], np.ascontiguousarray(pools[None, 1:2]))
```

```python
from contextlib import ExitStack

import concourse.bass as bass
from concourse import mybir

ALU = mybir.AluOpType
ACT = mybir.ActivationFunctionType
F32 = mybir.dt.float32
F16 = mybir.dt.float16
BF16 = mybir.dt.bfloat16
U8 = mybir.dt.uint8
AX_X = mybir.AxisListType.X

P = 128
D_MODEL, SEQ, DEC_SEQ, D_FF = 1024, 1024, 32, 2816
HEADS, DK = 8, 128
POOL_WINDOWS, POOL_BUF = (2, 4, 8, 16), 15
PLE_DIM = 256
EPS = 1e-6
KD = D_MODEL // P
KF = D_FF // P
KP = PLE_DIM // P
T = SEQ + DEC_SEQ
G = 3
N = T // G
C = 64
NC = (T + C - 1) // C
TP = NC * C
PT = SEQ // C
WS = 32.0
UT = 4
HALF = KD // 2
PARTS, PART = 4, KD // 4

STAGES = {
    "ffn1_up": dict(units=8, turns=11, ks=[KD] * 4, kinds="G" + "P" * 10, banks=6),
    "ffn1_down": dict(units=11, turns=4, ks=[KF] * 2, kinds="MMMG", banks=6),
    "heads": dict(units=8, turns=HEADS + 1, ks=[KD] * 4, kinds="G" + "M" * HEADS, banks=4),
    "gates0": dict(units=8, turns=1, ks=[KD, KD, 1, 1, 1, 1, KD, 4], kinds="M", banks=6),
    "gates": dict(units=7, turns=7, ks=[KD, KD, KD, 4], kinds="M" * 7, banks=6),
    "out": dict(units=8, turns=2, ks=[KD] * 4, kinds="MG", banks=6),
    "ffn2_up": dict(units=8, turns=11, ks=[KD] * 4, kinds="G" + "P" * 10, banks=6),
    "ffn2_down": dict(units=11, turns=4, ks=[KF] * 2, kinds="MMMG", banks=6),
    "ple": dict(units=10, turns=2, ks=[KD, KP] * 4, kinds="GG", banks=6),
}
ORDER = list(STAGES)
RING = max(s["units"] for s in STAGES.values())

HG_PIECES = (["vT"] * 3 + ["kT"] * 3 + ["L32"] * 2 + ["L16"] * 2 + ["D16"] * 2
             + ["P"] * 5 + ["O"] * 4 + ["SS"] * 3)
HG_FIRST = {k: HG_PIECES.index(k) for k in dict.fromkeys(HG_PIECES)}
TOK_TILES = [(0, 4), (4, 7), (7, 9)]
P_CHUNKS = [range(0, 8, 2), range(1, 8, 2), range(8, 16, 2), range(9, 16, 2), range(16, 17)]
O_CHUNKS = [range(0, 16, 2), range(1, 8, 2), range(9, 16, 2), range(16, 17)]
CALLS = [("pre", 0, g) for g in range(G)]
CALLS += [c for q in range(3) for g in range(G) for c in (("post", q, g), ("pre", q + 1, g))]
CALLS += [("post", 3, g) for g in range(G)]
Y_STAGES = ["ffn1_down", "out", "ffn2_down", "ple"]


def y_tiles(name):
    s = STAGES[name]
    step = 2 if name == "ple" else 1
    per = len(s["ks"]) // step
    return [(i, pos, i * per + t // step, g) for i, kind in enumerate(s["kinds"])
            for pos, (t, g) in enumerate(jobs_of(name, kind)) if t % step == step - 1]


EARLY = {"ffn1_down": 1, "out": 2, "ffn2_down": 1}


def y_adds(q, m, g):
    tiles = [(m2, g2) for _, _, m2, g2 in y_tiles(Y_STAGES[q])]
    before = tiles[:tiles.index((m, g)) + 1]
    return q * (KD - 1) * G + sum(m2 > 0 for m2, _ in before)


def jobs_of(name, kind):
    a = len(STAGES[name]["ks"])
    if kind == "M":
        return [(t, g) for t in range(a) for g in range(G)]
    if kind == "G":
        return [(t, g) for g in range(G) for t in range(a)]
    return [(2 * q + r, g) for q in range(a // 2) for g in range(G) for r in range(2)]


class Plan:

    def __init__(self):
        uses = [0] * 8
        unit = 0
        loads = [0] * RING
        first = 0
        self.base, self.unit0, self.load0, self.first = {}, {}, {}, {}
        self.hg_base = None
        self.norm = []
        norm_uses = iter(range(len(CALLS)))

        def norms(k):
            for _ in range(k):
                c = next(norm_uses)
                b = 6 + c % 2
                self.norm.append((b, uses[b]))
                uses[b] += 1

        before = {"ffn1_up": 3, "heads": 6, "ffn2_up": 6, "ple": 6}
        for name in ORDER:
            s = STAGES[name]
            norms(before.get(name, 0))
            self.base[name] = list(uses)
            self.unit0[name] = unit
            self.load0[name] = list(loads)
            per = len(s["ks"]) * G // s["banks"]
            for b in range(s["banks"]):
                uses[b] += per * s["turns"]
            unit += s["units"] * s["turns"]
            self.first[name] = first
            for u in range(s["units"]):
                loads[self.slot(name, u)] += s["turns"]
            first = (first + s["units"]) % RING
            if name == "heads":
                self.hg_base = list(uses)
                for b in range(4, 8):
                    uses[b] += HEADS * len(HG_PIECES) // 4
        norms(3)
        self.units = unit

    def slot(self, name, u):
        return (self.first[name] + u) % RING

    def job(self, name, i, pos):
        s = STAGES[name]
        r = s["banks"]
        per = len(s["ks"]) * G // r
        return pos % r, i * per + (self.base[name][pos % r] + pos // r)

    def piece(self, head, n):
        b = 4 + n % 4
        return b, head * (len(HG_PIECES) // 4) + (self.hg_base[b] + n // 4)

    def freed_by(self, name, i, u):
        s = STAGES[name]
        kind = s["kinds"][i] if isinstance(i, int) else "M" if "M" in s["kinds"] else "P"
        ends, t = [], 0
        for k in s["ks"]:
            ends.append((t // UT, (t + k - 1) // UT))
            t += k
        pos = max(n for n, (t, _) in enumerate(jobs_of(name, kind)) if ends[t][0] <= u <= ends[t][1])
        return self.job(name, i, pos)


class Tally:

    def __init__(self, sem):
        self.sem, self.base, self.n, self.loop = sem, 0, 0, None

    def inc(self, ins, k=1):
        ins.then_inc(self.sem, k)
        self.n += k

    @property
    def value(self):
        return self.base + self.n

    def enter(self, i, first, per):
        at = self.base + self.n
        self.loop = (at, per)
        self.base = i * per + (at - first * per) if per else at
        self.n = 0

    def leave(self, trips):
        at, per = self.loop
        assert self.n == per, (str(self.sem), self.n, per)
        self.base, self.n, self.loop = at + trips * per, 0, None


def turn_runs(name):
    s = STAGES[name]
    runs = []
    for i, k in enumerate(s["kinds"]):
        if runs and runs[-1][2] == k and i > 1:
            runs[-1][1] = i + 1
        else:
            runs.append([i, i + 1, k])
    return runs


def build(nc, xT, pT, weights, cols, lbT, consts, masks, inv_count, state_in, pool_in,
          out_x, out_states, out_pools):
    plan = Plan()
    with ExitStack() as ctx:
        def sb(name, shape, dt):
            return ctx.enter_context(nc.sbuf_tensor(name, shape, dt))

        def sem(name):
            return ctx.enter_context(nc.semaphore(name))

        x = sb("x", [P, KD, T], F32)
        hy = sb("hy", [P, G, KD, 2 * N], F16)
        hid = sb("hid", [P, KF, G, 2 * N], F16)
        ring = sb("ring", [P, RING, 2 * UT * P], F16)
        wtmp = sb("wtmp", [P, UT * P], F32)
        scratch = sb("scratch", [P, KD, N], F32)
        wconst = sb("wconst", [P, 2], F32)
        u1 = sb("u1", [P, TP], F32)
        sbuf2 = sb("sbuf2", [P, 2, N], F32)
        half_sum = sb("half_sum", [P, N], F32)
        rinv = sb("rinv", [P, 2, N], F32)
        cst = sb("cst", [P, 2 * P], F32)
        msk = sb("msk", [P, 3, 512], U8)
        invc = sb("invc", [P, 4, 16], F32)
        col = sb("col", [P, 8 * KD + 1 + 4 + 2], F32)
        lbl = sb("lbl", [P, 2, HEADS], F32)
        oneml = sb("oneml", [P, HEADS], F32)
        mark = sb("mark", [P, 8], F32)
        eg = sb("eg", [P, NC], F32)
        bank = [ctx.enter_context(nc.psum_tensor(f"bank{b}", [P, 512], F32)) for b in range(8)]

        ident, ones = cst[:, 0:P], cst[:, P:2 * P]
        gain = lambda n, k: col[:, n * KD + k:n * KD + k + 1]
        anorm = col[:, 8 * KD:8 * KD + 1]
        pscale = lambda j: col[:, 8 * KD + 1 + j:8 * KD + 2 + j]
        eps, one = col[:, 8 * KD + 5:8 * KD + 6], col[:, 8 * KD + 6:8 * KD + 7]

        def xg(g, k=None):
            return x[:, :, g * N:(g + 1) * N] if k is None else x[:, k, g * N:(g + 1) * N]

        def ssq(g):
            return u1[:, g * N:(g + 1) * N]

        def gate_buf(n):
            return hidv[:, PL0 + 6 * KP, n % 2, :]

        def hyp(g, k, w):
            return hy[:, g, k, w * N:(w + 1) * N]

        yv = hy[:, :, :, :].rearrange("p g k n -> p (g k n)").bitcast(F32).rearrange(
            "p (g k n) -> p g k n", g=G, k=KD)
        hidf = hid[:, :, :, :].rearrange("p s g n -> p (s g n)").bitcast(F32)
        hidv = hidf.rearrange("p (s g n) -> p s g n", s=KF, g=G)
        area = hidf[:, 8 * T:KF * T]

        def arr(n):
            return area[:, n * TP:(n + 1) * TP]

        V, Q, K_, GG = arr(0), arr(1), arr(2), arr(3)
        W = [arr(4 + n) for n in range(6)]
        vtok = area[:, 10 * TP:10 * TP + 9 * P]
        ktok = area[:, 10 * TP + 9 * P:10 * TP + 18 * P]
        att = area[:, 10 * TP + 18 * P:10 * TP + 18 * P + 9 * C]
        a0 = 10 * TP + 18 * P + 9 * C
        smask = area[:, a0:a0 + TP // 2].bitcast(BF16)
        S = scratch[:, :, :].rearrange("p k n -> p (k n)")[:, 0:18 * P]

        def Sn(n):
            return S[:, n * P:(n + 1) * P]

        S_IN, S_OUT = 16, 17
        U = [V, u1[:, :], Q, K_]
        UP, US = POOL_BUF, POOL_BUF + SEQ + POOL_BUF
        pooled = [u[:, 0:T].bitcast(F16).rearrange("p (g n) -> p g n", g=G) for u in U]
        TMP_FIRST = [W[2], W[4]]
        M0, TMP0, MIX0 = 8, 16, 18
        Y0, PL0 = 0, 8
        p_raw = hidv[:, PL0 + 3 * KP:PL0 + 6 * KP, 0, :]
        p_split = hid[:, PL0:PL0 + 3 * KP, 0, :]

        slot_loaded = [sem(f"slot_loaded{u}") for u in range(RING)]
        unit_ready = sem("unit_ready")
        bank_full = [sem(f"bank_full{b}") for b in range(8)]
        bank_read = [sem(f"bank_read{b}") for b in range(8)]
        ones_loaded = sem("ones_loaded")
        cols_loaded = sem("cols_loaded")
        rest_loaded = sem("rest_loaded")
        x_loaded = [sem(f"x_loaded{n}") for n in range(2 * G)]
        p_loaded = sem("p_loaded")
        p_ready = sem("p_ready")
        cols_ready = sem("cols_ready")
        lb_diff = sem("lb_diff")
        lb_ready = sem("lb_ready")
        squares_ready = sem("squares_ready")
        sums_ready = sem("sums_ready")
        rinv_ready = sem("rinv_ready")
        ysq_ready = sem("ysq_ready")
        ysq_added = sem("ysq_added")
        x_updated = sem("x_updated")
        hfull_ready = sem("hfull_ready")
        hhi_ready = sem("hhi_ready")
        h_ready = sem("h_ready")
        hidden_ready = sem("hidden_ready")
        sigmoid_ready = sem("sigmoid_ready")
        k_ready = sem("k_ready")
        logf_ready = sem("logf_ready")
        cum_ready = sem("cum_ready")
        diff_ready = sem("diff_ready")
        exp_ready = sem("exp_ready")
        operand_ready = sem("operand_ready")
        o_ready = sem("o_ready")
        osq_ready = sem("osq_ready")
        ss_ready = sem("ss_ready")
        orstd_ready = sem("orstd_ready")
        head_ready = sem("head_ready")
        chain_ready = sem("chain_ready")
        state_loaded = sem("state_loaded")
        state_stored = sem("state_stored")
        pads_set = sem("pads_set")
        wconst_set = sem("wconst_set")
        pool_loaded = [sem(f"pool_loaded{j}") for j in range(4)]
        u_ready = sem("u_ready")
        pool_stored = [sem(f"pool_stored{j}") for j in range(4)]
        pooled_ready = sem("pooled_ready")
        mixed_hi_ready = sem("mixed_hi_ready")
        mixed_ready = sem("mixed_ready")
        x_stored = sem("x_stored")
        vec_chain = sem("vec_chain")
        act_chain = sem("act_chain")
        pool_chain = sem("pool_chain")

        block = ctx.enter_context(nc.Block())

        def loops(eng, name, body, runs=None):
            for a, b, kind in runs or turn_runs(name):
                if b - a >= 3:
                    with eng.Fori(a, b) as i:
                        body(i, kind)
                else:
                    for i in range(a, b):
                        body(i, kind)

        def load_x(eng, g):
            for hf in range(2):
                ks = slice(hf * HALF, (hf + 1) * HALF)
                eng.dma_start(x[:, ks, g * N:(g + 1) * N], xT[:, ks, g * N:(g + 1) * N])\
                    .then_inc(x_loaded[2 * g + hf], 16)

        @block.sync
        def _(sp):
            load_x(sp, 0)
            last = {}

            def load(name, i, u, freed, unit0=False):
                if unit0 and u == 2:
                    sp.wait_ge(x_loaded[1], 16)
                if freed is not None:
                    sp.wait_ge(bank_full[freed[0]], freed[1] + 1)
                n = i * STAGES[name]["units"] + (plan.unit0[name] + u)
                slot = plan.slot(name, u)
                src = weights[n, :, :] if isinstance(n, int) else weights[
                    bass.ds(n, 1), :, :].rearrange("a p c -> p (a c)")
                sp.dma_start(ring[:, slot, :].bitcast(F32), src).then_inc(slot_loaded[slot], 16)

            for name in ORDER:
                s = STAGES[name]
                runs = []
                for i in range(s["turns"]):
                    k = s["kinds"][i - 1] if i else None
                    if runs and runs[-1][2] == k:
                        runs[-1][1] = i + 1
                    else:
                        runs.append([i, i + 1, k])
                for a, b, k in runs:
                    if b - a >= 3:
                        with sp.Fori(a, b) as i:
                            for u in range(s["units"]):
                                load(name, i, u, plan.freed_by(name, i - 1, u))
                    else:
                        for i in range(a, b):
                            for u in range(s["units"]):
                                load(name, i, u, plan.freed_by(name, i - 1, u) if i else last.get(plan.slot(name, u)),
                                     name == ORDER[0] and i == 0)
                for u in range(s["units"]):
                    last[plan.slot(name, u)] = plan.freed_by(name, s["turns"] - 1, u)
            for g in range(G):
                for hf in range(2):
                    ks = slice(hf * HALF, (hf + 1) * HALF)
                    sp.wait_ge(x_updated, 2 * (9 + g) + hf + 1)
                    sp.dma_start(out_x[:, ks, g * N:(g + 1) * N], x[:, ks, g * N:(g + 1) * N]).then_inc(x_stored, 16)
            sp.wait_ge(x_stored, 16 * 2 * G)

        @block.gpsimd
        def _(pool):
            chain = Tally(pool_chain)
            done = Tally(unit_ready)
            ws_all = wconst[:, 0:1].to_broadcast([P, UT * P])
            one_all = wconst[:, 1:2].to_broadcast([P, UT * P])
            nc.gpsimd.memset(wconst[:, 0:1], WS).then_inc(wconst_set, 1)
            nc.gpsimd.memset(wconst[:, 1:2], 1.0).then_inc(wconst_set, 1)
            pool.wait_ge(wconst_set, 2)

            def split(name, i, u):
                slot = plan.slot(name, u)
                raw = ring[:, slot, :].bitcast(F32)
                hi, lo = ring[:, slot, 0:UT * P], ring[:, slot, UT * P:2 * UT * P]
                pool.wait_ge(slot_loaded[slot], i * 16 + 16 * (plan.load0[name][slot] + 1))
                if not (isinstance(i, int) and name == ORDER[0] and i == 0 and u == 0):
                    pool.wait_ge(unit_ready, done.value)
                chain.inc(nc.gpsimd.tensor_tensor(wtmp[:], raw, ws_all, ALU.mult))
                pool.wait_ge(pool_chain, chain.value)
                chain.inc(nc.gpsimd.tensor_tensor(hi, wtmp[:], one_all, ALU.mult))
                pool.wait_ge(pool_chain, chain.value)
                done.inc(nc.gpsimd.tensor_tensor(lo, wtmp[:], hi, ALU.subtract))

            for name in ORDER:
                s = STAGES[name]
                first = 1 if name == ORDER[0] else 0
                for i in range(first):
                    for u in range(s["units"]):
                        split(name, i, u)
                if s["turns"] - first >= 3:
                    with pool.Fori(first, s["turns"]) as i:
                        chain.enter(i, first, 2 * s["units"])
                        done.enter(i, first, s["units"])
                        for u in range(s["units"]):
                            split(name, i, u)
                    chain.leave(s["turns"] - first)
                    done.leave(s["turns"] - first)
                else:
                    for i in range(first, s["turns"]):
                        for u in range(s["units"]):
                            split(name, i, u)

        @block.tensor
        def _(pe):
            def take(b, uses):
                if not (isinstance(uses, int) and uses == 0):
                    pe.wait_ge(bank_read[b], uses)

            def turn(name, i, kind, rhs, ready=None, hooks=None):
                s = STAGES[name]
                starts = [sum(s["ks"][:t]) for t in range(len(s["ks"]))]
                seen = set()
                for pos, (t, g) in enumerate(jobs_of(name, kind)):
                    b, uses = plan.job(name, i, pos)
                    take(b, uses)
                    for k in range(s["ks"][t]):
                        if ready:
                            ready(i, t, g, pos, k)
                        u, q = divmod(starts[t] + k, UT)
                        if u not in seen:
                            seen.add(u)
                            pe.wait_ge(unit_ready, i * s["units"] + (plan.unit0[name] + u + 1))
                        slot = plan.slot(name, u)
                        whi = ring[:, slot, q * P:(q + 1) * P]
                        wlo = ring[:, slot, (UT + q) * P:(UT + q + 1) * P]
                        out = bank[b][:, 0:N]
                        end = k == s["ks"][t] - 1
                        nc.tensor.matmul(out, whi, rhs(t, k, g, 0), start=(k == 0), stop=False)
                        nc.tensor.matmul(out, whi, rhs(t, k, g, 1), start=False, stop=False)
                        mm = nc.tensor.matmul(out, wlo, rhs(t, k, g, 0), start=False, stop=end)
                        if end:
                            mm.then_inc(bank_full[b], 1)
                        elif hooks and (pos, k) in hooks:
                            for f in hooks[(pos, k)]:
                                f()
                    if hooks and (pos, None) in hooks:
                        for f in hooks[(pos, None)]:
                            f()

            def norm(c):
                b, uses = plan.norm[c]
                what, n, g = CALLS[c]
                if what == "pre":
                    pe.wait_ge(sums_ready, 3 * n + g + 1)
                else:
                    pe.wait_ge(ysq_added, y_adds(n, KD - 1, g))
                take(b, uses)
                nc.tensor.matmul(bank[b][:, 0:N], ones, ssq(g), start=True, stop=True).then_inc(bank_full[b], 1)

            def h_rhs(t, k, g, w):
                return hyp(g, k, w)

            def hid_rhs(base):
                return lambda t, k, g, w: hid[:, base + k, g, w * N:(w + 1) * N]

            def h_wait(p):
                def ready(i, t, g, pos, k):
                    if isinstance(i, int) and i == 0 and t == 0 and k % PART == 0:
                        pe.wait_ge(h_ready, PARTS * (3 * p + g) + k // PART + 1)
                return ready

            def up(name, p, hooks):
                for a, b, kind in turn_runs(name):
                    if a == 0:
                        turn(name, 0, kind, h_rhs, h_wait(p), hooks)
                    else:
                        with pe.Fori(a, b) as i:
                            turn(name, i, kind, h_rhs)

            def down(name, f, hooks):
                def ready(i, t, g, pos, k):
                    if isinstance(i, int) and i == 0 and pos == 0 and k == 0:
                        pe.wait_ge(hidden_ready, 66 * (f + 1))
                turn(name, 0, "M", hid_rhs(0), ready)
                for i in (1, 2):
                    turn(name, i, "M", hid_rhs(0))
                turn(name, 3, "G", hid_rhs(0), None, hooks)

            def calls(*cs):
                return [lambda c=c: norm(c) for c in cs]

            def piece(head, n, fill):
                b, uses = plan.piece(head, n)
                take(b, uses)
                fill(b).then_inc(bank_full[b], 1)

            def head_transposes(head, kind, src):
                for r, (j0, j1) in enumerate(TOK_TILES):
                    def fill(b, j0=j0, j1=j1):
                        for j in range(j0, j1):
                            w = min(P, TP - j * P)
                            last = nc.tensor.transpose(bank[b][0:w, (j - j0) * P:(j - j0 + 1) * P],
                                                       src[:, j * P:j * P + w], ident)
                        return last
                    piece(head, HG_FIRST[kind] + r, fill)

            def head_scores(head, kind, kk, qq):
                for r, (c0, c1) in enumerate([(0, PT), (PT, NC)]):
                    def fill(b, c0=c0, c1=c1):
                        for c in range(c0, c1):
                            h0 = C * (c % 2)
                            last = nc.tensor.matmul(bank[b][h0:h0 + C, (c - c0) // 2 * C:((c - c0) // 2 + 1) * C],
                                                    kk[:, c * C:(c + 1) * C], qq[:, c * C:(c + 1) * C],
                                                    start=True, stop=True)
                        return last
                    piece(head, HG_FIRST[kind] + r, fill)

            def head_updates(head, rs):
                for r in rs:
                    def fill(b, r=r):
                        for n, c in enumerate(P_CHUNKS[r]):
                            h0 = C * (c % 2)
                            j = c // 2
                            last = nc.tensor.matmul(bank[b][:, n * P:(n + 1) * P],
                                                    ktok[h0:h0 + C, j * P:(j + 1) * P],
                                                    vtok[h0:h0 + C, j * P:(j + 1) * P], start=True, stop=True)
                        return last
                    piece(head, HG_FIRST["P"] + r, fill)

            def head_outputs(head):
                pe.wait_ge(chain_ready, head * 1 + 1)
                for r, cs in enumerate(O_CHUNKS):
                    def fill(b, cs=cs):
                        for n, c in enumerate(cs):
                            h0, j = C * (c % 2), c // 2
                            nc.tensor.matmul(bank[b][:, n * C:(n + 1) * C], vtok[h0:h0 + C, j * P:(j + 1) * P],
                                             att[h0:h0 + C, j * C:(j + 1) * C],
                                             start=(n == 0), stop=True, skip_group_check=True)
                        for n, c in enumerate(cs):
                            if c:
                                last = nc.tensor.matmul(bank[b][:, n * C:(n + 1) * C],
                                                        Sn(c - 1 if c < PT else S_IN), W[5][:, c * C:(c + 1) * C],
                                                        start=False, stop=True, skip_group_check=True)
                        return last
                    piece(head, HG_FIRST["O"] + r, fill)

            def head_sumsq(head):
                pe.wait_ge(osq_ready, head * 1 + 1)
                for r in range(3):
                    c0, c1 = r * 512, min(r * 512 + 512, TP)
                    def fill(b, c0=c0, c1=c1):
                        return nc.tensor.matmul(bank[b][:, 0:c1 - c0], ones, W[4][:, c0:c1], start=True, stop=True)
                    piece(head, HG_FIRST["SS"] + r, fill)

            def operands(head, n):
                pe.wait_ge(operand_ready, head * 8 + n)

            def head_hooks(h):
                hh = h - 1
                return {
                    (0, 3): [lambda: pe.wait_ge(k_ready, h), lambda: head_transposes(hh, "vT", V)],
                    (4, None): [lambda: operands(hh, 1), lambda: head_transposes(hh, "kT", W[3])],
                    (5, None): [lambda: operands(hh, 3), lambda: head_scores(hh, "L32", W[0], W[0])],
                    (6, None): [lambda: operands(hh, 5), lambda: head_scores(hh, "L16", W[1], W[1]),
                                lambda: operands(hh, 7), lambda: head_scores(hh, "D16", W[4], W[2])],
                    (7, None): [lambda: head_updates(hh, range(4))],
                    (8, 4): [lambda: head_updates(hh, [4])],
                    (9, None): [lambda: operands(hh, 8), lambda: head_outputs(hh)],
                    (11, None): [lambda: head_sumsq(hh)],
                }

            pe.wait_ge(ones_loaded, 16)
            norm(0)
            up("ffn1_up", 0, {(1, 2): calls(1), (4, 3): calls(2)})
            down("ffn1_down", 0, {(2, 5): calls(3), (3, 9): calls(4), (4, 5): calls(5), (5, 9): calls(6)})
            turn("heads", 0, "G", h_rhs, h_wait(1), {(0, 5): calls(7), (3, 6): calls(8)})
            with pe.Fori(1, HEADS + 1) as h:
                turn("heads", h, "M", h_rhs, None, head_hooks(h))

            def gate_rhs(t, k, g, w):
                if t < 2:
                    return hyp(g, k, w)
                return hid[:, (0 if t == 2 else MIX0) + k, g, w * N:(w + 1) * N]

            def first_gate_rhs(t, k, g, w):
                if 2 <= t < 6:
                    return pooled[t - 2][:, g, w * N:(w + 1) * N]
                return gate_rhs(t if t < 2 else t - 4, k, g, w)

            def first_gate_ready(i, t, g, pos, k):
                if 2 <= t < 6 and g == 0:
                    pe.wait_ge(pooled_ready, t - 1)
                if t == 6 and g == 0 and k in (0, KD - 1):
                    pe.wait_ge(head_ready, HEADS if k else HEADS - 1)
                if t == 7 and g == 0 and k == 0:
                    pe.wait_ge(mixed_ready, 1)

            turn("gates0", 0, "M", first_gate_rhs, first_gate_ready)
            with pe.Fori(0, KD - 1) as i:
                turn("gates", i, "M", gate_rhs)
            pe.wait_ge(mixed_ready, 1 + 24)
            turn("out", 0, "M", hid_rhs(M0))
            turn("out", 1, "G", hid_rhs(M0), None,
                 {(4, 5): calls(9), (7, 6): calls(10), (9, 5): calls(11)})
            up("ffn2_up", 2, {(1, 2): calls(12), (3, 3): calls(13), (5, None): calls(14)})
            down("ffn2_down", 1, {(2, 5): calls(15), (3, 9): calls(16), (4, 5): calls(17), (5, 9): calls(18)})

            def ple_rhs(t, k, g, w):
                return hyp(g, k, w) if t % 2 == 0 else p_split[:, G * k + g, w * N:(w + 1) * N]

            def ple_ready(i, t, g, pos, k):
                h_wait(3)(i, t, g, pos, k)
                if i == 0 and t == 1 and g == 0 and k == 0:
                    pe.wait_ge(p_ready, 1)

            turn("ple", 0, "G", ple_rhs, ple_ready, {(0, 5): calls(19), (5, None): calls(20)})
            turn("ple", 1, "G", ple_rhs, None, {(8, 5): calls(21), (16, 5): calls(22)})
            norm(23)

        @block.scalar
        def _(act):
            chain = Tally(act_chain)

            act.dma_start(col[:], cols).then_inc(cols_loaded, 16)
            act.dma_start(cst[:], consts).then_inc(ones_loaded, 16)
            load_x(act, 1)
            load_x(act, 2)
            act.dma_start(lbl[:], lbT).then_inc(rest_loaded, 16)
            act.dma_start(hidf[:, 0:3 * C], masks).then_inc(rest_loaded, 16)
            act.dma_start(invc[:], inv_count).then_inc(rest_loaded, 16)

            def step(ins):
                chain.inc(ins)
                act.wait_ge(act_chain, chain.value)

            def ln_exp_tables():
                nc.scalar.preload_act_table_set("natural_log_exp_and_others")

            def norm(c):
                if c >= 2:
                    what, n, g = CALLS[c - 2]
                    if what == "pre":
                        act.wait_ge(hfull_ready, PARTS * (3 * n + g + 1))
                    else:
                        act.wait_ge(x_updated, 2 * (3 * n + g + 1))
                b, uses = plan.norm[c]
                r = rinv[:, c % 2, :]
                if c == 0:
                    act.wait_ge(cols_ready, 1)
                act.wait_ge(bank_full[b], uses + 1)
                nc.scalar.activation(r, bank[b][:, 0:N], ACT.Ln, scale=1.0 / D_MODEL, bias=eps)\
                    .then_inc(bank_read[b], 1)
                act.wait_ge(bank_read[b], uses + 1)
                nc.scalar.activation(r, r, ACT.Exp, scale=-0.5).then_inc(rinv_ready, 1)

            def pre(p, c, g, between=None):
                n = 3 * p + g
                for hf in range(2):
                    ks = slice(hf * HALF, (hf + 1) * HALF)
                    if p == 0:
                        act.wait_ge(x_loaded[2 * g + hf], 16)
                    else:
                        act.wait_ge(x_updated, 2 * (n - 3) + hf + 1)
                    if n:
                        act.wait_ge(h_ready, PARTS * (n - 1) + 2 * hf + 2)
                    nc.scalar.activation(scratch[:, ks, :], xg(g)[:, ks, :], ACT.Square).then_inc(squares_ready, 1)
                if between:
                    between()
                norm(c)
                for part in range(PARTS):
                    ks = slice(part * PART, (part + 1) * PART)
                    act.wait_ge(hfull_ready, PARTS * n + part + 1)
                    nc.scalar.activation(hy[:, g, ks, 0:N], scratch[:, ks, :], ACT.Copy).then_inc(hhi_ready, 1)

            def up(name, f):
                def body(i, kind):
                    jobs = jobs_of(name, kind)
                    n = 0
                    for pos, (t, g) in enumerate(jobs):
                        if t % 2:
                            continue
                        b, uses = plan.job(name, i, pos)
                        if not (isinstance(i, int) and i == 0 and n < 2 and f == 0):
                            act.wait_ge(hidden_ready, i * 6 + (66 * f + n - 1))
                        act.wait_ge(bank_full[b], uses + 1)
                        nc.scalar.activation(sbuf2[:, n % 2, :], bank[b][:, 0:N], ACT.Silu, scale=1.0 / WS)\
                            .then_inc(bank_read[b], 1)
                        n += 1
                loops(act, name, body)

            def square_y(q, m, g, src, scale=1.0):
                if m == 0:
                    return nc.scalar.activation(ssq(g), src, ACT.Square, scale=scale)
                n = y_adds(q, m, g) - 1
                if n >= 2:
                    act.wait_ge(ysq_added, n - 1)
                return nc.scalar.activation(sbuf2[:, n % 2, :], src, ACT.Square, scale=scale)

            def evac_y(name, q, i, pos, m, g):
                b, uses = plan.job(name, i, pos)
                act.wait_ge(bank_full[b], uses + 1)
                ins = square_y(q, m, g, bank[b][:, 0:N], 1.0 / WS)
                if m:
                    ins.then_inc(ysq_ready, 1)
                nc.scalar.activation(yv[:, g, m, :], bank[b][:, 0:N], ACT.Copy, scale=1.0 / WS)\
                    .then_inc(bank_read[b], 1)

            def seams(name, q):
                last = [[t for t in y_tiles(name) if t[0] == STAGES[name]["turns"] - 1 and t[3] == g]
                        for g in range(G)] + [[]]
                early = EARLY[name]
                ln_exp_tables()

                def evac(tiles):
                    for i, pos, m, g in tiles:
                        evac_y(name, q, i, pos, m, g)

                evac(last[0][:early])
                for g in range(G):
                    evac(last[g][early:])
                    if q == 2 and g == 0:
                        act.dma_start(p_raw, pT).then_inc(p_loaded, 16)
                    c = 3 + 6 * q + 2 * g
                    norm(c)
                    pre(q + 1, c + 1, g, lambda: evac(last[g + 1][:early]))

            def down(name, q):
                for i, pos, m, g in y_tiles(name):
                    if i < STAGES[name]["turns"] - 1:
                        evac_y(name, q, i, pos, m, g)
                seams(name, q)

            def head_job(h, kind, t, g):
                pos = jobs_of("heads", kind).index((t, g))
                b, uses = plan.job("heads", h, pos)
                act.wait_ge(bank_full[b], uses + 1)
                return b

            def gcols(a, g):
                return a[:, g * N:(g + 1) * N]

            def wait_piece(head, kind, r):
                b, uses = plan.piece(head, HG_FIRST[kind] + r)
                act.wait_ge(bank_full[b], uses + 1)

            def v_copy(h, kind, g, first):
                if not first:
                    for r in range(3):
                        wait_piece(h - 1, "vT", r)
                b = head_job(h, kind, 0, g)
                nc.scalar.activation(gcols(V, g), bank[b][:, 0:N], ACT.Copy, scale=1.0 / WS).then_inc(bank_read[b], 1)

            def og_sigmoid(h, kind, g):
                b = head_job(h, kind, 1, g)
                dst = hidv[:, h, g, :] if isinstance(h, int) else hidv[:, bass.ds(h, 1), g, :].rearrange(
                    "p a n -> p (a n)")
                nc.scalar.activation(dst, bank[b][:, 0:N], ACT.Sigmoid, scale=1.0 / WS).then_inc(sigmoid_ready, 1)

            def q_sigmoid(h, kind, g):
                b = head_job(h, kind, 2, g)
                nc.scalar.activation(gcols(Q, g), bank[b][:, 0:N], ACT.Sigmoid, scale=1.0 / WS).then_inc(sigmoid_ready, 1)

            def f_sigmoid(h, kind, g):
                b = head_job(h, kind, 3, g)
                nc.scalar.activation(gcols(K_, g), bank[b][:, 0:N], ACT.Sigmoid, scale=-1.0 / WS)\
                    .then_inc(bank_read[b], 1)

            def halves(a, w, right):
                v = a.rearrange("p (b s w) -> p b s w", s=2, w=w // 2)
                return v[:, :, 1 if right else 0, :]

            def onorm(head):
                act.wait_ge(ss_ready, head + 1)
                step(nc.scalar.activation(W[1], W[1], ACT.Ln, scale=1.0 / DK, bias=eps))
                nc.scalar.activation(W[1], W[1], ACT.Exp, scale=-0.5).then_inc(orstd_ready, 1)

            def logf(head):
                act.wait_ge(k_ready, head + 1)
                nc.scalar.activation(GG, K_, ACT.Ln, scale=-1.0, bias=one).then_inc(logf_ready, 1)

            def exps(head, first):
                def e(out, in_, scale, last=False):
                    nc.scalar.activation(out, in_, ACT.Exp, scale=scale).then_inc(exp_ready, 1)
                act.wait_ge(diff_ready, head * 4 + 1)
                e(W[3], W[3], 1.0)
                act.wait_ge(diff_ready, head * 4 + 2)
                e(halves(W[0], 64, False), halves(W[0], 64, False), -1.0)
                e(halves(W[0], 64, True), halves(W[0], 64, True), 1.0)
                act.wait_ge(diff_ready, head * 4 + 3)
                e(halves(W[1], 32, False), halves(W[1], 32, False), -1.0)
                e(halves(W[1], 32, True), halves(W[1], 32, True), 1.0)
                act.wait_ge(diff_ready, head * 4 + 4)
                e(W[4], W[2], -1.0)
                act.wait_ge(exp_ready, head * 9 + 6)
                e(W[2], W[2], 1.0)
                act.wait_ge(cum_ready, head + 1)
                e(W[5], GG, 1.0)
                e(eg[:], GG.rearrange("p (c t) -> p c t", t=C)[:, :, C - 1], 1.0)

            def osquare(head):
                act.wait_ge(o_ready, head + 1)
                nc.scalar.activation(W[4], W[3], ACT.Square).then_inc(osq_ready, 1)

            def state_load(head):
                if not (isinstance(head, int) and head == 0):
                    wait_piece(head - 1, "O", 3)
                else:
                    act.wait_ge(h_ready, PARTS * 6)
                    act.wait_ge(pads_set, 3)
                src = state_in[head] if isinstance(head, int) else state_in[
                    bass.ds(head, 1), :, :].rearrange("a k v -> k (a v)")
                act.dma_start(Sn(S_IN), src).then_inc(state_loaded, 16)

            def state_store(head):
                act.wait_ge(chain_ready, head + 1)
                for w, n in ((0, PT - 1), (1, S_OUT)):
                    dst = out_states[w, head] if isinstance(head, int) else out_states[
                        w, bass.ds(head, 1), :, :].rearrange("a k v -> k (a v)")
                    act.dma_start(dst, Sn(n)).then_inc(state_stored, 16)

            def head_turn(h, with_norm, u_turn=False):
                hh = h - 1
                ln_exp_tables()
                if with_norm:
                    onorm(h - 2)
                logf(hh)
                state_load(hh)
                if u_turn:
                    for g in range(G):
                        u_copy(0, g)
                else:
                    for g in range(G):
                        v_copy(h, "M", g, False)
                exps(hh, False)
                if u_turn:
                    for g in range(G):
                        u_copy(1, g)
                    act.wait_ge(operand_ready, hh * 8 + 8)
                    for g in range(G):
                        u_copy(2, g)
                else:
                    for g in range(G):
                        og_sigmoid(h, "M", g)
                    act.wait_ge(operand_ready, hh * 8 + 8)
                    for g in range(G):
                        q_sigmoid(h, "M", g)
                for g in range(G):
                    if u_turn:
                        u_copy(3, g)
                    else:
                        f_sigmoid(h, "M", g)
                    if g == 0:
                        osquare(hh)
                state_store(hh)

            def u_copy(j, g):
                if j == 0:
                    for r in range(3):
                        wait_piece(HEADS - 1, "vT", r)
                b = head_job(HEADS, "M", j, g)
                end = min((g + 1) * N, SEQ) - g * N
                ins = nc.scalar.activation(U[j][:, UP + g * N:UP + g * N + end], bank[b][:, 0:end],
                                           ACT.Copy, scale=1.0 / WS)
                if g < G - 1:
                    ins.then_inc(bank_read[b], 1)
                    return
                nc.scalar.activation(U[j][:, US:US + DEC_SEQ], bank[b][:, end:N], ACT.Copy, scale=1.0 / WS)\
                    .then_inc(bank_read[b], 1)
                act.wait_ge(bank_read[b], plan.job("heads", HEADS, jobs_of("heads", "M").index((j, g)))[1] + 1)
                act.dma_start(U[j][:, US - POOL_BUF:US], pool_in[:, j, :]).then_inc(pool_loaded[j], 16)
                act.dma_start(out_pools[0, j], U[j][:, UP + SEQ - POOL_BUF:UP + SEQ]).then_inc(pool_stored[j], 16)
                act.dma_start(out_pools[1, j], U[j][:, US + DEC_SEQ - POOL_BUF:US + DEC_SEQ])\
                    .then_inc(pool_stored[j], 16)

            def gate(name, i, t, g, dst):
                b, uses = plan.job(name, i, 3 * t + g)
                act.wait_ge(bank_full[b], uses + 1)
                nc.scalar.activation(dst, bank[b][:, 0:N], ACT.Sigmoid, scale=1.0 / WS).then_inc(bank_read[b], 1)

            def gates():
                for t in range(2):
                    for g in range(G):
                        gate("gates0", 0, t, g, gcols(TMP_FIRST[t], g))
                for n, (t, g) in enumerate((t, g) for t in range(4) for g in range(G)):
                    b, uses = plan.job("gates0", 0, 6 + n)
                    act.wait_ge(bank_full[b], uses + 1)
                    nc.scalar.activation(hid[:, MIX0 + t, g, 0:N], bank[b][:, 0:N], ACT.Copy, scale=pscale(t))\
                        .then_inc(mixed_hi_ready, 1)
                with act.Fori(0, KD - 1) as i:
                    for t in range(2):
                        for g in range(G):
                            if t == 0 and g == 0:
                                act.wait_ge(mixed_ready, i * 3 + (1 + 3))
                            gate("gates", i, t, g, hidv[:, TMP0 + t, g, :])

            ln_exp_tables()
            for g in range(G):
                pre(0, g, g)
            act.wait_ge(lb_diff, 1)
            nc.scalar.activation(oneml[:], oneml[:], ACT.Sigmoid).then_inc(lb_ready, 1)
            up("ffn1_up", 0)
            down("ffn1_down", 0)
            act.wait_ge(pads_set, 3)
            for g in range(G):
                v_copy(0, "G", g, True)
                og_sigmoid(0, "G", g)
                q_sigmoid(0, "G", g)
                f_sigmoid(0, "G", g)
            head_turn(1, False)
            with act.Fori(2, HEADS) as h:
                chain.enter(h, 2, 1)
                head_turn(h, True)
            chain.leave(HEADS - 2)
            head_turn(HEADS, True, True)
            ln_exp_tables()
            onorm(HEADS - 1)
            gates()
            act.wait_ge(state_stored, 32 * HEADS)
            down("out", 1)
            up("ffn2_up", 1)
            down("ffn2_down", 2)
            for n, (i, pos, m, g) in enumerate(y_tiles("ple")):
                ba, uses_a = plan.job("ple", i, pos - 1)
                b, uses = plan.job("ple", i, pos)
                if n >= 2:
                    _, pos2, m2, g2 = y_tiles("ple")[n - 2]
                    act.wait_ge(ysq_added, y_adds(3, m2, g2))
                act.wait_ge(bank_full[ba], uses_a + 1)
                nc.scalar.activation(gate_buf(n), bank[ba][:, 0:N], ACT.Sigmoid, scale=1.0 / WS)\
                    .then_inc(bank_read[ba], 1)
                act.wait_ge(bank_read[b], uses + 1)
                ins = square_y(3, m, g, hidv[:, Y0 + m, g, :])
                if m:
                    ins.then_inc(ysq_ready, 1)
                if m == KD - 1:
                    ln_exp_tables()
                    norm(21 + g)
            act.wait_ge(state_stored, 32 * HEADS)

        @block.vector
        def _(dve):
            chain = Tally(vec_chain)

            def step(ins):
                chain.inc(ins)
                dve.wait_ge(vec_chain, chain.value)

            V_ = nc.vector
            dve.wait_ge(cols_loaded, 16)
            for n in (1, 5):
                step(V_.tensor_scalar(col[:, n * KD:(n + 1) * KD], col[:, n * KD:(n + 1) * KD], 0.5, None, ALU.mult))
            V_.tensor_scalar(col[:, 8 * KD + 1:8 * KD + 5], col[:, 8 * KD + 1:8 * KD + 5], 1.0 / WS, None, ALU.mult)\
                .then_inc(cols_ready, 1)
            dve.wait_ge(cols_ready, 1)

            def pre(p, c, g, between=None):
                n = 3 * p + g
                for hf in range(2):
                    ks = slice(hf * HALF, (hf + 1) * HALF)
                    dve.wait_ge(squares_ready, 2 * n + hf + 1)
                    step(V_.tensor_reduce(half_sum[:] if hf else ssq(g), scratch[:, ks, :].rearrange("p k n -> p n k"),
                                          AX_X, ALU.add))
                V_.tensor_tensor(ssq(g), ssq(g), half_sum[:], ALU.add).then_inc(sums_ready, 1)
                if between:
                    between()
                dve.wait_ge(rinv_ready, c + 1)
                def part(n_):
                    for k in range(n_ * PART, (n_ + 1) * PART):
                        ins = V_.scalar_tensor_tensor(out=scratch[:, k, :], in0=xg(g, k), scalar=gain(2 * p, k),
                                                      in1=rinv[:, c % 2, :], op0=ALU.mult, op1=ALU.mult)
                    ins.then_inc(hfull_ready, 1)

                def low(n_):
                    ks = slice(n_ * PART, (n_ + 1) * PART)
                    dve.wait_ge(hhi_ready, PARTS * n + n_ + 1)
                    V_.tensor_tensor(hy[:, g, ks, N:2 * N], scratch[:, ks, :], hy[:, g, ks, 0:N], ALU.subtract)\
                        .then_inc(h_ready, 1)

                part(0)
                for n_ in range(1, PARTS):
                    part(n_)
                    low(n_ - 1)
                low(PARTS - 1)

            def add_square(q, m, g):
                if m:
                    n = y_adds(q, m, g) - 1
                    dve.wait_ge(ysq_ready, n + 1)
                    if n:
                        dve.wait_ge(ysq_added, n)
                    V_.tensor_tensor(ssq(g), ssq(g), sbuf2[:, n % 2, :], ALU.add).then_inc(ysq_added, 1)

            def post(q, c, g, y):
                dve.wait_ge(rinv_ready, c + 1)
                for hf in range(2):
                    ks = slice(hf * HALF, (hf + 1) * HALF)
                    step(V_.tensor_tensor(y[:, ks, :], y[:, ks, :],
                                          rinv[:, c % 2, :].unsqueeze(1).to_broadcast([P, HALF, N]), ALU.mult))
                    for k in range(hf * HALF, (hf + 1) * HALF):
                        ins = V_.scalar_tensor_tensor(out=xg(g, k), in0=y[:, k, :], scalar=gain(2 * q + 1, k),
                                                      in1=xg(g, k), op0=ALU.mult, op1=ALU.add)
                    ins.then_inc(x_updated, 1)

            def seams(name, q):
                tiles = y_tiles(name)
                last = [[t for t in tiles if t[0] == STAGES[name]["turns"] - 1 and t[3] == g]
                        for g in range(G)] + [[]]
                early = EARLY[name]

                def add(ts):
                    for _, _, m, g in ts:
                        add_square(q, m, g)

                add([t for t in tiles if t[0] < STAGES[name]["turns"] - 1])
                add(last[0][:early])
                for g in range(G):
                    add(last[g][early:])
                    c = 3 + 6 * q + 2 * g
                    post(q, c, g, yv[:, g, :, :])
                    dve.wait_ge(x_updated, 2 * (3 * q + g + 1))
                    pre(q + 1, c + 1, g, lambda: add(last[g + 1][:early]))
                    if q == 2 and g == 0:
                        split_p()

            def up(name, f):
                per = 12
                def body(i, kind):
                    jobs = jobs_of(name, kind)
                    n = 0
                    for pos, (t, g) in enumerate(jobs):
                        if not t % 2:
                            continue
                        ba, uses_a = plan.job(name, i, pos - 1)
                        b, uses = plan.job(name, i, pos)
                        s = sbuf2[:, n % 2, :]
                        m = i * 2 + t // 2
                        dst = hid[:, m, g, :] if isinstance(m, int) else hid[:, bass.ds(m, 1), g, :].rearrange(
                            "p a n -> p (a n)")
                        dve.wait_ge(bank_read[ba], uses_a + 1)
                        dve.wait_ge(bank_full[b], uses + 1)
                        V_.scalar_tensor_tensor(out=s, in0=bank[b][:, 0:N], scalar=1.0 / WS, in1=s,
                                                op0=ALU.mult, op1=ALU.mult).then_inc(bank_read[b], 1)
                        dve.wait_ge(bank_read[b], uses + 1)
                        step(V_.tensor_scalar(dst[:, 0:N], s, 1.0, None, ALU.mult))
                        V_.tensor_tensor(dst[:, N:2 * N], s, dst[:, 0:N], ALU.subtract).then_inc(hidden_ready, 1)
                        n += 1
                for a, b, kind in turn_runs(name):
                    if b - a >= 3:
                        with dve.Fori(a, b) as i:
                            chain.enter(i, a, 6)
                            body(i, kind)
                        chain.leave(b - a)
                    else:
                        for i in range(a, b):
                            body(i, kind)

            def gcols(a, g):
                return a[:, g * N:(g + 1) * N]

            def head_bank(h, kind, t, g):
                pos = jobs_of("heads", kind).index((t, g))
                return plan.job("heads", h, pos)

            def slot(h, g):
                return hidv[:, h, g, :] if isinstance(h, int) else hidv[:, bass.ds(h, 1), g, :].rearrange(
                    "p a n -> p (a n)")

            def silu_og(h, kind, g, n):
                b, _ = head_bank(h, kind, 1, g)
                dve.wait_ge(sigmoid_ready, h * 6 + n)
                V_.scalar_tensor_tensor(out=slot(h, g), in0=bank[b][:, 0:N], scalar=1.0 / WS, in1=slot(h, g),
                                        op0=ALU.mult, op1=ALU.mult).then_inc(bank_read[b], 1)

            def silu_q(h, kind, g, n):
                b, _ = head_bank(h, kind, 2, g)
                dve.wait_ge(sigmoid_ready, h * 6 + n)
                V_.scalar_tensor_tensor(out=gcols(Q, g), in0=bank[b][:, 0:N], scalar=1.0 / WS, in1=gcols(Q, g),
                                        op0=ALU.mult, op1=ALU.mult).then_inc(bank_read[b], 1)

            def evac(head, kind, r, f):
                b, uses = plan.piece(head, HG_FIRST[kind] + r)
                dve.wait_ge(bank_full[b], uses + 1)
                if kind in ("L32", "L16", "D16"):
                    if kind != "L32":
                        b1, uses1 = plan.piece(head, HG_FIRST[kind] + r - 2)
                        dve.wait_ge(bank_read[b1], uses1 + 1)
                    n = 2 + 2 * ("L32", "L16", "D16").index(kind) + r
                    V_.tensor_copy(mark[:, n:n + 1], mark[:, 0:1])
                f(bank[b]).then_inc(bank_read[b], 1)
                return b, uses

            def evac_tok(head, kind, dst):
                def copy(b, j0, j1):
                    if j1 == 9:
                        V_.tensor_copy(dst[:, j0 * P:8 * P], b[:, 0:(8 - j0) * P])
                        return V_.tensor_copy(dst[0:C, 8 * P:9 * P], b[0:C, (8 - j0) * P:(9 - j0) * P])
                    return V_.tensor_copy(dst[:, j0 * P:j1 * P], b[:, 0:(j1 - j0) * P])
                for r, (j0, j1) in enumerate(TOK_TILES):
                    evac(head, kind, r, lambda b: copy(b, j0, j1))

            def evac_scores(head, kind, m):
                evac(head, kind, 0, lambda b: V_.copy_predicated(att[:, 0:512], msk[:, m, :], b[:, 0:512]))
                evac(head, kind, 1, lambda b: V_.copy_predicated(att[0:C, 512:512 + C], msk[0:C, m, 0:C],
                                                                 b[0:C, 0:C]))

            def chunks(a, w):
                return a.rearrange("p (b w) -> p b w", w=w)

            def halves(a, w, right):
                v = a.rearrange("p (b s w) -> p b s w", s=2, w=w // 2)
                return v[:, :, 1 if right else 0, :]

            def minus_ref(out, w, at):
                v = chunks(GG, w)
                ref = v[:, :, at:at + 1].to_broadcast([P, TP // w, w])
                V_.tensor_tensor(chunks(out, w), v, ref, ALU.subtract).then_inc(diff_ready, 1)

            def decay_keys(head):
                if isinstance(head, int) and head == 0:
                    kind = "G"
                else:
                    kind = "M"
                for t in (0, 3):
                    for g in range(G):
                        b, uses = head_bank(head, kind, t, g)
                        dve.wait_ge(bank_read[b], uses + 1)
                sc = oneml[:, head:head + 1] if isinstance(head, int) else oneml[:, bass.ds(head, 1)]
                V_.tensor_scalar(K_[:, 0:T], K_[:, 0:T], sc, None, ALU.mult).then_inc(k_ready, 1)

            def onorm(head):
                dve.wait_ge(orstd_ready, head + 1)
                step(V_.scalar_tensor_tensor(out=W[3], in0=W[3], scalar=anorm, in1=W[1],
                                             op0=ALU.mult, op1=ALU.mult))
                s32 = hidv[:, head, :, :] if isinstance(head, int) else hidv[:, bass.ds(head, 1), :, :].rearrange(
                    "p a g n -> p (a g) n")
                s16 = hid[:, head, :, :] if isinstance(head, int) else hid[:, bass.ds(head, 1), :, :].rearrange(
                    "p a g n -> p (a g) n")
                o = W[3][:, 0:T].rearrange("p (g n) -> p g n", g=G)
                step(V_.tensor_tensor(o, o, s32, ALU.mult))
                step(V_.tensor_scalar(s16[:, :, 0:N], o, 1.0, None, ALU.mult))
                V_.tensor_tensor(s16[:, :, N:2 * N], o, s16[:, :, 0:N], ALU.subtract).then_inc(head_ready, 1)

            def operand(out, in0, head, n):
                dve.wait_ge(exp_ready, head * 9 + n)
                V_.tensor_tensor(out, out, in0, ALU.mult).then_inc(operand_ready, 1)

            def head_turn(h, with_norm, u_turn=False):
                hh = h - 1
                evac_tok(hh, "vT", vtok)
                if with_norm:
                    onorm(h - 2)
                dve.wait_ge(logf_ready, hh + 1)
                V_.tensor_tensor_scan(W[2], smask, GG, 0.0, ALU.mult, ALU.add).then_inc(vec_chain, 1)
                chain.n += 1
                dve.wait_ge(vec_chain, chain.value)
                V_.tensor_copy(GG, W[2]).then_inc(cum_ready, 1)
                dve.wait_ge(cum_ready, hh + 1)
                v = chunks(GG, C)
                V_.tensor_tensor(chunks(W[3], C), v[:, :, C - 1:C].to_broadcast([P, NC, C]), v, ALU.subtract)\
                    .then_inc(diff_ready, 1)
                minus_ref(W[0], 64, 31)
                minus_ref(W[1], 32, 15)
                minus_ref(W[2], 16, 7)
                operand(W[3], K_, hh, 1)
                operand(halves(W[0], 64, False), halves(K_, 64, False), hh, 2)
                operand(halves(W[0], 64, True), halves(Q, 64, True), hh, 3)
                operand(halves(W[1], 32, False), halves(K_, 32, False), hh, 4)
                operand(halves(W[1], 32, True), halves(Q, 32, True), hh, 5)
                operand(W[4], K_, hh, 6)
                operand(W[2], Q, hh, 7)
                operand(W[5], Q, hh, 8)
                evac_tok(hh, "kT", ktok)
                evac_scores(hh, "L32", 0)
                evac_scores(hh, "L16", 1)
                if not u_turn:
                    for g in range(G):
                        silu_og(h, "M", g, g + 1)
                evac_scores(hh, "D16", 2)
                dve.wait_ge(exp_ready, hh * 9 + 9)
                dve.wait_ge(state_loaded, hh * 16 + 16)
                if not (isinstance(hh, int) and hh == 0):
                    dve.wait_ge(state_stored, hh * 32)
                for rs in ((0, 1), (2, 3), (4,)):
                    for r in rs:
                        b, uses = plan.piece(hh, HG_FIRST["P"] + r)
                        dve.wait_ge(bank_full[b], uses + 1)
                    for c in sorted(c for r in rs for c in P_CHUNKS[r]):
                        r = next(r for r in rs if c in P_CHUNKS[r])
                        b, uses = plan.piece(hh, HG_FIRST["P"] + r)
                        n = P_CHUNKS[r].index(c)
                        src = bank[b][:, n * P:(n + 1) * P]
                        if c == 0:
                            ins = V_.tensor_copy(Sn(0), src)
                        elif c < PT:
                            ins = V_.scalar_tensor_tensor(out=Sn(c), in0=Sn(c - 1), scalar=eg[:, c:c + 1], in1=src,
                                                          op0=ALU.mult, op1=ALU.add)
                        else:
                            ins = V_.scalar_tensor_tensor(out=Sn(S_OUT), in0=Sn(S_IN), scalar=eg[:, c:c + 1],
                                                          in1=src, op0=ALU.mult, op1=ALU.add)
                        if c == P_CHUNKS[r][-1]:
                            ins.then_inc(bank_read[b], 1)
                            if c < NC - 1:
                                dve.wait_ge(bank_read[b], uses + 1)
                        else:
                            step(ins)
                dve.wait_ge(bank_read[b], uses + 1)
                V_.tensor_copy(mark[:, 1:2], mark[:, 0:1]).then_inc(chain_ready, 1)
                if u_turn:
                    pooling(0)
                    pooling(1)
                else:
                    for g in range(G):
                        silu_q(h, "M", g, g + 4)
                for r, cs in enumerate(O_CHUNKS):
                    dst = chunks(W[3], C)[:, cs[0]:cs[-1] + 1:cs.step, :]
                    b, uses = evac(hh, "O", r, lambda b: V_.tensor_copy(
                        dst, b[:, 0:len(cs) * C].rearrange("p (c t) -> p c t", t=C)))
                dve.wait_ge(bank_read[b], uses + 1)
                V_.tensor_copy(mark[:, 1:2], mark[:, 0:1]).then_inc(o_ready, 1)
                for r in range(3):
                    w = min(512, TP - r * 512)
                    b, uses = evac(hh, "SS", r, lambda b: V_.tensor_copy(W[1][:, r * 512:r * 512 + w], b[:, 0:w]))
                dve.wait_ge(bank_read[b], uses + 1)
                V_.tensor_copy(mark[:, 1:2], mark[:, 0:1]).then_inc(ss_ready, 1)
                if u_turn:
                    pooling(2)
                else:
                    decay_keys(h)

            HEAD_STEPS = 3 + 1 + 12

            def pooling(j):
                w = POOL_WINDOWS[j]
                for g in range(G):
                    b, uses = head_bank(HEADS, "M", j, g)
                    dve.wait_ge(bank_read[b], uses + 1)
                dve.wait_ge(pool_loaded[j], 16)
                step(V_.memset(U[j][:, 0:POOL_BUF], 0.0))
                src, n, bufs = U[j], 1, [W[0], GG]
                end = US + DEC_SEQ
                k = 0
                while n < w:
                    dst = bufs[k % 2]
                    step(V_.tensor_tensor(dst[:, 2 * n - 1:end], src[:, 2 * n - 1:end],
                                          src[:, n - 1:end - n], ALU.add))
                    src, n, k = dst, 2 * n, k + 1
                t = bufs[k % 2]
                step(V_.tensor_tensor(t[:, 0:POOL_BUF], src[:, UP:UP + POOL_BUF], invc[:, j, 0:POOL_BUF], ALU.mult))
                step(V_.tensor_tensor(t[:, 0:POOL_BUF], t[:, 0:POOL_BUF], U[j][:, UP:UP + POOL_BUF], ALU.subtract))
                step(V_.scalar_tensor_tensor(out=t[:, POOL_BUF:SEQ], in0=src[:, UP + POOL_BUF:UP + SEQ],
                                             scalar=1.0 / w, in1=U[j][:, UP + POOL_BUF:UP + SEQ],
                                             op0=ALU.mult, op1=ALU.subtract))
                step(V_.scalar_tensor_tensor(out=t[:, SEQ:T], in0=src[:, US:US + DEC_SEQ], scalar=1.0 / w,
                                             in1=U[j][:, US:US + DEC_SEQ], op0=ALU.mult, op1=ALU.subtract))
                dve.wait_ge(pool_stored[j], 32)
                tg = t[:, 0:T].rearrange("p (g n) -> p g n", g=G)
                step(V_.tensor_copy(pooled[j][:, :, 0:N], tg))
                V_.tensor_tensor(pooled[j][:, :, N:2 * N], tg, pooled[j][:, :, 0:N], ALU.subtract)\
                    .then_inc(pooled_ready, 1)

            def mixed():
                for n, (t, g) in enumerate((t, g) for t in range(4) for g in range(G)):
                    b, _ = plan.job("gates0", 0, 6 + n)
                    dst = hid[:, MIX0 + t, g, :]
                    dve.wait_ge(mixed_hi_ready, n + 1)
                    V_.scalar_tensor_tensor(out=dst[:, N:2 * N], in0=bank[b][:, 0:N], scalar=pscale(t),
                                            in1=dst[:, 0:N], op0=ALU.mult, op1=ALU.subtract).then_inc(bank_read[b], 1)
                dve.wait_ge(bank_read[b], plan.job("gates0", 0, 6 + n)[1] + 1)
                V_.tensor_copy(mark[:, 1:2], mark[:, 0:1]).then_inc(mixed_ready, 1)

            def gated(name, i, t, g, pos, s):
                bs, uses_s = plan.job(name, i, 3 * (t - 2) + g)
                b, uses = plan.job(name, i, pos)
                dve.wait_ge(bank_read[bs], uses_s + 1)
                dve.wait_ge(bank_full[b], uses + 1)
                V_.scalar_tensor_tensor(out=s, in0=bank[b][:, 0:N], scalar=1.0 / WS, in1=s,
                                        op0=ALU.mult, op1=ALU.mult).then_inc(bank_read[b], 1)
                return lambda: dve.wait_ge(bank_read[b], uses + 1)

            def join(a, s, dst):
                step(V_.tensor_tensor(a, a, s, ALU.add))
                step(V_.tensor_scalar(dst[:, 0:N], a, 1.0, None, ALU.mult))
                V_.tensor_tensor(dst[:, N:2 * N], a, dst[:, 0:N], ALU.subtract).then_inc(mixed_ready, 1)

            def gates():
                ta, tb = TMP_FIRST
                mixed()
                for g in range(G):
                    gated("gates0", 0, 2, g, 18 + g, gcols(ta, g))
                for g in range(G):
                    gated("gates0", 0, 3, g, 21 + g, gcols(tb, g))()
                    join(gcols(ta, g), gcols(tb, g), hid[:, M0, g, :])
                with dve.Fori(0, KD - 1) as i:
                    chain.enter(i, 0, 6)
                    for t in (2, 3):
                        for g in range(G):
                            s = hidv[:, TMP0 + t - 2, g, :]
                            there = gated("gates", i, t, g, 3 * t + g, s)
                            if t == 3:
                                there()
                                join(hidv[:, TMP0, g, :], s, hid[:, bass.ds(i + (M0 + 1), 1), g, :].rearrange(
                                    "p a n -> p (a n)"))
                chain.leave(KD - 1)

            def split_p():
                dve.wait_ge(p_loaded, 16)
                step(V_.tensor_copy(p_split[:, :, 0:N], p_raw))
                V_.tensor_tensor(p_split[:, :, N:2 * N], p_raw, p_split[:, :, 0:N], ALU.subtract)\
                    .then_inc(p_ready, 1)

            for g in range(G):
                for hf in range(2):
                    dve.wait_ge(x_loaded[2 * g + hf], 16)
                pre(0, g, g)
            dve.wait_ge(rest_loaded, 16 * 3)
            V_.tensor_tensor(oneml[:], lbl[:, 1, :], lbl[:, 0, :], ALU.subtract).then_inc(lb_diff, 1)
            step(V_.memset(mark[:], 0.0))
            step(V_.tensor_copy(msk[:].rearrange("p m (r c) -> p m r c", c=C), hidf[:, 0:3 * C].rearrange(
                "p (m c) -> p m c", m=3).unsqueeze(2).to_broadcast([P, 3, 512 // C, C])))
            up("ffn1_up", 0)
            seams("ffn1_down", 0)
            V_.memset(V[:, T:TP], 0.0).then_inc(pads_set, 1)
            V_.memset(Q[:, T:TP], 0.0)
            V_.memset(K_[:, T:TP], 0.0).then_inc(pads_set, 1)
            V_.memset(att, 0.0).then_inc(pads_set, 1)
            step(V_.memset(smask, 1.0))
            step(V_.memset(smask.rearrange("p (c t) -> p c t", t=C)[:, :, 0], 0.0))
            for g in range(G):
                silu_og(0, "G", g, 2 * g + 1)
                silu_q(0, "G", g, 2 * g + 2)
            dve.wait_ge(lb_ready, 1)
            decay_keys(0)
            head_turn(1, False)
            with dve.Fori(2, HEADS) as h:
                chain.enter(h, 2, HEAD_STEPS + 0)
                head_turn(h, True)
            chain.leave(HEADS - 2)
            head_turn(HEADS, True, True)
            onorm(HEADS - 1)
            pooling(3)
            gates()
            seams("out", 1)
            up("ffn2_up", 1)
            seams("ffn2_down", 2)
            for n, (i, pos, m, g) in enumerate(y_tiles("ple")):
                ba, uses_a = plan.job("ple", i, pos - 1)
                b, uses = plan.job("ple", i, pos)
                dve.wait_ge(bank_read[ba], uses_a + 1)
                dve.wait_ge(bank_full[b], uses + 1)
                V_.scalar_tensor_tensor(out=hidv[:, Y0 + m, g, :], in0=bank[b][:, 0:N],
                                        scalar=1.0 / WS, in1=gate_buf(n),
                                        op0=ALU.mult, op1=ALU.mult).then_inc(bank_read[b], 1)
                add_square(3, m, g)
                if m == KD - 1:
                    post(3, 21 + g, g, hidv[:, Y0:Y0 + KD, g, :])


def kernel(x_prompt, x_sample, p_prompt, p_sample, state_hgrn, state_pool, norm_gains, lb_logits,
           w_ffn1_gu, w_ffn1_down, w_in, a_gnorm, w_a_up, w_pool, pool_scale, w_b_up, w_out,
           w_ffn2_gu, w_ffn2_down, w_ple_proj, w_ple_gate):
    import numpy as np
    import concourse.bacc as bacc
    from concourse.bass_utils import run_bass_kernel_spmd

    f32 = np.float32

    def tiles(w):
        w = np.asarray(w)
        r, c = w.shape
        return w.reshape(r // P, P, c // P, P).transpose(0, 2, 1, 3)

    stream = []

    def column(w, m):
        stream.append(w[:, m])

    def ffn(gu, dn):
        gu, dn = tiles(gu), tiles(dn)
        for j in range(KF):
            column(gu, j)
            column(gu, KF + j)
        for m in range(KD):
            column(dn, m)

    ffn(w_ffn1_gu[0], w_ffn1_down[0])
    win = tiles(w_in[0])
    q0, f0, i0, og0, up0 = 0, 8, 16, 24, 32
    ga0, gb0 = 36, 44
    for h in range(HEADS):
        for base in (i0, og0, q0, f0):
            column(win, base + h)
    for j in range(4):
        column(win, up0 + j)
    wa, wb = tiles(w_a_up[0]), tiles(w_b_up[0])
    for m in range(KD):
        column(win, ga0 + m)
        column(win, gb0 + m)
        if m == 0:
            for j in range(4):
                stream.append(np.asarray(w_pool)[0, j][None])
        column(wa, m)
        column(wb, m)
    wo = tiles(w_out[0])
    for m in range(KD):
        column(wo, m)
    ffn(w_ffn2_gu[0], w_ffn2_down[0])
    wg, wp = tiles(w_ple_gate[0]), tiles(w_ple_proj[0])
    for m in range(KD):
        column(wg, m)
        column(wp, m)
    st = np.concatenate(stream, axis=0)
    units = st.shape[0] // UT
    st = np.ascontiguousarray(st.reshape(units, UT, P, P).transpose(0, 2, 1, 3).reshape(units, P, UT * P))

    def feature_major(a, b):
        t = np.concatenate([np.asarray(a), np.asarray(b)], axis=0).T
        return np.ascontiguousarray(t.reshape(t.shape[0] // P, P, T).transpose(1, 0, 2))

    def by_partition(v):
        return np.asarray(v).reshape(-1, P).T

    cols = np.concatenate([by_partition(norm_gains[0]), by_partition(a_gnorm[0]), by_partition(pool_scale[0]),
                           np.full((P, 1), EPS, f32), np.ones((P, 1), f32)], axis=1)
    s, t = np.arange(P)[:, None] % C, np.arange(C)[None, :]
    masks = np.stack([(s < 32) & (t >= 32),
                      (s // 32 == t // 32) & (s % 32 < 16) & (t % 32 >= 16),
                      (s // 16 == t // 16) & (s <= t)], axis=1).astype(f32).reshape(P, 3 * C)
    count = np.array([[1.0 / min(w, n + 1) for n in range(16)] for w in POOL_WINDOWS], f32)
    arrays = {
        "xT": feature_major(x_prompt[0], x_sample[0]),
        "pT": feature_major(p_prompt[0, 0], p_sample[0, 0]).reshape(P, KP * G, N),
        "weights": st,
        "cols": np.ascontiguousarray(cols),
        "lbT": np.ascontiguousarray(np.asarray(lb_logits).reshape(2, HEADS, P).transpose(2, 0, 1)),
        "consts": np.concatenate([np.eye(P, dtype=f32), np.ones((P, P), f32)], axis=1),
        "masks": masks,
        "inv_count": np.ascontiguousarray(np.broadcast_to(count, (P, 4, 16))),
        "state_in": np.ascontiguousarray(state_hgrn[0, 0]),
        "pool_in": np.ascontiguousarray(np.asarray(state_pool)[0, 0].T.reshape(4, P, POOL_BUF).transpose(1, 0, 2)),
    }
    outs = {"out_x": (P, KD, T), "out_states": (2, HEADS, DK, DK), "out_pools": (2, 4, P, POOL_BUF)}

    nc = bacc.Bacc("TRN2", target_bir_lowering=False, num_devices=1)
    args = {n: nc.dram_tensor(n, a.shape, mybir.dt.from_np(a.dtype), kind="ExternalInput").ap()
            for n, a in arrays.items()}
    args.update({n: nc.dram_tensor(n, sh, F32, kind="ExternalOutput").ap() for n, sh in outs.items()})
    build(nc, **args)
    r = run_bass_kernel_spmd(nc, [arrays], core_ids=[0]).results[0]

    y = np.asarray(r["out_x"]).transpose(1, 0, 2).reshape(D_MODEL, T).T
    states, pools = np.asarray(r["out_states"]), np.asarray(r["out_pools"])
    pools = pools.reshape(2, 4 * P, POOL_BUF).transpose(0, 2, 1)
    return (np.ascontiguousarray(y[None, :SEQ]), np.ascontiguousarray(y[None, SEQ:]),
            states[None, 0:1], np.ascontiguousarray(pools[None, 0:1]),
            states[None, 1:2], np.ascontiguousarray(pools[None, 1:2]))
```

```python
from contextlib import ExitStack

import concourse.bass as bass
from concourse import mybir

ALU = mybir.AluOpType
ACT = mybir.ActivationFunctionType
F32 = mybir.dt.float32
F16 = mybir.dt.float16
BF16 = mybir.dt.bfloat16
U8 = mybir.dt.uint8
AX_X = mybir.AxisListType.X

P = 128
D_MODEL, SEQ, DEC_SEQ, D_FF = 1024, 1024, 32, 2816
HEADS, DK = 8, 128
POOL_WINDOWS, POOL_BUF = (2, 4, 8, 16), 15
PLE_DIM = 256
EPS = 1e-6
KD = D_MODEL // P
KF = D_FF // P
KP = PLE_DIM // P
T = SEQ + DEC_SEQ
G = 3
N = T // G
C = 64
NC = (T + C - 1) // C
TP = NC * C
PT = SEQ // C
WS = 32.0
UT = 4
HALF = KD // 2
PARTS, PART = 4, KD // 4

STAGES = {
    "ffn1_up": dict(units=8, turns=11, ks=[KD] * 4, kinds="G" + "P" * 10, banks=6),
    "ffn1_down": dict(units=11, turns=4, ks=[KF] * 2, kinds="MMMG", banks=6),
    "head0": dict(units=8, turns=1, ks=[KD] * 4, kinds="G", banks=6),
    "heads": dict(units=8, turns=HEADS, ks=[KD] * 4, kinds="M" * HEADS, banks=4),
    "gates0": dict(units=8, turns=1, ks=[KD, KD, 1, 1, 1, 1, KD, 4], kinds="M", banks=6),
    "gates": dict(units=7, turns=7, ks=[KD, KD, KD, 4], kinds="M" * 7, banks=6),
    "out0": dict(units=6, turns=1, ks=[KD] * 3, kinds="M", banks=3),
    "out1": dict(units=10, turns=1, ks=[KD] * 5, kinds="G", banks=5),
    "ffn2_up": dict(units=8, turns=11, ks=[KD] * 4, kinds="G" + "P" * 10, banks=6),
    "ffn2_down": dict(units=11, turns=4, ks=[KF] * 2, kinds="MMMG", banks=6),
    "ple": dict(units=10, turns=2, ks=[KD, KP] * 4, kinds="GG", banks=6),
}
ORDER = list(STAGES)
RING = max(s["units"] for s in STAGES.values())

HG_PIECES = (["vT"] * 3 + ["kT"] * 3 + ["L32"] * 2 + ["L16"] * 2 + ["D16"] * 2
             + ["P"] * 5 + ["O"] * 4 + ["SS"] * 3)
HG_FIRST = {k: HG_PIECES.index(k) for k in dict.fromkeys(HG_PIECES)}
TOK_TILES = [(0, 4), (4, 7), (7, 9)]
P_CHUNKS = [range(0, 8, 2), range(1, 8, 2), range(8, 16, 2), range(9, 16, 2), range(16, 17)]
O_PAIRS = [(0, 3), (3, 6), (6, 8), (8, 9)]
CALLS = [("pre", 0, g) for g in range(G)]
CALLS += [c for q in range(3) for g in range(G) for c in (("post", q, g), ("pre", q + 1, g))]
CALLS += [("post", 3, g) for g in range(G)]
Y_STAGES = [["ffn1_down"], ["out0", "out1"], ["ffn2_down"], ["ple"]]


def y_tiles(q):
    tiles, m0 = [], 0
    for name in Y_STAGES[q]:
        s = STAGES[name]
        step = 2 if name == "ple" else 1
        per = len(s["ks"]) // step
        for i, kind in enumerate(s["kinds"]):
            tiles += [(name, i, pos, m0 + t // step, g)
                      for pos, (t, g) in enumerate(jobs_of(name, kind)) if t % step == step - 1]
            m0 += per
    return tiles


def seam_tiles(q):
    tiles = y_tiles(q)
    name, turn = tiles[-1][:2]
    last = [[t for t in tiles if t[:2] == (name, turn) and t[4] == g] for g in range(G)]
    return [t for t in tiles if t[:2] != (name, turn)], last + [[]]


NEXT = 2
EARLY = [1, 2, 1]


def y_adds(q, m, g):
    tiles = [(m2, g2) for _, _, _, m2, g2 in y_tiles(q)]
    before = tiles[:tiles.index((m, g)) + 1]
    return q * (KD - 1) * G + sum(m2 > 0 for m2, _ in before)


def jobs_of(name, kind):
    a = len(STAGES[name]["ks"])
    if kind == "M":
        return [(t, g) for t in range(a) for g in range(G)]
    if kind == "G":
        return [(t, g) for g in range(G) for t in range(a)]
    return [(2 * q + r, g) for q in range(a // 2) for g in range(G) for r in range(2)]


class Plan:

    def __init__(self):
        uses = [0] * 8
        unit = 0
        loads = [0] * RING
        first = 0
        self.base, self.unit0, self.load0, self.first, self.used0 = {}, {}, {}, {}, {}
        used = 0
        self.hg_base = None
        self.norm = []
        norm_uses = iter(range(len(CALLS)))

        def norms(k):
            for _ in range(k):
                c = next(norm_uses)
                b = 6 + c % 2
                self.norm.append((b, uses[b]))
                uses[b] += 1

        before = {"ffn1_up": 3, "head0": 6, "ffn2_up": 6, "ple": 6}
        for name in ORDER:
            s = STAGES[name]
            norms(before.get(name, 0))
            self.base[name] = list(uses)
            self.unit0[name] = unit
            self.load0[name] = list(loads)
            per = len(s["ks"]) * G // s["banks"]
            for b in range(s["banks"]):
                uses[b] += per * s["turns"]
            unit += s["units"] * s["turns"]
            self.first[name] = first
            self.used0[name] = used
            used += len(mid_units(name)) * s["turns"]
            for u in range(s["units"]):
                loads[self.slot(name, u)] += s["turns"]
            first = (first + s["units"]) % RING
            if name == "heads":
                self.hg_base = list(uses)
                for b in range(4, 8):
                    uses[b] += HEADS * len(HG_PIECES) // 4
        norms(3)
        self.units = unit

    def head_job(self, h, t, g):
        if isinstance(h, int) and h == 0:
            return self.job("head0", 0, jobs_of("head0", "G").index((t, g)))
        return self.job("heads", h - 1, jobs_of("heads", "M").index((t, g)))

    def slot(self, name, u):
        return (self.first[name] + u) % RING

    def job(self, name, i, pos):
        s = STAGES[name]
        r = s["banks"]
        per = len(s["ks"]) * G // r
        return pos % r, i * per + (self.base[name][pos % r] + pos // r)

    def piece(self, head, n):
        b = 4 + n % 4
        return b, head * (len(HG_PIECES) // 4) + (self.hg_base[b] + n // 4)

    def freed_by(self, name, i, u):
        s = STAGES[name]
        if u in mid_units(name):
            n = mid_units(name).index(u)
            return None, i * len(mid_units(name)) + (self.used0[name] + n + 1)
        kind = s["kinds"][i] if isinstance(i, int) else "M" if "M" in s["kinds"] else "P"
        last_tile, t = UT * u + UT - 1, 0
        while last_tile >= s["ks"][t]:
            last_tile -= s["ks"][t]
            t += 1
        b, uses = self.job(name, i, jobs_of(name, kind).index((t, G - 1)))
        return b, uses + 1


def mid_units(name):
    ends = {sum(STAGES[name]["ks"][:t + 1]) for t in range(len(STAGES[name]["ks"]))}
    return [u for u in range(STAGES[name]["units"]) if UT * (u + 1) not in ends]


class Tally:

    def __init__(self, sem):
        self.sem, self.base, self.n, self.loop = sem, 0, 0, None

    def inc(self, ins, k=1):
        ins.then_inc(self.sem, k)
        self.n += k

    @property
    def value(self):
        return self.base + self.n

    def enter(self, i, first, per):
        at = self.base + self.n
        self.loop = (at, per)
        self.base = i * per + (at - first * per) if per else at
        self.n = 0

    def leave(self, trips):
        at, per = self.loop
        assert self.n == per, (str(self.sem), self.n, per)
        self.base, self.n, self.loop = at + trips * per, 0, None


def turn_runs(name):
    s = STAGES[name]
    runs = []
    for i, k in enumerate(s["kinds"]):
        if runs and runs[-1][2] == k and i > 1:
            runs[-1][1] = i + 1
        else:
            runs.append([i, i + 1, k])
    return runs


def build(nc, xT, pT, weights, cols, lbT, consts, masks, inv_count, state_in, pool_in,
          out_x, out_states, out_pools):
    plan = Plan()
    with ExitStack() as ctx:
        def sb(name, shape, dt):
            return ctx.enter_context(nc.sbuf_tensor(name, shape, dt))

        def sem(name):
            return ctx.enter_context(nc.semaphore(name))

        x = sb("x", [P, KD, T], F32)
        hy = sb("hy", [P, G, KD, 2 * N], F16)
        hid = sb("hid", [P, KF, G, 2 * N], F16)
        ring = sb("ring", [P, RING, 2 * UT * P], F16)
        wtmp = sb("wtmp", [P, UT * P], F32)
        scratch = sb("scratch", [P, KD, N], F32)
        wconst = sb("wconst", [P, 2], F32)
        u1 = sb("u1", [P, TP], F32)
        sbuf2 = sb("sbuf2", [P, 2, N], F32)
        half_sum = sb("half_sum", [P, N], F32)
        rinv = sb("rinv", [P, 2, N], F32)
        cst = sb("cst", [P, 2 * P], F32)
        msk = sb("msk", [P, 3, 512], U8)
        invc = sb("invc", [P, 4, 16], F32)
        col = sb("col", [P, 8 * KD + 1 + 4 + 2], F32)
        lbl = sb("lbl", [P, 2, HEADS], F32)
        oneml = sb("oneml", [P, HEADS], F32)
        mark = sb("mark", [P, 8], F32)
        eg = sb("eg", [P, NC], F32)
        bank = [ctx.enter_context(nc.psum_tensor(f"bank{b}", [P, 512], F32)) for b in range(8)]

        ident, ones = cst[:, 0:P], cst[:, P:2 * P]
        gain = lambda n, k: col[:, n * KD + k:n * KD + k + 1]
        anorm = col[:, 8 * KD:8 * KD + 1]
        pscale = lambda j: col[:, 8 * KD + 1 + j:8 * KD + 2 + j]
        eps, one = col[:, 8 * KD + 5:8 * KD + 6], col[:, 8 * KD + 6:8 * KD + 7]

        def xg(g, k=None):
            return x[:, :, g * N:(g + 1) * N] if k is None else x[:, k, g * N:(g + 1) * N]

        def ssq(g):
            return u1[:, g * N:(g + 1) * N]

        def gate_buf(n):
            return hidv[:, PL0 + 6 * KP, n % 2, :]

        def hyp(g, k, w):
            return hy[:, g, k, w * N:(w + 1) * N]

        yv = hy[:, :, :, :].rearrange("p g k n -> p (g k n)").bitcast(F32).rearrange(
            "p (g k n) -> p g k n", g=G, k=KD)
        hidf = hid[:, :, :, :].rearrange("p s g n -> p (s g n)").bitcast(F32)
        hidv = hidf.rearrange("p (s g n) -> p s g n", s=KF, g=G)
        area = hidf[:, 8 * T:KF * T]

        def arr(n):
            return area[:, n * TP:(n + 1) * TP]

        V, Q, K_, GG = arr(0), arr(1), arr(2), arr(3)
        W = [arr(4 + n) for n in range(6)]
        vtok = area[:, 10 * TP:10 * TP + 9 * P]
        ktok = area[:, 10 * TP + 9 * P:10 * TP + 18 * P]
        att = area[:, 10 * TP + 18 * P:10 * TP + 18 * P + TP]
        smask = u1[:, 0:TP // 2].bitcast(BF16)
        S = scratch[:, :, :].rearrange("p k n -> p (k n)")[:, 0:18 * P]

        def Sn(n):
            return S[:, n * P:(n + 1) * P]

        S_IN, S_OUT = 16, 17
        U = [V, u1[:, :], Q, K_]
        UP, US = POOL_BUF, POOL_BUF + SEQ + POOL_BUF
        pooled = [u[:, 0:T].bitcast(F16).rearrange("p (g n) -> p g n", g=G) for u in U]
        TMP_FIRST = [W[2], W[4]]
        M0, TMP0, MIX0 = 8, 16, 18
        Y0, PL0 = 0, 8
        mask_raw = hidf[:, 21 * T:21 * T + 3 * C]
        p_raw = hidv[:, PL0 + 3 * KP:PL0 + 6 * KP, 0, :]
        p_split = hid[:, PL0:PL0 + 3 * KP, 0, :]

        slot_loaded = [sem(f"slot_loaded{u}") for u in range(RING)]
        unit_ready = sem("unit_ready")
        unit_used = sem("unit_used")
        bank_full = [sem(f"bank_full{b}") for b in range(8)]
        bank_read = [sem(f"bank_read{b}") for b in range(8)]
        ones_loaded = sem("ones_loaded")
        cols_loaded = sem("cols_loaded")
        rest_loaded = sem("rest_loaded")
        x_loaded = [sem(f"x_loaded{n}") for n in range(2 * G)]
        p_loaded = sem("p_loaded")
        p_ready = sem("p_ready")
        cols_ready = sem("cols_ready")
        lb_diff = sem("lb_diff")
        lb_ready = sem("lb_ready")
        squares_ready = sem("squares_ready")
        sums_ready = sem("sums_ready")
        rinv_ready = sem("rinv_ready")
        ysq_ready = sem("ysq_ready")
        ysq_added = sem("ysq_added")
        x_updated = sem("x_updated")
        hfull_ready = sem("hfull_ready")
        hhi_ready = sem("hhi_ready")
        h_ready = sem("h_ready")
        hidden_ready = sem("hidden_ready")
        sigmoid_ready = sem("sigmoid_ready")
        k_ready = sem("k_ready")
        logf_ready = sem("logf_ready")
        cum_ready = sem("cum_ready")
        diff_ready = sem("diff_ready")
        exp_ready = sem("exp_ready")
        operand_ready = sem("operand_ready")
        o_ready = sem("o_ready")
        osq_ready = sem("osq_ready")
        ss_ready = sem("ss_ready")
        orstd_ready = sem("orstd_ready")
        head_ready = sem("head_ready")
        chain_ready = sem("chain_ready")
        state_loaded = sem("state_loaded")
        state_stored = sem("state_stored")
        pads_set = sem("pads_set")
        wconst_set = sem("wconst_set")
        pool_loaded = [sem(f"pool_loaded{j}") for j in range(4)]
        u_ready = sem("u_ready")
        pool_stored = [sem(f"pool_stored{j}") for j in range(4)]
        pooled_ready = sem("pooled_ready")
        mixed_hi_ready = sem("mixed_hi_ready")
        mixed_ready = sem("mixed_ready")
        x_stored = sem("x_stored")
        vec_chain = sem("vec_chain")
        act_chain = sem("act_chain")
        pool_chain = sem("pool_chain")

        block = ctx.enter_context(nc.Block())

        def loops(eng, name, body, runs=None):
            for a, b, kind in runs or turn_runs(name):
                if b - a >= 3:
                    with eng.Fori(a, b) as i:
                        body(i, kind)
                else:
                    for i in range(a, b):
                        body(i, kind)

        def load_x(eng, g):
            for hf in range(2):
                ks = slice(hf * HALF, (hf + 1) * HALF)
                eng.dma_start(x[:, ks, g * N:(g + 1) * N], xT[:, ks, g * N:(g + 1) * N])\
                    .then_inc(x_loaded[2 * g + hf], 16)

        @block.sync
        def _(sp):
            load_x(sp, 0)
            last = {}

            def load(name, i, u, freed, unit0=False):
                if unit0 and u == 2:
                    sp.wait_ge(x_loaded[0], 16)
                if freed is not None:
                    sp.wait_ge(unit_used if freed[0] is None else bank_full[freed[0]], freed[1])
                n = i * STAGES[name]["units"] + (plan.unit0[name] + u)
                slot = plan.slot(name, u)
                src = weights[n, :, :] if isinstance(n, int) else weights[
                    bass.ds(n, 1), :, :].rearrange("a p c -> p (a c)")
                sp.dma_start(ring[:, slot, :].bitcast(F32), src).then_inc(slot_loaded[slot], 16)

            for name in ORDER:
                s = STAGES[name]
                runs = []
                for i in range(s["turns"]):
                    k = s["kinds"][i - 1] if i else None
                    if runs and runs[-1][2] == k:
                        runs[-1][1] = i + 1
                    else:
                        runs.append([i, i + 1, k])
                for a, b, k in runs:
                    if b - a >= 3:
                        with sp.Fori(a, b) as i:
                            for u in range(s["units"]):
                                load(name, i, u, plan.freed_by(name, i - 1, u))
                    else:
                        for i in range(a, b):
                            for u in range(s["units"]):
                                load(name, i, u, plan.freed_by(name, i - 1, u) if i else last.get(plan.slot(name, u)),
                                     name == ORDER[0] and i == 0)
                for u in range(s["units"]):
                    last[plan.slot(name, u)] = plan.freed_by(name, s["turns"] - 1, u)
            for g in range(G):
                for hf in range(2):
                    ks = slice(hf * HALF, (hf + 1) * HALF)
                    sp.wait_ge(x_updated, 2 * (9 + g) + hf + 1)
                    sp.dma_start(out_x[:, ks, g * N:(g + 1) * N], x[:, ks, g * N:(g + 1) * N]).then_inc(x_stored, 16)
            sp.wait_ge(x_stored, 16 * 2 * G)

        @block.gpsimd
        def _(pool):
            chain = Tally(pool_chain)
            done = Tally(unit_ready)
            ws_all = wconst[:, 0:1].to_broadcast([P, UT * P])
            one_all = wconst[:, 1:2].to_broadcast([P, UT * P])
            nc.gpsimd.memset(wconst[:, 0:1], WS).then_inc(wconst_set, 1)
            nc.gpsimd.memset(wconst[:, 1:2], 1.0).then_inc(wconst_set, 1)
            pool.wait_ge(wconst_set, 2)

            def split(name, i, u):
                slot = plan.slot(name, u)
                raw = ring[:, slot, :].bitcast(F32)
                hi, lo = ring[:, slot, 0:UT * P], ring[:, slot, UT * P:2 * UT * P]
                pool.wait_ge(slot_loaded[slot], i * 16 + 16 * (plan.load0[name][slot] + 1))
                if not (isinstance(i, int) and name == ORDER[0] and i == 0 and u == 0):
                    pool.wait_ge(unit_ready, done.value)
                chain.inc(nc.gpsimd.tensor_tensor(wtmp[:], raw, ws_all, ALU.mult))
                pool.wait_ge(pool_chain, chain.value)
                chain.inc(nc.gpsimd.tensor_tensor(hi, wtmp[:], one_all, ALU.mult))
                pool.wait_ge(pool_chain, chain.value)
                done.inc(nc.gpsimd.tensor_tensor(lo, wtmp[:], hi, ALU.subtract))

            for name in ORDER:
                s = STAGES[name]
                first = 1 if name == ORDER[0] else 0
                for i in range(first):
                    for u in range(s["units"]):
                        split(name, i, u)
                if s["turns"] - first >= 3:
                    with pool.Fori(first, s["turns"]) as i:
                        chain.enter(i, first, 2 * s["units"])
                        done.enter(i, first, s["units"])
                        for u in range(s["units"]):
                            split(name, i, u)
                    chain.leave(s["turns"] - first)
                    done.leave(s["turns"] - first)
                else:
                    for i in range(first, s["turns"]):
                        for u in range(s["units"]):
                            split(name, i, u)

        @block.tensor
        def _(pe):
            def take(b, uses):
                if not (isinstance(uses, int) and uses == 0):
                    pe.wait_ge(bank_read[b], uses)

            def turn(name, i, kind, rhs, ready=None, hooks=None):
                s = STAGES[name]
                starts = [sum(s["ks"][:t]) for t in range(len(s["ks"]))]
                seen = set()
                for pos, (t, g) in enumerate(jobs_of(name, kind)):
                    b, uses = plan.job(name, i, pos)
                    take(b, uses)
                    for k in range(s["ks"][t]):
                        if ready:
                            ready(i, t, g, pos, k)
                        u, q = divmod(starts[t] + k, UT)
                        if u not in seen:
                            seen.add(u)
                            pe.wait_ge(unit_ready, i * s["units"] + (plan.unit0[name] + u + 1))
                        slot = plan.slot(name, u)
                        whi = ring[:, slot, q * P:(q + 1) * P]
                        wlo = ring[:, slot, (UT + q) * P:(UT + q + 1) * P]
                        out = bank[b][:, 0:N]
                        end = k == s["ks"][t] - 1
                        nc.tensor.matmul(out, whi, rhs(t, k, g, 0), start=(k == 0), stop=False)
                        nc.tensor.matmul(out, whi, rhs(t, k, g, 1), start=False, stop=False)
                        mm = nc.tensor.matmul(out, wlo, rhs(t, k, g, 0), start=False, stop=end)
                        if end:
                            mm.then_inc(bank_full[b], 1)
                        elif g == G - 1 and q == UT - 1:
                            mm.then_inc(unit_used, 1)
                        if not end and hooks and (pos, k) in hooks:
                            for f in hooks[(pos, k)]:
                                f()
                    if hooks and (pos, None) in hooks:
                        for f in hooks[(pos, None)]:
                            f()

            def norm(c):
                b, uses = plan.norm[c]
                what, n, g = CALLS[c]
                if what == "pre":
                    pe.wait_ge(sums_ready, 3 * n + g + 1)
                else:
                    pe.wait_ge(ysq_added, y_adds(n, KD - 1, g))
                take(b, uses)
                nc.tensor.matmul(bank[b][:, 0:N], ones, ssq(g), start=True, stop=True).then_inc(bank_full[b], 1)

            def h_rhs(t, k, g, w):
                return hyp(g, k, w)

            def hid_rhs(base):
                return lambda t, k, g, w: hid[:, base + k, g, w * N:(w + 1) * N]

            def h_wait(p):
                def ready(i, t, g, pos, k):
                    if isinstance(i, int) and i == 0 and t == 0 and k % PART == 0:
                        pe.wait_ge(h_ready, PARTS * (3 * p + g) + k // PART + 1)
                return ready

            def up(name, p, hooks):
                for a, b, kind in turn_runs(name):
                    if a == 0:
                        turn(name, 0, kind, h_rhs, h_wait(p), hooks)
                    else:
                        with pe.Fori(a, b) as i:
                            turn(name, i, kind, h_rhs)

            def down(name, f, hooks):
                def ready(i, t, g, pos, k):
                    if i == 0 and t == 0 and (k >= KF - 2 or k + g == 0):
                        before = 3 * (k - KF + 2) + g + 1 if k else 0
                        pe.wait_ge(hidden_ready, 66 * f + 60 + before)
                turn(name, 0, "M", hid_rhs(0), ready)
                for i in (1, 2):
                    turn(name, i, "M", hid_rhs(0))
                turn(name, 3, "G", hid_rhs(0), None, hooks)

            def calls(*cs):
                return [lambda c=c: norm(c) for c in cs]

            def piece(head, n, fill):
                b, uses = plan.piece(head, n)
                take(b, uses)
                fill(b).then_inc(bank_full[b], 1)

            def head_transposes(head, kind, src):
                for r, (j0, j1) in enumerate(TOK_TILES):
                    def fill(b, j0=j0, j1=j1):
                        for j in range(j0, j1):
                            w = min(P, TP - j * P)
                            last = nc.tensor.transpose(bank[b][0:w, (j - j0) * P:(j - j0 + 1) * P],
                                                       src[:, j * P:j * P + w], ident)
                        return last
                    piece(head, HG_FIRST[kind] + r, fill)

            def head_scores(head, kind, kk, qq):
                for r, (c0, c1) in enumerate([(0, PT), (PT, NC)]):
                    def fill(b, c0=c0, c1=c1):
                        for c in range(c0, c1):
                            h0 = C * (c % 2)
                            last = nc.tensor.matmul(bank[b][h0:h0 + C, (c - c0) // 2 * C:((c - c0) // 2 + 1) * C],
                                                    kk[:, c * C:(c + 1) * C], qq[:, c * C:(c + 1) * C],
                                                    start=True, stop=True)
                        return last
                    piece(head, HG_FIRST[kind] + r, fill)

            def head_updates(head, rs):
                for r in rs:
                    def fill(b, r=r):
                        for n, c in enumerate(P_CHUNKS[r]):
                            h0 = C * (c % 2)
                            j = c // 2
                            last = nc.tensor.matmul(bank[b][:, n * P:(n + 1) * P],
                                                    ktok[h0:h0 + C, j * P:(j + 1) * P],
                                                    vtok[h0:h0 + C, j * P:(j + 1) * P], start=True, stop=True)
                        return last
                    piece(head, HG_FIRST["P"] + r, fill)

            def head_outputs(head):
                pe.wait_ge(chain_ready, head * 1 + 1)
                for r, (j0, j1) in enumerate(O_PAIRS):
                    def fill(b, j0=j0, j1=j1):
                        for j in range(j0, j1):
                            w = min(P, TP - j * P)
                            nc.tensor.matmul(bank[b][:, (j - j0) * P:(j - j0) * P + w], vtok[0:w, j * P:(j + 1) * P],
                                             att[0:w, j * P:j * P + w],
                                             start=(j == j0), stop=True, skip_group_check=True)
                        for c in range(max(2 * j0, 1), min(2 * j1, NC)):
                            n = c - 2 * j0
                            last = nc.tensor.matmul(bank[b][:, n * C:(n + 1) * C],
                                                    Sn(c - 1 if c < PT else S_IN), W[5][:, c * C:(c + 1) * C],
                                                    start=False, stop=True, skip_group_check=True)
                        return last
                    piece(head, HG_FIRST["O"] + r, fill)

            def head_sumsq(head):
                pe.wait_ge(osq_ready, head * 1 + 1)
                for r in range(3):
                    c0, c1 = r * 512, min(r * 512 + 512, TP)
                    def fill(b, c0=c0, c1=c1):
                        return nc.tensor.matmul(bank[b][:, 0:c1 - c0], ones, W[4][:, c0:c1], start=True, stop=True)
                    piece(head, HG_FIRST["SS"] + r, fill)

            def operands(head, n):
                pe.wait_ge(operand_ready, head * 8 + n)

            def head_hooks(h):
                hh = h - 1
                return {
                    (0, 3): [lambda: pe.wait_ge(k_ready, h), lambda: head_transposes(hh, "vT", V)],
                    (4, None): [lambda: operands(hh, 1), lambda: head_transposes(hh, "kT", W[3])],
                    (5, None): [lambda: operands(hh, 3), lambda: head_scores(hh, "L32", W[0], W[0])],
                    (6, None): [lambda: operands(hh, 5), lambda: head_scores(hh, "L16", W[1], W[1]),
                                lambda: operands(hh, 7), lambda: head_scores(hh, "D16", W[4], W[2])],
                    (7, None): [lambda: head_updates(hh, range(4))],
                    (8, 4): [lambda: head_updates(hh, [4])],
                    (9, None): [lambda: operands(hh, 8), lambda: head_outputs(hh)],
                    (11, None): [lambda: head_sumsq(hh)],
                }

            pe.wait_ge(ones_loaded, 16)
            norm(0)
            up("ffn1_up", 0, {(1, 2): calls(1), (4, 3): calls(2)})
            down("ffn1_down", 0, {(2, 5): calls(3), (3, 9): calls(4), (4, 8): calls(5), (5, 12): calls(6)})
            turn("head0", 0, "G", h_rhs, h_wait(1), {(1, 2): calls(7), (3, None): calls(8)})
            with pe.Fori(1, HEADS + 1) as h:
                turn("heads", h - 1, "M", h_rhs, None, head_hooks(h))

            def gate_rhs(t, k, g, w):
                if t < 2:
                    return hyp(g, k, w)
                return hid[:, (0 if t == 2 else MIX0) + k, g, w * N:(w + 1) * N]

            def first_gate_rhs(t, k, g, w):
                if 2 <= t < 6:
                    return pooled[t - 2][:, g, w * N:(w + 1) * N]
                return gate_rhs(t if t < 2 else t - 4, k, g, w)

            def first_gate_ready(i, t, g, pos, k):
                if 2 <= t < 6 and g == 0:
                    pe.wait_ge(pooled_ready, t - 1)
                if t == 6 and g == 0 and k in (0, KD - 1):
                    pe.wait_ge(head_ready, HEADS if k else HEADS - 1)
                if t == 7 and g == 0 and k == 0:
                    pe.wait_ge(mixed_ready, 1)

            turn("gates0", 0, "M", first_gate_rhs, first_gate_ready)
            with pe.Fori(0, KD - 1) as i:
                turn("gates", i, "M", gate_rhs)
            def m_ready(i, t, g, pos, k):
                if t == 0 and (k == KD - 1 or k + g == 0):
                    pe.wait_ge(mixed_ready, 1 + 21 + (g + 1 if k else 0))

            turn("out0", 0, "M", hid_rhs(M0), m_ready)
            turn("out1", 0, "G", hid_rhs(M0), None,
                 {(5, 5): calls(9), (8, None): calls(10), (11, 5): calls(11), (14, 6): calls(12)})
            up("ffn2_up", 2, {(2, 0): calls(13), (5, 2): calls(14)})
            down("ffn2_down", 1, {(2, 5): calls(15), (3, 9): calls(16), (4, 12): calls(17), (5, 14): calls(18)})

            def ple_rhs(t, k, g, w):
                return hyp(g, k, w) if t % 2 == 0 else p_split[:, G * k + g, w * N:(w + 1) * N]

            def ple_ready(i, t, g, pos, k):
                h_wait(3)(i, t, g, pos, k)
                if i == 0 and t == 1 and k == 0:
                    pe.wait_ge(p_ready, g + 1)

            turn("ple", 0, "G", ple_rhs, ple_ready, {(1, None): calls(19), (6, 2): calls(20)})
            turn("ple", 1, "G", ple_rhs, None, {(8, 5): calls(21), (16, 5): calls(22)})
            norm(23)

        @block.scalar
        def _(act):
            chain = Tally(act_chain)

            def ln_exp_tables():
                nc.scalar.preload_act_table_set("natural_log_exp_and_others")

            act.dma_start(col[:], cols).then_inc(cols_loaded, 16)
            act.dma_start(cst[:], consts).then_inc(ones_loaded, 16)
            ln_exp_tables()
            load_x(act, 1)
            load_x(act, 2)
            act.dma_start(lbl[:], lbT).then_inc(rest_loaded, 16)
            act.dma_start(mask_raw, masks).then_inc(rest_loaded, 16)
            act.dma_start(invc[:], inv_count).then_inc(rest_loaded, 16)

            def step(ins):
                chain.inc(ins)
                act.wait_ge(act_chain, chain.value)

            def norm(c):
                if c >= 2:
                    what, n, g = CALLS[c - 2]
                    if what == "pre":
                        act.wait_ge(hfull_ready, PARTS * (3 * n + g + 1))
                    else:
                        act.wait_ge(x_updated, 2 * (3 * n + g + 1))
                b, uses = plan.norm[c]
                r = rinv[:, c % 2, :]
                if c == 0:
                    act.wait_ge(cols_ready, 1)
                act.wait_ge(bank_full[b], uses + 1)
                nc.scalar.activation(r, bank[b][:, 0:N], ACT.Ln, scale=1.0 / D_MODEL, bias=eps)\
                    .then_inc(bank_read[b], 1)
                act.wait_ge(bank_read[b], uses + 1)
                nc.scalar.activation(r, r, ACT.Exp, scale=-0.5).then_inc(rinv_ready, 1)

            def pre(p, c, g, between=None):
                n = 3 * p + g
                for hf in range(2):
                    ks = slice(hf * HALF, (hf + 1) * HALF)
                    if p == 0:
                        act.wait_ge(x_loaded[2 * g + hf], 16)
                    else:
                        act.wait_ge(x_updated, 2 * (n - 3) + hf + 1)
                    if n:
                        act.wait_ge(h_ready, PARTS * (n - 1) + 2 * hf + 2)
                    nc.scalar.activation(scratch[:, ks, :], xg(g)[:, ks, :], ACT.Square).then_inc(squares_ready, 1)
                if between:
                    between()
                    if g == G - 1 and p != 1:
                        ln_exp_tables()
                norm(c)
                for part in range(PARTS):
                    ks = slice(part * PART, (part + 1) * PART)
                    act.wait_ge(hfull_ready, PARTS * n + part + 1)
                    nc.scalar.activation(hy[:, g, ks, 0:N], scratch[:, ks, :], ACT.Copy).then_inc(hhi_ready, 1)

            def silus(name, f, i, kind, ns):
                pairs = [pos for pos, (t, _) in enumerate(jobs_of(name, kind)) if t % 2 == 0]
                for n in ns:
                    b, uses = plan.job(name, i, pairs[n])
                    if not (isinstance(i, int) and i == 0 and n < 2 and f == 0):
                        act.wait_ge(hidden_ready, i * 6 + (66 * f + n - 1))
                    act.wait_ge(bank_full[b], uses + 1)
                    nc.scalar.activation(sbuf2[:, n % 2, :], bank[b][:, 0:N], ACT.Silu, scale=1.0 / WS)\
                        .then_inc(bank_read[b], 1)

            def up(name, f):
                silus(name, f, 0, "G", range(NEXT, 6))
                loops(act, name, lambda i, kind: silus(name, f, i, kind, range(6)),
                      [run for run in turn_runs(name) if run[0]])

            def square_y(q, m, g, src, scale=1.0):
                if m == 0:
                    return nc.scalar.activation(ssq(g), src, ACT.Square, scale=scale)
                n = y_adds(q, m, g) - 1
                if n >= 2:
                    act.wait_ge(ysq_added, n - 1)
                return nc.scalar.activation(sbuf2[:, n % 2, :], src, ACT.Square, scale=scale)

            def evac_y(q, name, i, pos, m, g):
                b, uses = plan.job(name, i, pos)
                act.wait_ge(bank_full[b], uses + 1)
                ins = square_y(q, m, g, bank[b][:, 0:N], 1.0 / WS)
                if m:
                    ins.then_inc(ysq_ready, 1)
                nc.scalar.activation(yv[:, g, m, :], bank[b][:, 0:N], ACT.Copy, scale=gain(2 * q + 1, m))\
                    .then_inc(bank_read[b], 1)

            def down(q, next_stage):
                before, last = seam_tiles(q)
                early = EARLY[q]

                def evac(tiles):
                    for tile in tiles:
                        evac_y(q, *tile)

                evac(before)
                ln_exp_tables()
                evac(last[0][:early])
                for g in range(G):
                    evac(last[g][early:])
                    if q == 2 and g == 0:
                        act.dma_start(p_raw, pT).then_inc(p_loaded, 16)
                    c = 3 + 6 * q + 2 * g
                    norm(c)
                    pre(q + 1, c + 1, g, next_stage if g == G - 1 else lambda: evac(last[g + 1][:early]))

            def head_job(h, kind, t, g):
                b, uses = plan.head_job(h, t, g)
                act.wait_ge(bank_full[b], uses + 1)
                return b

            def gcols(a, g):
                return a[:, g * N:(g + 1) * N]

            def wait_piece(head, kind, r):
                b, uses = plan.piece(head, HG_FIRST[kind] + r)
                act.wait_ge(bank_full[b], uses + 1)

            def v_copy(h, kind, g, first):
                if not first:
                    for r in range(3):
                        wait_piece(h - 1, "vT", r)
                b = head_job(h, kind, 0, g)
                nc.scalar.activation(gcols(V, g), bank[b][:, 0:N], ACT.Copy, scale=1.0 / WS).then_inc(bank_read[b], 1)

            def og_sigmoid(h, kind, g):
                b = head_job(h, kind, 1, g)
                dst = hidv[:, h, g, :] if isinstance(h, int) else hidv[:, bass.ds(h, 1), g, :].rearrange(
                    "p a n -> p (a n)")
                nc.scalar.activation(dst, bank[b][:, 0:N], ACT.Sigmoid, scale=1.0 / WS).then_inc(sigmoid_ready, 1)

            def q_sigmoid(h, kind, g):
                b = head_job(h, kind, 2, g)
                nc.scalar.activation(gcols(Q, g), bank[b][:, 0:N], ACT.Sigmoid, scale=1.0 / WS).then_inc(sigmoid_ready, 1)

            def f_sigmoid(h, kind, g):
                b = head_job(h, kind, 3, g)
                nc.scalar.activation(gcols(K_, g), bank[b][:, 0:N], ACT.Sigmoid, scale=-1.0 / WS)\
                    .then_inc(bank_read[b], 1)

            def halves(a, w, right):
                v = a.rearrange("p (b s w) -> p b s w", s=2, w=w // 2)
                return v[:, :, 1 if right else 0, :]

            def onorm(head):
                act.wait_ge(ss_ready, head + 1)
                step(nc.scalar.activation(W[1], W[1], ACT.Ln, scale=1.0 / DK, bias=eps))
                nc.scalar.activation(W[1], W[1], ACT.Exp, scale=-0.5).then_inc(orstd_ready, 1)

            def logf(head):
                act.wait_ge(k_ready, head + 1)
                nc.scalar.activation(GG, K_, ACT.Ln, scale=-1.0, bias=one).then_inc(logf_ready, 1)

            def exps(head, first):
                def e(out, in_, scale, last=False):
                    nc.scalar.activation(out, in_, ACT.Exp, scale=scale).then_inc(exp_ready, 1)
                act.wait_ge(diff_ready, head * 4 + 1)
                e(W[3], W[3], 1.0)
                act.wait_ge(diff_ready, head * 4 + 2)
                e(halves(W[0], 64, False), halves(W[0], 64, False), -1.0)
                e(halves(W[0], 64, True), halves(W[0], 64, True), 1.0)
                act.wait_ge(diff_ready, head * 4 + 3)
                e(halves(W[1], 32, False), halves(W[1], 32, False), -1.0)
                e(halves(W[1], 32, True), halves(W[1], 32, True), 1.0)
                act.wait_ge(diff_ready, head * 4 + 4)
                e(W[4], W[2], -1.0)
                act.wait_ge(exp_ready, head * 9 + 6)
                e(W[2], W[2], 1.0)
                act.wait_ge(cum_ready, head + 1)
                e(W[5], GG, 1.0)
                e(eg[:], GG.rearrange("p (c t) -> p c t", t=C)[:, :, C - 1], 1.0)

            def osquare(head):
                act.wait_ge(o_ready, head + 1)
                nc.scalar.activation(W[4], W[3], ACT.Square).then_inc(osq_ready, 1)

            def state_load(head):
                if not (isinstance(head, int) and head == 0):
                    wait_piece(head - 1, "O", 3)
                else:
                    act.wait_ge(h_ready, PARTS * 6)
                    act.wait_ge(pads_set, 3)
                src = state_in[head] if isinstance(head, int) else state_in[
                    bass.ds(head, 1), :, :].rearrange("a k v -> k (a v)")
                act.dma_start(Sn(S_IN), src).then_inc(state_loaded, 16)

            def state_store(head):
                act.wait_ge(chain_ready, head + 1)
                for w, n in ((0, PT - 1), (1, S_OUT)):
                    dst = out_states[w, head] if isinstance(head, int) else out_states[
                        w, bass.ds(head, 1), :, :].rearrange("a k v -> k (a v)")
                    act.dma_start(dst, Sn(n)).then_inc(state_stored, 16)

            def head_turn(h, with_norm, u_turn=False):
                hh = h - 1
                ln_exp_tables()
                if with_norm:
                    onorm(h - 2)
                logf(hh)
                state_load(hh)
                if u_turn:
                    for g in range(G):
                        u_copy(0, g)
                else:
                    for g in range(G):
                        v_copy(h, "M", g, False)
                exps(hh, False)
                if u_turn:
                    for g in range(G):
                        u_copy(1, g)
                    act.wait_ge(operand_ready, hh * 8 + 8)
                    for g in range(G):
                        u_copy(2, g)
                else:
                    for g in range(G):
                        og_sigmoid(h, "M", g)
                    act.wait_ge(operand_ready, hh * 8 + 8)
                    for g in range(G):
                        q_sigmoid(h, "M", g)
                for g in range(G):
                    if u_turn:
                        u_copy(3, g)
                    else:
                        f_sigmoid(h, "M", g)
                    if g == 0:
                        osquare(hh)
                state_store(hh)

            def u_copy(j, g):
                if j == 0:
                    for r in range(3):
                        wait_piece(HEADS - 1, "vT", r)
                b = head_job(HEADS, "M", j, g)
                end = min((g + 1) * N, SEQ) - g * N
                ins = nc.scalar.activation(U[j][:, UP + g * N:UP + g * N + end], bank[b][:, 0:end],
                                           ACT.Copy, scale=1.0 / WS)
                if g < G - 1:
                    ins.then_inc(bank_read[b], 1)
                    return
                nc.scalar.activation(U[j][:, US:US + DEC_SEQ], bank[b][:, end:N], ACT.Copy, scale=1.0 / WS)\
                    .then_inc(bank_read[b], 1)
                act.wait_ge(bank_read[b], plan.head_job(HEADS, j, g)[1] + 1)
                act.dma_start(U[j][:, US - POOL_BUF:US], pool_in[:, j, :]).then_inc(pool_loaded[j], 16)
                act.dma_start(out_pools[0, j], U[j][:, UP + SEQ - POOL_BUF:UP + SEQ]).then_inc(pool_stored[j], 16)
                act.dma_start(out_pools[1, j], U[j][:, US + DEC_SEQ - POOL_BUF:US + DEC_SEQ])\
                    .then_inc(pool_stored[j], 16)

            def gate(name, i, t, g, dst):
                b, uses = plan.job(name, i, 3 * t + g)
                act.wait_ge(bank_full[b], uses + 1)
                nc.scalar.activation(dst, bank[b][:, 0:N], ACT.Sigmoid, scale=1.0 / WS).then_inc(bank_read[b], 1)

            def gates():
                for t in range(2):
                    for g in range(G):
                        gate("gates0", 0, t, g, gcols(TMP_FIRST[t], g))
                for n, (t, g) in enumerate((t, g) for t in range(4) for g in range(G)):
                    b, uses = plan.job("gates0", 0, 6 + n)
                    act.wait_ge(bank_full[b], uses + 1)
                    nc.scalar.activation(hid[:, MIX0 + t, g, 0:N], bank[b][:, 0:N], ACT.Copy, scale=pscale(t))\
                        .then_inc(mixed_hi_ready, 1)
                with act.Fori(0, KD - 1) as i:
                    for t in range(2):
                        for g in range(G):
                            if t == 0 and g == 0:
                                act.wait_ge(mixed_ready, i * 3 + (1 + 3))
                            gate("gates", i, t, g, hidv[:, TMP0 + t, g, :])

            def gates_and_squares(ns):
                for n in ns:
                    _, i, pos, m, g = y_tiles(3)[n]
                    ba, uses_a = plan.job("ple", i, pos - 1)
                    b, uses = plan.job("ple", i, pos)
                    if n >= 2:
                        _, _, _, m2, g2 = y_tiles(3)[n - 2]
                        act.wait_ge(ysq_added, y_adds(3, m2, g2))
                    act.wait_ge(bank_full[ba], uses_a + 1)
                    nc.scalar.activation(gate_buf(n), bank[ba][:, 0:N], ACT.Sigmoid, scale=1.0 / WS)\
                        .then_inc(bank_read[ba], 1)
                    act.wait_ge(bank_read[b], uses + 1)
                    ins = square_y(3, m, g, hidv[:, Y0 + m, g, :])
                    if m:
                        ins.then_inc(ysq_ready, 1)
                    if m == KD - 1:
                        ln_exp_tables()
                        norm(21 + g)

            for g in range(G):
                pre(0, g, g, (lambda: silus("ffn1_up", 0, 0, "G", range(NEXT))) if g == G - 1 else None)
            act.wait_ge(lb_diff, 1)
            nc.scalar.activation(oneml[:], oneml[:], ACT.Sigmoid).then_inc(lb_ready, 1)
            up("ffn1_up", 0)
            down(0, lambda: v_copy(0, "G", 0, True))
            for g in range(G):
                if g:
                    v_copy(0, "G", g, True)
                og_sigmoid(0, "G", g)
                q_sigmoid(0, "G", g)
                f_sigmoid(0, "G", g)
            head_turn(1, False)
            with act.Fori(2, HEADS) as h:
                chain.enter(h, 2, 1)
                head_turn(h, True)
            chain.leave(HEADS - 2)
            head_turn(HEADS, True, True)
            ln_exp_tables()
            onorm(HEADS - 1)
            gates()
            act.wait_ge(state_stored, 32 * HEADS)
            down(1, lambda: silus("ffn2_up", 1, 0, "G", range(NEXT)))
            up("ffn2_up", 1)
            down(2, lambda: gates_and_squares(range(NEXT + 1)))
            gates_and_squares(range(NEXT + 1, KD * G))
            act.wait_ge(state_stored, 32 * HEADS)

        @block.vector
        def _(dve):
            chain = Tally(vec_chain)

            def step(ins):
                chain.inc(ins)
                dve.wait_ge(vec_chain, chain.value)

            V_ = nc.vector
            dve.wait_ge(cols_loaded, 16)
            for n, step_size in ((1, 0.5), (3, 1.0), (5, 0.5)):
                step(V_.tensor_scalar(col[:, n * KD:(n + 1) * KD], col[:, n * KD:(n + 1) * KD], step_size / WS,
                                      None, ALU.mult))
            V_.tensor_scalar(col[:, 8 * KD + 1:8 * KD + 5], col[:, 8 * KD + 1:8 * KD + 5], 1.0 / WS, None, ALU.mult)\
                .then_inc(cols_ready, 1)
            dve.wait_ge(cols_ready, 1)

            def pre(p, c, g, between=None):
                n = 3 * p + g
                for hf in range(2):
                    ks = slice(hf * HALF, (hf + 1) * HALF)
                    dve.wait_ge(squares_ready, 2 * n + hf + 1)
                    step(V_.tensor_reduce(half_sum[:] if hf else ssq(g), scratch[:, ks, :].rearrange("p k n -> p n k"),
                                          AX_X, ALU.add))
                V_.tensor_tensor(ssq(g), ssq(g), half_sum[:], ALU.add).then_inc(sums_ready, 1)
                if between:
                    between()
                dve.wait_ge(rinv_ready, c + 1)
                def part(n_):
                    for k in range(n_ * PART, (n_ + 1) * PART):
                        ins = V_.scalar_tensor_tensor(out=scratch[:, k, :], in0=xg(g, k), scalar=gain(2 * p, k),
                                                      in1=rinv[:, c % 2, :], op0=ALU.mult, op1=ALU.mult)
                    ins.then_inc(hfull_ready, 1)

                def low(n_):
                    ks = slice(n_ * PART, (n_ + 1) * PART)
                    dve.wait_ge(hhi_ready, PARTS * n + n_ + 1)
                    V_.tensor_tensor(hy[:, g, ks, N:2 * N], scratch[:, ks, :], hy[:, g, ks, 0:N], ALU.subtract)\
                        .then_inc(h_ready, 1)

                part(0)
                for n_ in range(1, PARTS):
                    part(n_)
                    low(n_ - 1)
                low(PARTS - 1)

            def add_square(q, m, g):
                if m:
                    n = y_adds(q, m, g) - 1
                    dve.wait_ge(ysq_ready, n + 1)
                    if n:
                        dve.wait_ge(ysq_added, n)
                    V_.tensor_tensor(ssq(g), ssq(g), sbuf2[:, n % 2, :], ALU.add).then_inc(ysq_added, 1)

            def post(q, c, g, y):
                dve.wait_ge(rinv_ready, c + 1)
                for hf in range(2):
                    ks = slice(hf * HALF, (hf + 1) * HALF)
                    step(V_.tensor_tensor(y[:, ks, :], y[:, ks, :],
                                          rinv[:, c % 2, :].unsqueeze(1).to_broadcast([P, HALF, N]), ALU.mult))
                    if q < 3:
                        V_.tensor_tensor(xg(g)[:, ks, :], xg(g)[:, ks, :], y[:, ks, :], ALU.add).then_inc(x_updated, 1)
                        continue
                    for k in range(hf * HALF, (hf + 1) * HALF):
                        ins = V_.scalar_tensor_tensor(out=xg(g, k), in0=y[:, k, :], scalar=gain(2 * q + 1, k),
                                                      in1=xg(g, k), op0=ALU.mult, op1=ALU.add)
                    ins.then_inc(x_updated, 1)

            def down(q, next_stage):
                before, last = seam_tiles(q)
                early = EARLY[q]

                def add(ts):
                    for *_, m, g in ts:
                        add_square(q, m, g)

                add(before)
                add(last[0][:early])
                for g in range(G):
                    add(last[g][early:])
                    c = 3 + 6 * q + 2 * g
                    post(q, c, g, yv[:, g, :, :])
                    dve.wait_ge(x_updated, 2 * (3 * q + g + 1))
                    pre(q + 1, c + 1, g, next_stage if g == G - 1 else lambda: add(last[g + 1][:early]))
                    if q == 2:
                        split_p(g)

            def products(name, f, i, kind, ns):
                pairs = [(pos, t, g) for pos, (t, g) in enumerate(jobs_of(name, kind)) if t % 2]
                for n in ns:
                    pos, t, g = pairs[n]
                    ba, uses_a = plan.job(name, i, pos - 1)
                    b, uses = plan.job(name, i, pos)
                    s = sbuf2[:, n % 2, :]
                    m = i * 2 + t // 2
                    dst = hid[:, m, g, :] if isinstance(m, int) else hid[:, bass.ds(m, 1), g, :].rearrange(
                        "p a n -> p (a n)")
                    dve.wait_ge(bank_read[ba], uses_a + 1)
                    dve.wait_ge(bank_full[b], uses + 1)
                    V_.scalar_tensor_tensor(out=s, in0=bank[b][:, 0:N], scalar=1.0 / WS, in1=s,
                                            op0=ALU.mult, op1=ALU.mult).then_inc(bank_read[b], 1)
                    dve.wait_ge(bank_read[b], uses + 1)
                    step(V_.tensor_scalar(dst[:, 0:N], s, 1.0, None, ALU.mult))
                    V_.tensor_tensor(dst[:, N:2 * N], s, dst[:, 0:N], ALU.subtract).then_inc(hidden_ready, 1)

            def up(name, f):
                products(name, f, 0, "G", range(NEXT, 6))
                for a, b, kind in turn_runs(name):
                    if a:
                        with dve.Fori(a, b) as i:
                            chain.enter(i, a, 6)
                            products(name, f, i, kind, range(6))
                        chain.leave(b - a)

            def gcols(a, g):
                return a[:, g * N:(g + 1) * N]

            def head_bank(h, kind, t, g):
                return plan.head_job(h, t, g)

            def slot(h, g):
                return hidv[:, h, g, :] if isinstance(h, int) else hidv[:, bass.ds(h, 1), g, :].rearrange(
                    "p a n -> p (a n)")

            def silu_og(h, kind, g, n):
                b, _ = head_bank(h, kind, 1, g)
                dve.wait_ge(sigmoid_ready, h * 6 + n)
                V_.scalar_tensor_tensor(out=slot(h, g), in0=bank[b][:, 0:N], scalar=1.0 / WS, in1=slot(h, g),
                                        op0=ALU.mult, op1=ALU.mult).then_inc(bank_read[b], 1)

            def silu_q(h, kind, g, n):
                b, _ = head_bank(h, kind, 2, g)
                dve.wait_ge(sigmoid_ready, h * 6 + n)
                V_.scalar_tensor_tensor(out=gcols(Q, g), in0=bank[b][:, 0:N], scalar=1.0 / WS, in1=gcols(Q, g),
                                        op0=ALU.mult, op1=ALU.mult).then_inc(bank_read[b], 1)

            def evac(head, kind, r, f):
                b, uses = plan.piece(head, HG_FIRST[kind] + r)
                dve.wait_ge(bank_full[b], uses + 1)
                if kind in ("L32", "L16", "D16"):
                    if kind != "L32":
                        b1, uses1 = plan.piece(head, HG_FIRST[kind] + r - 2)
                        dve.wait_ge(bank_read[b1], uses1 + 1)
                    n = 2 + 2 * ("L32", "L16", "D16").index(kind) + r
                    V_.tensor_copy(mark[:, n:n + 1], mark[:, 0:1])
                f(bank[b]).then_inc(bank_read[b], 1)
                return b, uses

            def evac_tok(head, kind, dst):
                def copy(b, j0, j1):
                    if j1 == 9:
                        V_.tensor_copy(dst[:, j0 * P:8 * P], b[:, 0:(8 - j0) * P])
                        return V_.tensor_copy(dst[0:C, 8 * P:9 * P], b[0:C, (8 - j0) * P:(9 - j0) * P])
                    return V_.tensor_copy(dst[:, j0 * P:j1 * P], b[:, 0:(j1 - j0) * P])
                for r, (j0, j1) in enumerate(TOK_TILES):
                    evac(head, kind, r, lambda b: copy(b, j0, j1))

            def evac_scores(head, kind, m):
                def pairs(b):
                    for h0 in (0, C):
                        ins = V_.copy_predicated(att[h0:h0 + C, 0:PT // 2 * P].rearrange(
                            "p (j s c) -> p j s c", s=2, c=C)[:, :, h0 // C, :],
                            msk[h0:h0 + C, m, :].rearrange("p (j c) -> p j c", c=C),
                            b[h0:h0 + C, 0:512].rearrange("p (j c) -> p j c", c=C))
                    return ins

                evac(head, kind, 0, pairs)
                evac(head, kind, 1, lambda b: V_.copy_predicated(att[0:C, PT // 2 * P:TP], msk[0:C, m, 0:C],
                                                                 b[0:C, 0:C]))

            def chunks(a, w):
                return a.rearrange("p (b w) -> p b w", w=w)

            def halves(a, w, right):
                v = a.rearrange("p (b s w) -> p b s w", s=2, w=w // 2)
                return v[:, :, 1 if right else 0, :]

            def minus_ref(out, w, at):
                v = chunks(GG, w)
                ref = v[:, :, at:at + 1].to_broadcast([P, TP // w, w])
                V_.tensor_tensor(chunks(out, w), v, ref, ALU.subtract).then_inc(diff_ready, 1)

            def decay_keys(head):
                if isinstance(head, int) and head == 0:
                    kind = "G"
                else:
                    kind = "M"
                for t in (0, 3):
                    for g in range(G):
                        b, uses = head_bank(head, kind, t, g)
                        dve.wait_ge(bank_read[b], uses + 1)
                sc = oneml[:, head:head + 1] if isinstance(head, int) else oneml[:, bass.ds(head, 1)]
                V_.tensor_scalar(K_[:, 0:T], K_[:, 0:T], sc, None, ALU.mult).then_inc(k_ready, 1)

            def onorm(head):
                dve.wait_ge(orstd_ready, head + 1)
                step(V_.scalar_tensor_tensor(out=W[3], in0=W[3], scalar=anorm, in1=W[1],
                                             op0=ALU.mult, op1=ALU.mult))
                s32 = hidv[:, head, :, :] if isinstance(head, int) else hidv[:, bass.ds(head, 1), :, :].rearrange(
                    "p a g n -> p (a g) n")
                s16 = hid[:, head, :, :] if isinstance(head, int) else hid[:, bass.ds(head, 1), :, :].rearrange(
                    "p a g n -> p (a g) n")
                o = W[3][:, 0:T].rearrange("p (g n) -> p g n", g=G)
                step(V_.tensor_tensor(o, o, s32, ALU.mult))
                step(V_.tensor_scalar(s16[:, :, 0:N], o, 1.0, None, ALU.mult))
                V_.tensor_tensor(s16[:, :, N:2 * N], o, s16[:, :, 0:N], ALU.subtract).then_inc(head_ready, 1)

            def operand(out, in0, head, n):
                dve.wait_ge(exp_ready, head * 9 + n)
                V_.tensor_tensor(out, out, in0, ALU.mult).then_inc(operand_ready, 1)

            def head_turn(h, with_norm, u_turn=False):
                hh = h - 1
                evac_tok(hh, "vT", vtok)
                if with_norm:
                    onorm(h - 2)
                dve.wait_ge(logf_ready, hh + 1)
                V_.tensor_tensor_scan(W[2], smask, GG, 0.0, ALU.mult, ALU.add).then_inc(vec_chain, 1)
                chain.n += 1
                dve.wait_ge(vec_chain, chain.value)
                V_.tensor_copy(GG, W[2]).then_inc(cum_ready, 1)
                dve.wait_ge(cum_ready, hh + 1)
                v = chunks(GG, C)
                V_.tensor_tensor(chunks(W[3], C), v[:, :, C - 1:C].to_broadcast([P, NC, C]), v, ALU.subtract)\
                    .then_inc(diff_ready, 1)
                minus_ref(W[0], 64, 31)
                minus_ref(W[1], 32, 15)
                minus_ref(W[2], 16, 7)
                operand(W[3], K_, hh, 1)
                operand(halves(W[0], 64, False), halves(K_, 64, False), hh, 2)
                operand(halves(W[0], 64, True), halves(Q, 64, True), hh, 3)
                operand(halves(W[1], 32, False), halves(K_, 32, False), hh, 4)
                operand(halves(W[1], 32, True), halves(Q, 32, True), hh, 5)
                operand(W[4], K_, hh, 6)
                operand(W[2], Q, hh, 7)
                operand(W[5], Q, hh, 8)
                evac_tok(hh, "kT", ktok)
                evac_scores(hh, "L32", 0)
                evac_scores(hh, "L16", 1)
                if not u_turn:
                    for g in range(G):
                        silu_og(h, "M", g, g + 1)
                evac_scores(hh, "D16", 2)
                dve.wait_ge(exp_ready, hh * 9 + 9)
                dve.wait_ge(state_loaded, hh * 16 + 16)
                if not (isinstance(hh, int) and hh == 0):
                    dve.wait_ge(state_stored, hh * 32)
                for rs in ((0, 1), (2, 3), (4,)):
                    for r in rs:
                        b, uses = plan.piece(hh, HG_FIRST["P"] + r)
                        dve.wait_ge(bank_full[b], uses + 1)
                    for c in sorted(c for r in rs for c in P_CHUNKS[r]):
                        r = next(r for r in rs if c in P_CHUNKS[r])
                        b, uses = plan.piece(hh, HG_FIRST["P"] + r)
                        n = P_CHUNKS[r].index(c)
                        src = bank[b][:, n * P:(n + 1) * P]
                        if c == 0:
                            ins = V_.tensor_copy(Sn(0), src)
                        elif c < PT:
                            ins = V_.scalar_tensor_tensor(out=Sn(c), in0=Sn(c - 1), scalar=eg[:, c:c + 1], in1=src,
                                                          op0=ALU.mult, op1=ALU.add)
                        else:
                            ins = V_.scalar_tensor_tensor(out=Sn(S_OUT), in0=Sn(S_IN), scalar=eg[:, c:c + 1],
                                                          in1=src, op0=ALU.mult, op1=ALU.add)
                        if c == P_CHUNKS[r][-1]:
                            ins.then_inc(bank_read[b], 1)
                            if c < NC - 1:
                                dve.wait_ge(bank_read[b], uses + 1)
                        else:
                            step(ins)
                dve.wait_ge(bank_read[b], uses + 1)
                V_.tensor_copy(mark[:, 1:2], mark[:, 0:1]).then_inc(chain_ready, 1)
                if u_turn:
                    pooling(0)
                    pooling(1)
                else:
                    for g in range(G):
                        silu_q(h, "M", g, g + 4)
                for r, (j0, j1) in enumerate(O_PAIRS):
                    w = min(j1 * P, TP) - j0 * P
                    b, uses = evac(hh, "O", r, lambda b: V_.tensor_copy(W[3][:, j0 * P:j0 * P + w], b[:, 0:w]))
                dve.wait_ge(bank_read[b], uses + 1)
                V_.tensor_copy(mark[:, 1:2], mark[:, 0:1]).then_inc(o_ready, 1)
                for r in range(3):
                    w = min(512, TP - r * 512)
                    b, uses = evac(hh, "SS", r, lambda b: V_.tensor_copy(W[1][:, r * 512:r * 512 + w], b[:, 0:w]))
                dve.wait_ge(bank_read[b], uses + 1)
                V_.tensor_copy(mark[:, 1:2], mark[:, 0:1]).then_inc(ss_ready, 1)
                if u_turn:
                    pooling(2)
                else:
                    decay_keys(h)

            HEAD_STEPS = 3 + 1 + 12

            def pooling(j):
                w = POOL_WINDOWS[j]
                for g in range(G):
                    b, uses = head_bank(HEADS, "M", j, g)
                    dve.wait_ge(bank_read[b], uses + 1)
                dve.wait_ge(pool_loaded[j], 16)
                step(V_.memset(U[j][:, 0:POOL_BUF], 0.0))
                src, n, bufs = U[j], 1, [W[0], GG]
                end = US + DEC_SEQ
                k = 0
                while n < w:
                    dst = bufs[k % 2]
                    step(V_.tensor_tensor(dst[:, 2 * n - 1:end], src[:, 2 * n - 1:end],
                                          src[:, n - 1:end - n], ALU.add))
                    src, n, k = dst, 2 * n, k + 1
                t = bufs[k % 2]
                step(V_.tensor_tensor(t[:, 0:POOL_BUF], src[:, UP:UP + POOL_BUF], invc[:, j, 0:POOL_BUF], ALU.mult))
                step(V_.tensor_tensor(t[:, 0:POOL_BUF], t[:, 0:POOL_BUF], U[j][:, UP:UP + POOL_BUF], ALU.subtract))
                step(V_.scalar_tensor_tensor(out=t[:, POOL_BUF:SEQ], in0=src[:, UP + POOL_BUF:UP + SEQ],
                                             scalar=1.0 / w, in1=U[j][:, UP + POOL_BUF:UP + SEQ],
                                             op0=ALU.mult, op1=ALU.subtract))
                step(V_.scalar_tensor_tensor(out=t[:, SEQ:T], in0=src[:, US:US + DEC_SEQ], scalar=1.0 / w,
                                             in1=U[j][:, US:US + DEC_SEQ], op0=ALU.mult, op1=ALU.subtract))
                dve.wait_ge(pool_stored[j], 32)
                tg = t[:, 0:T].rearrange("p (g n) -> p g n", g=G)
                step(V_.tensor_copy(pooled[j][:, :, 0:N], tg))
                V_.tensor_tensor(pooled[j][:, :, N:2 * N], tg, pooled[j][:, :, 0:N], ALU.subtract)\
                    .then_inc(pooled_ready, 1)

            def mixed():
                for n, (t, g) in enumerate((t, g) for t in range(4) for g in range(G)):
                    b, _ = plan.job("gates0", 0, 6 + n)
                    dst = hid[:, MIX0 + t, g, :]
                    dve.wait_ge(mixed_hi_ready, n + 1)
                    V_.scalar_tensor_tensor(out=dst[:, N:2 * N], in0=bank[b][:, 0:N], scalar=pscale(t),
                                            in1=dst[:, 0:N], op0=ALU.mult, op1=ALU.subtract).then_inc(bank_read[b], 1)
                dve.wait_ge(bank_read[b], plan.job("gates0", 0, 6 + n)[1] + 1)
                V_.tensor_copy(mark[:, 1:2], mark[:, 0:1]).then_inc(mixed_ready, 1)

            def gated(name, i, t, g, pos, s):
                bs, uses_s = plan.job(name, i, 3 * (t - 2) + g)
                b, uses = plan.job(name, i, pos)
                dve.wait_ge(bank_read[bs], uses_s + 1)
                dve.wait_ge(bank_full[b], uses + 1)
                V_.scalar_tensor_tensor(out=s, in0=bank[b][:, 0:N], scalar=1.0 / WS, in1=s,
                                        op0=ALU.mult, op1=ALU.mult).then_inc(bank_read[b], 1)
                return lambda: dve.wait_ge(bank_read[b], uses + 1)

            def join(a, s, dst):
                step(V_.tensor_tensor(a, a, s, ALU.add))
                step(V_.tensor_scalar(dst[:, 0:N], a, 1.0, None, ALU.mult))
                V_.tensor_tensor(dst[:, N:2 * N], a, dst[:, 0:N], ALU.subtract).then_inc(mixed_ready, 1)

            def gates():
                ta, tb = TMP_FIRST
                mixed()
                for g in range(G):
                    gated("gates0", 0, 2, g, 18 + g, gcols(ta, g))
                for g in range(G):
                    gated("gates0", 0, 3, g, 21 + g, gcols(tb, g))()
                    join(gcols(ta, g), gcols(tb, g), hid[:, M0, g, :])
                with dve.Fori(0, KD - 1) as i:
                    chain.enter(i, 0, 6)
                    for t in (2, 3):
                        for g in range(G):
                            s = hidv[:, TMP0 + t - 2, g, :]
                            there = gated("gates", i, t, g, 3 * t + g, s)
                            if t == 3:
                                there()
                                join(hidv[:, TMP0, g, :], s, hid[:, bass.ds(i + (M0 + 1), 1), g, :].rearrange(
                                    "p a n -> p (a n)"))
                chain.leave(KD - 1)

            def split_p(g):
                raw, parts = p_raw[:, g:G * KP:G, :], p_split[:, g:G * KP:G, :]
                dve.wait_ge(p_loaded, 16)
                step(V_.tensor_copy(parts[:, :, 0:N], raw))
                V_.tensor_tensor(parts[:, :, N:2 * N], raw, parts[:, :, 0:N], ALU.subtract).then_inc(p_ready, 1)

            for g in range(G):
                for hf in range(2):
                    dve.wait_ge(x_loaded[2 * g + hf], 16)
                pre(0, g, g, (lambda: products("ffn1_up", 0, 0, "G", range(NEXT))) if g == G - 1 else None)
            dve.wait_ge(rest_loaded, 16 * 3)
            V_.tensor_tensor(oneml[:], lbl[:, 1, :], lbl[:, 0, :], ALU.subtract).then_inc(lb_diff, 1)
            step(V_.memset(mark[:], 0.0))
            step(V_.tensor_copy(msk[:].rearrange("p m (r c) -> p m r c", c=C), mask_raw.rearrange(
                "p (m c) -> p m c", m=3).unsqueeze(2).to_broadcast([P, 3, 512 // C, C])))
            up("ffn1_up", 0)
            down(0, None)
            V_.memset(V[:, T:TP], 0.0).then_inc(pads_set, 1)
            V_.memset(Q[:, T:TP], 0.0)
            V_.memset(K_[:, T:TP], 0.0).then_inc(pads_set, 1)
            V_.memset(att, 0.0).then_inc(pads_set, 1)
            step(V_.memset(smask, 1.0))
            step(V_.memset(smask.rearrange("p (c t) -> p c t", t=C)[:, :, 0], 0.0))
            for g in range(G):
                silu_og(0, "G", g, 2 * g + 1)
                silu_q(0, "G", g, 2 * g + 2)
            dve.wait_ge(lb_ready, 1)
            decay_keys(0)
            head_turn(1, False)
            with dve.Fori(2, HEADS) as h:
                chain.enter(h, 2, HEAD_STEPS + 0)
                head_turn(h, True)
            chain.leave(HEADS - 2)
            head_turn(HEADS, True, True)
            onorm(HEADS - 1)
            pooling(3)
            gates()
            def gated_products(ns):
                for n in ns:
                    _, i, pos, m, g = y_tiles(3)[n]
                    ba, uses_a = plan.job("ple", i, pos - 1)
                    b, uses = plan.job("ple", i, pos)
                    dve.wait_ge(bank_read[ba], uses_a + 1)
                    dve.wait_ge(bank_full[b], uses + 1)
                    V_.scalar_tensor_tensor(out=hidv[:, Y0 + m, g, :], in0=bank[b][:, 0:N],
                                            scalar=1.0 / WS, in1=gate_buf(n),
                                            op0=ALU.mult, op1=ALU.mult).then_inc(bank_read[b], 1)
                    add_square(3, m, g)
                    if m == KD - 1:
                        post(3, 21 + g, g, hidv[:, Y0:Y0 + KD, g, :])

            down(1, lambda: products("ffn2_up", 1, 0, "G", range(NEXT)))
            up("ffn2_up", 1)
            down(2, lambda: gated_products(range(NEXT + 1)))
            gated_products(range(NEXT + 1, KD * G))


def kernel(x_prompt, x_sample, p_prompt, p_sample, state_hgrn, state_pool, norm_gains, lb_logits,
           w_ffn1_gu, w_ffn1_down, w_in, a_gnorm, w_a_up, w_pool, pool_scale, w_b_up, w_out,
           w_ffn2_gu, w_ffn2_down, w_ple_proj, w_ple_gate):
    import numpy as np
    import concourse.bacc as bacc
    from concourse.bass_utils import run_bass_kernel_spmd

    f32 = np.float32

    def tiles(w):
        w = np.asarray(w)
        r, c = w.shape
        return w.reshape(r // P, P, c // P, P).transpose(0, 2, 1, 3)

    stream = []

    def column(w, m):
        stream.append(w[:, m])

    def ffn(gu, dn):
        gu, dn = tiles(gu), tiles(dn)
        for j in range(KF):
            column(gu, j)
            column(gu, KF + j)
        for m in range(KD):
            column(dn, m)

    ffn(w_ffn1_gu[0], w_ffn1_down[0])
    win = tiles(w_in[0])
    q0, f0, i0, og0, up0 = 0, 8, 16, 24, 32
    ga0, gb0 = 36, 44
    for h in range(HEADS):
        for base in (i0, og0, q0, f0):
            column(win, base + h)
    for j in range(4):
        column(win, up0 + j)
    wa, wb = tiles(w_a_up[0]), tiles(w_b_up[0])
    for m in range(KD):
        column(win, ga0 + m)
        column(win, gb0 + m)
        if m == 0:
            for j in range(4):
                stream.append(np.asarray(w_pool)[0, j][None])
        column(wa, m)
        column(wb, m)
    wo = tiles(w_out[0])
    for m in range(KD):
        column(wo, m)
    ffn(w_ffn2_gu[0], w_ffn2_down[0])
    wg, wp = tiles(w_ple_gate[0]), tiles(w_ple_proj[0])
    for m in range(KD):
        column(wg, m)
        column(wp, m)
    st = np.concatenate(stream, axis=0)
    units = st.shape[0] // UT
    st = np.ascontiguousarray(st.reshape(units, UT, P, P).transpose(0, 2, 1, 3).reshape(units, P, UT * P))

    def feature_major(a, b):
        t = np.concatenate([np.asarray(a), np.asarray(b)], axis=0).T
        return np.ascontiguousarray(t.reshape(t.shape[0] // P, P, T).transpose(1, 0, 2))

    def by_partition(v):
        return np.asarray(v).reshape(-1, P).T

    cols = np.concatenate([by_partition(norm_gains[0]), by_partition(a_gnorm[0]), by_partition(pool_scale[0]),
                           np.full((P, 1), EPS, f32), np.ones((P, 1), f32)], axis=1)
    s, t = np.arange(P)[:, None] % C, np.arange(C)[None, :]
    masks = np.stack([(s < 32) & (t >= 32),
                      (s // 32 == t // 32) & (s % 32 < 16) & (t % 32 >= 16),
                      (s // 16 == t // 16) & (s <= t)], axis=1).astype(f32).reshape(P, 3 * C)
    count = np.array([[1.0 / min(w, n + 1) for n in range(16)] for w in POOL_WINDOWS], f32)
    arrays = {
        "xT": feature_major(x_prompt[0], x_sample[0]),
        "pT": feature_major(p_prompt[0, 0], p_sample[0, 0]).reshape(P, KP * G, N),
        "weights": st,
        "cols": np.ascontiguousarray(cols),
        "lbT": np.ascontiguousarray(np.asarray(lb_logits).reshape(2, HEADS, P).transpose(2, 0, 1)),
        "consts": np.concatenate([np.eye(P, dtype=f32), np.ones((P, P), f32)], axis=1),
        "masks": masks,
        "inv_count": np.ascontiguousarray(np.broadcast_to(count, (P, 4, 16))),
        "state_in": np.ascontiguousarray(state_hgrn[0, 0]),
        "pool_in": np.ascontiguousarray(np.asarray(state_pool)[0, 0].T.reshape(4, P, POOL_BUF).transpose(1, 0, 2)),
    }
    outs = {"out_x": (P, KD, T), "out_states": (2, HEADS, DK, DK), "out_pools": (2, 4, P, POOL_BUF)}

    nc = bacc.Bacc("TRN2", target_bir_lowering=False, num_devices=1)
    args = {n: nc.dram_tensor(n, a.shape, mybir.dt.from_np(a.dtype), kind="ExternalInput").ap()
            for n, a in arrays.items()}
    args.update({n: nc.dram_tensor(n, sh, F32, kind="ExternalOutput").ap() for n, sh in outs.items()})
    build(nc, **args)
    r = run_bass_kernel_spmd(nc, [arrays], core_ids=[0]).results[0]

    y = np.asarray(r["out_x"]).transpose(1, 0, 2).reshape(D_MODEL, T).T
    states, pools = np.asarray(r["out_states"]), np.asarray(r["out_pools"])
    pools = pools.reshape(2, 4 * P, POOL_BUF).transpose(0, 2, 1)
    return (np.ascontiguousarray(y[None, :SEQ]), np.ascontiguousarray(y[None, SEQ:]),
            states[None, 0:1], np.ascontiguousarray(pools[None, 0:1]),
            states[None, 1:2], np.ascontiguousarray(pools[None, 1:2]))
```
